# Optimizing a Trainium2 kernel written in Bass

```python
import jax, jax.numpy as jnp
from jax import lax
import numpy as np

D_MODEL = 1024
BATCH = 1
SEQ = 2048
DEPTH = 1
DEC_BATCH = 8
DEC_SEQ = 1
PAST_LEN = 4096
PAGE_SIZE = 128

HEAD_DIM = D_MODEL // 8
HEADS_PER_GROUP = 4
ATTN_PATTERNS = ((128, 1), (512, 4), (2048, 16))
N_ATTN_GROUPS = len(ATTN_PATTERNS)
QKV_WIDTH = N_ATTN_GROUPS * HEADS_PER_GROUP * HEAD_DIM
ATTN_WIDTH = HEADS_PER_GROUP * HEAD_DIM
POOL_WINDOWS = (2, 4, 8, 16)
N_POOL_GROUPS = len(POOL_WINDOWS)
POOL_GROUP_DIM = D_MODEL // 8
POOL_WIDTH = N_POOL_GROUPS * POOL_GROUP_DIM
POOL_STATE = max(POOL_WINDOWS) - 1
Q_BLOCK = 128
IN_WIDTH = 3 * QKV_WIDTH + ATTN_WIDTH + 2 * POOL_WIDTH + 2 * D_MODEL
EPS = 1e-6

kernel_name = 'dilated_attn_pool_gated_hybrid_step'

def rms_norm(x, gain):
    xf = x.astype(jnp.float32)
    return xf * lax.rsqrt(jnp.mean(xf * xf, axis=-1, keepdims=True) + EPS) * gain.astype(jnp.float32)

def mixer_inputs(x, c, norm_g, w_ada, b_ada, w_in, q_gain, k_gain):
    B, L, _ = x.shape
    shift, scale, gate = jnp.split(jax.nn.silu(c) @ w_ada + b_ada, 3, axis=-1)
    h = (rms_norm(x, norm_g) * (1.0 + scale[:, None].astype(jnp.float32))
         + shift[:, None].astype(jnp.float32)).astype(x.dtype)
    proj = h @ w_in
    sizes = (QKV_WIDTH, QKV_WIDTH, QKV_WIDTH, ATTN_WIDTH, POOL_WIDTH, POOL_WIDTH, D_MODEL, D_MODEL)
    cuts = [sum(sizes[:i + 1]) for i in range(len(sizes) - 1)]
    q, k, v, z_a, u_b, z_b, g_a, g_b = jnp.split(proj, cuts, axis=-1)
    heads = (B, L, N_ATTN_GROUPS, HEADS_PER_GROUP, HEAD_DIM)
    q = rms_norm(q.reshape(heads), q_gain[:, None, :]) * (HEAD_DIM ** -0.5)
    k = rms_norm(k.reshape(heads), k_gain[:, None, :])
    v = v.reshape(heads).astype(jnp.float32)
    return q, k, v, z_a, u_b, z_b, g_a, g_b, gate

def dilated_attn_prompt(q, k, v, window, dilation):
    B, L, H, E = q.shape
    n_back = window // dilation
    span = dilation * Q_BLOCK
    Lp = -(-L // span) * span
    M = Lp // dilation
    nb = M // Q_BLOCK

    def to_blocks(t):
        t = jnp.pad(t, ((0, 0), (0, Lp - L), (0, 0), (0, 0)))
        t = t.reshape(B, M, dilation, H, E).transpose(0, 2, 1, 3, 4)
        return t.reshape(B, dilation, nb, Q_BLOCK, H, E)

    def with_prev(t):
        prev = jnp.pad(t, ((0, 0), (0, 0), (1, 0), (0, 0), (0, 0), (0, 0)))[:, :, :nb]
        return jnp.concatenate([prev, t], axis=3)

    qb = to_blocks(q)
    kc = with_prev(to_blocks(k))
    vc = with_prev(to_blocks(v))
    s = jnp.einsum('brnqhe,brnkhe->brnhqk', qb, kc)
    i = jnp.arange(Q_BLOCK)[:, None]
    j = jnp.arange(2 * Q_BLOCK)[None, :]
    dist = Q_BLOCK + i - j
    blk = jnp.arange(nb)[:, None, None]
    valid = (dist >= 0) & (dist <= n_back) & ((blk > 0) | (j >= Q_BLOCK))
    s = jnp.where(valid[:, None], s, -jnp.inf)
    lse = jax.nn.logsumexp(s, axis=-1)
    p = jnp.exp(s - lse[..., None])
    o = jnp.einsum('brnhqk,brnkhe->brnqhe', p, vc)
    o = o.reshape(B, dilation, M, H, E).transpose(0, 2, 1, 3, 4).reshape(B, Lp, H, E)[:, :L]
    lse = lse.transpose(0, 1, 2, 4, 3).reshape(B, dilation, M, H).transpose(0, 2, 1, 3).reshape(B, Lp, H)[:, :L]
    return o, lse

def dilated_attn_sample(q, k_new, v_new, kv_buf, window, dilation):
    B, S, H, E = q.shape
    Lb = kv_buf.shape[1]
    n_back = window // dilation
    k_all = jnp.concatenate([kv_buf[:, :, 0].astype(jnp.float32), k_new], axis=1)
    v_all = jnp.concatenate([kv_buf[:, :, 1].astype(jnp.float32), v_new], axis=1)
    idx = Lb + jnp.arange(S)[:, None] - dilation * jnp.arange(n_back + 1)[None, :]
    valid = idx >= 0
    idx = jnp.maximum(idx, 0)
    kg = k_all[:, idx]
    vg = v_all[:, idx]
    s = jnp.einsum('bshe,bsjhe->bshj', q, kg)
    s = jnp.where(valid[:, None, :], s, -jnp.inf)
    lse = jax.nn.logsumexp(s, axis=-1)
    p = jnp.exp(s - lse[..., None])
    o = jnp.einsum('bshj,bsjhe->bshe', p, vg)
    keep = min(window, Lb + S)
    new_buf = jnp.stack([k_all, v_all], axis=2)[:, Lb + S - keep:].astype(kv_buf.dtype)
    return o, lse, new_buf

def combine_groups(outs, lses):
    o = jnp.stack(outs, axis=2)
    w = jax.nn.softmax(jnp.stack(lses, axis=2), axis=2)
    a = jnp.einsum('blgh,blghe->blhe', w, o)
    return a.reshape(a.shape[0], a.shape[1], ATTN_WIDTH)

def pool_mix(u_full, n_new, pos0, w_pool, b_pool, pool_scale):
    B, N, _ = u_full.shape
    u = u_full.astype(jnp.float32).reshape(B, N, N_POOL_GROUPS, POOL_GROUP_DIM)
    cs = jnp.cumsum(u, axis=1)
    pos = pos0 + jnp.arange(n_new)
    means = []
    for g, w in enumerate(POOL_WINDOWS):
        csg = cs[:, :, g]
        lag = jnp.pad(csg, ((0, 0), (w, 0), (0, 0)))[:, :N]
        wsum = (csg - lag)[:, N - n_new:]
        cnt = jnp.minimum(w, pos + 1).astype(jnp.float32)
        means.append(wsum / cnt[None, :, None])
    mixed = jnp.stack(means, axis=2) - u[:, N - n_new:]
    y = jnp.einsum('blgc,gcd->blgd', mixed, w_pool.astype(jnp.float32)) + b_pool.astype(jnp.float32)
    return y.reshape(B, n_new, POOL_WIDTH) * pool_scale.astype(jnp.float32)

def mixer_output(x, a, p, z_a, z_b, g_a, g_b, gate, w_a_out, w_b_out, w_out):
    ya = (a.astype(x.dtype) * jax.nn.silu(z_a)) @ w_a_out
    yb = (p.astype(x.dtype) * jax.nn.silu(z_b)) @ w_b_out
    m = jax.nn.sigmoid(g_a) * ya + jax.nn.sigmoid(g_b) * yb
    return x + gate[:, None] * (m @ w_out)

def layer_prompt(x, c, norm_g, w_ada, b_ada, w_in, q_gain, k_gain, w_pool, b_pool, pool_scale,
                 w_a_out, w_b_out, w_out):
    L = x.shape[1]
    q, k, v, z_a, u_b, z_b, g_a, g_b, gate = mixer_inputs(x, c, norm_g, w_ada, b_ada, w_in, q_gain, k_gain)
    outs, lses, kv_new = [], [], []
    for g, (window, dilation) in enumerate(ATTN_PATTERNS):
        o, lse = dilated_attn_prompt(q[:, :, g], k[:, :, g], v[:, :, g], window, dilation)
        outs.append(o)
        lses.append(lse)
        kv_new.append(jnp.stack([k[:, :, g], v[:, :, g]], axis=2)[:, L - min(window, L):].astype(x.dtype))
    a = combine_groups(outs, lses)
    p = pool_mix(u_b, L, 0, w_pool, b_pool, pool_scale)
    pool_new = u_b[:, max(L - POOL_STATE, 0):]
    y = mixer_output(x, a, p, z_a, z_b, g_a, g_b, gate, w_a_out, w_b_out, w_out)
    return y, kv_new[0], kv_new[1], kv_new[2], pool_new

def layer_sample(x, c, kv_w128, kv_w512, kv_w2048, pool_buf, norm_g, w_ada, b_ada, w_in, q_gain, k_gain,
                 w_pool, b_pool, pool_scale, w_a_out, w_b_out, w_out):
    S = x.shape[1]
    q, k, v, z_a, u_b, z_b, g_a, g_b, gate = mixer_inputs(x, c, norm_g, w_ada, b_ada, w_in, q_gain, k_gain)
    outs, lses, kv_new = [], [], []
    for g, ((window, dilation), buf) in enumerate(zip(ATTN_PATTERNS, (kv_w128, kv_w512, kv_w2048))):
        o, lse, nbuf = dilated_attn_sample(q[:, :, g], k[:, :, g], v[:, :, g], buf, window, dilation)
        outs.append(o)
        lses.append(lse)
        kv_new.append(nbuf)
    a = combine_groups(outs, lses)
    u_full = jnp.concatenate([pool_buf.astype(u_b.dtype), u_b], axis=1)
    p = pool_mix(u_full, S, PAST_LEN, w_pool, b_pool, pool_scale)
    pool_new = u_full[:, u_full.shape[1] - POOL_STATE:].astype(pool_buf.dtype)
    y = mixer_output(x, a, p, z_a, z_b, g_a, g_b, gate, w_a_out, w_b_out, w_out)
    return y, kv_new[0], kv_new[1], kv_new[2], pool_new

def setup_inputs(seed: int = 0) -> dict:
    key = jax.random.key(seed)
    ks = jax.random.split(key, 24)
    f32 = jnp.float32
    nrm = lambda k, shape, s: jax.random.normal(k, shape, f32) * s
    kv_shape = lambda w: (DEPTH, DEC_BATCH, min(w, PAST_LEN), 2, HEADS_PER_GROUP, HEAD_DIM)
    return {
        'x_prompt': nrm(ks[0], (BATCH, SEQ, D_MODEL), 1.0),
        'x_sample': nrm(ks[1], (DEC_BATCH, DEC_SEQ, D_MODEL), 1.0),
        'state_kv_w128': nrm(ks[2], kv_shape(ATTN_PATTERNS[0][0]), 1.0),
        'state_kv_w512': nrm(ks[3], kv_shape(ATTN_PATTERNS[1][0]), 1.0),
        'state_kv_w2048': nrm(ks[4], kv_shape(ATTN_PATTERNS[2][0]), 1.0),
        'state_pool': nrm(ks[5], (DEPTH, DEC_BATCH, POOL_STATE, POOL_WIDTH), 1.0),
        'c_prompt': nrm(ks[6], (BATCH, D_MODEL), 1.0),
        'c_sample': nrm(ks[7], (DEC_BATCH, D_MODEL), 1.0),
        'norm_g': 1.0 + nrm(ks[8], (DEPTH, D_MODEL), 0.02),
        'w_ada': nrm(ks[9], (DEPTH, D_MODEL, 3 * D_MODEL), D_MODEL ** -0.5),
        'b_ada': nrm(ks[10], (DEPTH, 3 * D_MODEL), 0.02),
        'w_in': nrm(ks[11], (DEPTH, D_MODEL, IN_WIDTH), D_MODEL ** -0.5),
        'q_gain': 1.0 + nrm(ks[12], (DEPTH, N_ATTN_GROUPS, HEAD_DIM), 0.02),
        'k_gain': 1.0 + nrm(ks[13], (DEPTH, N_ATTN_GROUPS, HEAD_DIM), 0.02),
        'w_pool': nrm(ks[14], (DEPTH, N_POOL_GROUPS, POOL_GROUP_DIM, POOL_GROUP_DIM), POOL_GROUP_DIM ** -0.5),
        'b_pool': nrm(ks[15], (DEPTH, N_POOL_GROUPS, POOL_GROUP_DIM), 0.02),
        'pool_scale': 1.0 + nrm(ks[16], (DEPTH, POOL_WIDTH), 0.02),
        'w_a_out': nrm(ks[17], (DEPTH, ATTN_WIDTH, D_MODEL), ATTN_WIDTH ** -0.5),
        'w_b_out': nrm(ks[18], (DEPTH, POOL_WIDTH, D_MODEL), POOL_WIDTH ** -0.5),
        'w_out': nrm(ks[19], (DEPTH, D_MODEL, D_MODEL), D_MODEL ** -0.5),
    }

def reference(x_prompt, x_sample, state_kv_w128, state_kv_w512, state_kv_w2048, state_pool,
              c_prompt, c_sample, norm_g, w_ada, b_ada, w_in, q_gain, k_gain, w_pool, b_pool,
              pool_scale, w_a_out, w_b_out, w_out):
    y_p, y_s = x_prompt, x_sample
    new_p = [[], [], [], []]
    new_s = [[], [], [], []]
    for l in range(DEPTH):
        y_p, *st_p = layer_prompt(y_p, c_prompt, norm_g[l], w_ada[l], b_ada[l], w_in[l], q_gain[l], k_gain[l],
                                  w_pool[l], b_pool[l], pool_scale[l], w_a_out[l], w_b_out[l], w_out[l])
        y_s, *st_s = layer_sample(y_s, c_sample, state_kv_w128[l], state_kv_w512[l], state_kv_w2048[l],
                                  state_pool[l], norm_g[l], w_ada[l], b_ada[l], w_in[l], q_gain[l], k_gain[l],
                                  w_pool[l], b_pool[l], pool_scale[l], w_a_out[l], w_b_out[l], w_out[l])
        for lst, s_ in zip(new_p, st_p):
            lst.append(s_)
        for lst, s_ in zip(new_s, st_s):
            lst.append(s_)
    kv128_p = jnp.stack(new_p[0])
    kv512_p = jnp.stack(new_p[1])
    kv2048_p = jnp.stack(new_p[2])
    pool_p = jnp.stack(new_p[3])
    kv128_s = jnp.stack(new_s[0])
    kv512_s = jnp.stack(new_s[1])
    kv2048_s = jnp.stack(new_s[2])
    pool_s = jnp.stack(new_s[3])
    return (y_p, y_s, kv128_p, kv512_p, kv2048_p, pool_p, kv128_s, kv512_s, kv2048_s, pool_s)


_drawn_inputs = setup_inputs


def setup_inputs(seed=0):
    import zlib

    import numpy as np

    out = dict(_drawn_inputs(seed))
    spreads = {}
    factors = {'norm_g': 3.421, 'q_gain': 8.0, 'k_gain': 4.5, 'b_pool': 8.0, 'pool_scale': 8.0}
    for name, (base, spread) in spreads.items():
        noise = np.random.default_rng([zlib.crc32(name.encode()), seed]).standard_normal(out[name].shape)
        drawn = base * np.exp(spread * noise) if base else spread * noise
        out[name] = __import__('jax').numpy.asarray(drawn.astype(out[name].dtype))
    for name, factor in factors.items():
        out[name] = (out[name] * factor).astype(out[name].dtype)
    return out
```

```python
from contextlib import ExitStack

import concourse.bass as bass
from concourse import mybir

F32 = mybir.dt.float32
F32R = mybir.dt.float32r
ALU = mybir.AluOpType
ACT = mybir.ActivationFunctionType
AX = mybir.AxisListType

P = 128
D = 1024
KT = D // P
SEQ = 2048
NS = 8
TT = SEQ + NS
HEADS, GROUPS, E = 4, 3, 128
PATTERNS = ((128, 1), (512, 4), (2048, 16))
BLOCKS = SEQ // P
CH = 512
NCH = SEQ // CH
NBC = 5
BCH = -(-TT // NBC)
CQ, CK, CV, CZA, CU, CZB, CGA = 0, 1536, 3072, 4608, 5120, 5632, 6144
POOLS = (2, 4, 8, 16)
PADU = 16
NPS = 15
EPS = 1e-6
MASKED = -1e30
LEAD = 16
LEAD_DMA = 16
OW = E + 2
NO = GROUPS * HEADS


def after(n):
    return n + (LEAD + 1)


def block_tokens(g, b):
    d = PATTERNS[g][1]
    per = BLOCKS // d
    r, n = divmod(b, per)
    return r + d * P * n, d, n > 0


def strided(ap, start, count, step):
    return ap[start:start + (count - 1) * step + 1:step]


def build(nc, x_prompt, x_sample, state_kv_w128, state_kv_w512, state_kv_w2048, state_pool, c_prompt, c_sample,
          norm_g, w_ada, b_ada, w_in, q_gain, k_gain, w_pool, b_pool, pool_scale, w_a_out, w_b_out, w_out,
          y_p, y_s, kv128_p, kv512_p, kv2048_p, pool_p, kv128_s, kv512_s, kv2048_s, pool_s):
    states = (state_kv_w128, state_kv_w512, state_kv_w2048)
    kv_p = (kv128_p, kv512_p, kv2048_p)
    kv_s = (kv128_s, kv512_s, kv2048_s)
    xp, yp = x_prompt[0], y_p[0]
    xs = x_sample.rearrange("b s d -> (b s) d")
    ys = y_s.rearrange("b s d -> (b s) d")
    w_in_v = w_in[0].rearrange("(k p) c -> p k c", p=P)

    o_dram = nc.dram_tensor("o_dram", [SEQ, NO, OW], F32, kind="Internal").ap()
    bT_dram = nc.dram_tensor("bT_dram", [4, P, TT], F32, kind="Internal").ap()
    gT_dram = nc.dram_tensor("gT_dram", [20, P, TT], F32, kind="Internal").ap()
    samp_dram = nc.dram_tensor("samp_dram", [NS, 3, NO, E], F32, kind="Internal").ap()
    gate_dram = nc.dram_tensor("gate_dram", [1 + NS, D], F32, kind="Internal").ap()
    snew_dram = nc.dram_tensor("snew_dram", [NS, HEADS, GROUPS], F32, kind="Internal").ap()
    pnew_dram = nc.dram_tensor("pnew_dram", [NS, HEADS, GROUPS], F32, kind="Internal").ap()

    whole = ExitStack()
    phase_sems = []

    def end_phase():
        nc.clear_and_free_semaphores(phase_sems)
        phase_sems.clear()
        nc.all_engine_barrier()

    with whole:
        def scope(stack):
            def sb(name, shape, dt=F32):
                return stack.enter_context(nc.sbuf_tensor(name, shape, dt))

            def ps(name, shape, dt=F32):
                return stack.enter_context(nc.psum_tensor(name, shape, dt))

            def sem(name):
                one = nc.alloc_semaphore(name=name)
                if stack is not whole:
                    phase_sems.append(one)
                return one
            return sb, ps, sem

        keep_sb, _, keep_sem = scope(whole)
        ident = keep_sb("ident", [P, P])
        vecT = keep_sb("vecT", [P, 40])
        sampT = keep_sb("sampT", [P, 20, NS])
        bTs = keep_sb("bTs", [P, 4, NS])
        bulk = keep_sem("bulk")
        passed = {e.engine: keep_sem(f"passed{i}") for i, e in enumerate((nc.sync, nc.gpsimd, nc.vector))}
        late = keep_sem("late")

        big = ExitStack()
        whole.enter_context(big)
        big_sb, _, _ = scope(big)
        hH = big_sb("hH", [P, KT, TT], F32R)
        hL = big_sb("hL", [P, KT, TT], F32R)

        prepare(nc, scope, locals())
        end_phase()
        branches(nc, scope, locals())
        end_phase()
        attend(nc, scope, locals())
        end_phase()
        big.close()
        merge(nc, scope, locals())


def prepare(nc, scope, v):
    xp, xs, hH, hL, ident, vecT = v["xp"], v["xs"], v["hH"], v["hL"], v["ident"], v["vecT"]
    w_ada_v = v["w_ada"][0].rearrange("(k p) c -> p k c", p=P)
    gate_dram = v["gate_dram"]
    NC = 1 + NS
    XR, WR, SR = 8, 2, 3
    NX = SEQ // P
    NH = NCH * KT
    stack = ExitStack()
    with stack:
        sb, ps, sem = scope(stack)
        rows = sb("rows", [40, P])
        c_in = sb("c_in", [NC, D])
        c_sig = sb("c_sig", [NC, D])
        scT = sb("scT", [P, KT, NC])
        b_gate = sb("b_gate", [NC, D])
        gate_sb = c_in
        w_st = [sb(f"w_st{i}", [P, KT, 512]) for i in range(WR)]
        xt = [sb(f"xt{i}", [P, D]) for i in range(XR)]
        xst = sb("xst", [NS, D])
        junk = sb("junk", [P, D], mybir.dt.bfloat16)
        ss = sb("ss", [P, NX + 1])
        ms = sb("ms", [P, NX + 1])
        rs = sb("rs", [P, NX + 1])
        mhalf = sb("mhalf", [P, 1])
        addT = sb("addT", [P, KT, NC])
        scl1 = sb("scl1", [P, KT, NC])
        mulT = sb("mulT", [P, KT, NC])
        hst = [sb(f"hst{i}", [P, CH]) for i in range(SR)]
        hs_m = sb("hs_m", [P, KT, NS])
        hs_t = sb("hs_t", [P, KT, NS])
        ps_t = [ps(f"ps_t{i}", [P, CH]) for i in range(4)]
        ps_small = ps("ps_small", [P, 512])
        ps_mod = ps("ps_mod", [P, 512])
        ps_gate = [ps(f"ps_gate{i}", [P, 512]) for i in range(2)]
        mod = ps_mod[:, 0:2 * KT * NC].rearrange("p (f c) -> p f c", c=NC)
        cT = ps_small[:, 64:64 + KT * NC].rearrange("p (k c) -> p k c", c=NC)
        xsT = ps_small[:, 256:256 + KT * NS].rearrange("p (k c) -> p k c", c=NS)

        rows_in, c_landed, bg_landed, xs_landed = (sem(n) for n in ("rows_in", "c_landed", "bg_landed", "xs_landed"))
        w_landed = [sem(f"wa_landed{i}") for i in range(WR)]
        x_landed = [sem(f"x_landed{i}") for i in range(XR)]
        w_used, ident_zero, ident_ready, mhalf_ready = (sem(n) for n in ("wa_used", "ident_zero", "ident_ready", "mhalf_ready"))
        rows_T, vec_ready, c_sigm, c_silu, c_T, sc_ready = (sem(n) for n in ("rows_T", "vec_ready", "c_sigm", "c_silu", "c_T", "sc_ready"))
        mod_step, mod_ready, gate_done, gate_ready = (sem(n) for n in ("mod_step", "mod_ready", "gate_done", "gate_ready"))
        squared, meaned, powered, x_normed = (sem(n) for n in ("squared", "meaned", "powered", "x_normed"))
        hT_done, h_mod, h_hi, h_lo = (sem(n) for n in ("hT_done", "h_mod", "h_hi", "h_lo"))
        samp_T, samp_step, samp_hi, gate_stored = (sem(n) for n in ("samp_T", "samp_step", "samp_hi", "gate_stored"))

        with nc.Block() as block:
            @block.sync
            def _(sp):
                sp.dma_start(rows[0:24, :], v["b_ada"][0].rearrange("(a b) -> a b", b=P)).then_inc(rows_in, 16)
                sp.dma_start(rows[24:32, :], v["norm_g"][0].rearrange("(a b) -> a b", b=P)).then_inc(rows_in, 16)
                sp.dma_start(rows[32:36, :], v["b_pool"][0]).then_inc(rows_in, 16)
                sp.dma_start(rows[36:40, :], v["pool_scale"][0].rearrange("(a b) -> a b", b=P)).then_inc(rows_in, 16)
                sp.dma_start(c_in[0:1, :], v["c_prompt"]).then_inc(c_landed, 16)
                sp.dma_start(c_in[1:NC, :], v["c_sample"]).then_inc(c_landed, 16)
                sp.dma_start(b_gate[:, :], v["b_ada"][0:1, 2 * D:3 * D].to_broadcast([NC, D])).then_inc(bg_landed, 16)
                sp.dma_start(xst[:, :], xs).then_inc(xs_landed, 16)

                def load_w(n):
                    if n >= WR:
                        sp.wait_ge(w_used, n - WR + 1)
                    sp.dma_start(w_st[n % WR][:, :, :], w_ada_v[:, :, n * 512:(n + 1) * 512]).then_inc(w_landed[n % WR], 16)

                def load_x(t):
                    if t >= XR:
                        sp.wait_ge(hT_done, ((t - XR) // 4 + 1) * KT)
                    sp.dma_start(xt[t % XR][:, :], xp[t * P:(t + 1) * P, :]).then_inc(x_landed[t % XR], 16)

                load_w(0)
                load_w(1)
                for t in range(XR):
                    load_x(t)
                load_w(2)
                load_w(3)
                for t in range(XR, NX):
                    load_x(t)
                load_w(4)
                load_w(5)
                sp.wait_ge(gate_ready, 2)
                sp.dma_start(gate_dram, gate_sb[:, :]).then_inc(gate_stored, 16)
                sp.wait_ge(gate_stored, 16)

            @block.gpsimd
            def _(pool):
                nc.gpsimd.memset(ident[:, :], 0.0).then_inc(ident_zero, 1)
                nc.gpsimd.memset(mhalf[:, :], -0.5).then_inc(mhalf_ready, 1)
                pool.wait_ge(ident_zero, 1)
                nc.gpsimd.affine_select(out=ident[:, :], in_=ident[:, :], compare_op=ALU.not_equal, fill=1.0,
                                        base=0, pattern=[[-1, P]], channel_multiplier=1).then_inc(ident_ready, 1)
                pool.wait_ge(mhalf_ready, 1)

                def power(t, rows_n):
                    pool.wait_ge(meaned, t + 1)
                    nc.gpsimd.tensor_tensor(rs[0:rows_n, t:t + 1], ms[0:rows_n, t:t + 1], mhalf[0:rows_n, :],
                                            ALU.pow).then_inc(powered, 1)

                for t in range(4):
                    power(t, P)
                for tc in range(NCH):
                    if tc < NCH - 1:
                        for t in range(4 * tc + 4, 4 * tc + 8):
                            power(t, P)
                    for k in range(KT):
                        n = tc * KT + k
                        pool.wait_ge(h_mod, n + 1)
                        nc.gpsimd.tensor_copy(hH[:, k, tc * CH:(tc + 1) * CH], hst[n % SR][:, :]).then_inc(h_hi, 1)
                power(NX, NS)
                pool.wait_ge(samp_step, 2)
                nc.gpsimd.tensor_copy(hH[:, :, SEQ:TT], hs_t[:, :, :]).then_inc(samp_hi, 1)

            @block.scalar
            def _(act):
                act.wait_ge(c_landed, 32)
                nc.scalar.activation(c_sig[:, :], c_in[:, :], ACT.Sigmoid).then_inc(c_sigm, 1)

                def square(t):
                    act.wait_ge(x_landed[t % XR], 16 * (t // XR) + 16)
                    if t:
                        act.wait_ge(squared, t)
                    nc.scalar.activation(junk[:, :], xt[t % XR][:, :], ACT.Square, accum_out=ss[:, t:t + 1]).then_inc(squared, 1)

                for t in range(4):
                    square(t)
                for tc in range(NCH):
                    if tc < NCH - 1:
                        for t in range(4 * tc + 4, 4 * tc + 8):
                            square(t)
                    for k in range(KT):
                        n = tc * KT + k
                        act.wait_ge(mod_ready, 2)
                        act.wait_ge(hT_done, n + 1)
                        if n >= SR:
                            act.wait_ge(h_lo, n - SR + 1)
                        nc.scalar.activation(hst[n % SR][:, :], ps_t[n % 4][:, :], ACT.Identity,
                                             bias=addT[:, k, 0:1], scale=mulT[:, k, 0:1]).then_inc(h_mod, 1)
                act.wait_ge(xs_landed, 16)
                act.wait_ge(squared, NX)
                nc.scalar.activation(junk[0:NS, :], xst[:, :], ACT.Square, accum_out=ss[0:NS, NX:NX + 1]).then_inc(squared, 1)

            @block.vector
            def _(dve):
                dve.wait_ge(rows_T, 1)
                nc.vector.tensor_copy(vecT[:, :], ps_small[:, 0:40]).then_inc(vec_ready, 1)
                dve.wait_ge(c_sigm, 1)
                nc.vector.tensor_tensor(c_sig[:, :], c_sig[:, :], c_in[:, :], ALU.mult).then_inc(c_silu, 1)
                dve.wait_ge(c_T, 1)
                nc.vector.tensor_copy(scT[:, :, :], cT).then_inc(sc_ready, 1)

                def normalise(t, tile, rows_n):
                    dve.wait_ge(squared, t + 1)
                    nc.vector.tensor_scalar(ms[0:rows_n, t:t + 1], ss[0:rows_n, t:t + 1], 1.0 / D, EPS,
                                            ALU.mult, ALU.add).then_inc(meaned, 1)
                    dve.wait_ge(powered, t + 1)
                    nc.vector.tensor_scalar(tile, tile, rs[0:rows_n, t:t + 1], None, ALU.mult).then_inc(x_normed, 1)

                for t in range(4):
                    normalise(t, xt[t % XR][:, :], P)
                dve.wait_ge(w_used, 4)
                dve.wait_ge(vec_ready, 1)
                nc.vector.tensor_tensor(addT[:, :, :], mod[:, 0:KT, :], vecT[:, 0:KT].unsqueeze(2).to_broadcast([P, KT, NC]),
                                        ALU.add).then_inc(mod_ready, 1)
                nc.vector.tensor_tensor(scl1[:, :, :], mod[:, KT:2 * KT, :],
                                        vecT[:, KT:2 * KT].unsqueeze(2).to_broadcast([P, KT, NC]), ALU.add).then_inc(mod_step, 1)
                dve.wait_ge(mod_step, 1)
                nc.vector.tensor_scalar(scl1[:, :, :], scl1[:, :, :], 1.0, None, ALU.add).then_inc(mod_step, 1)
                dve.wait_ge(mod_step, 2)
                nc.vector.tensor_tensor(mulT[:, :, :], scl1[:, :, :], vecT[:, 24:32].unsqueeze(2).to_broadcast([P, KT, NC]),
                                        ALU.mult).then_inc(mod_ready, 1)
                for tc in range(NCH):
                    if tc < NCH - 1:
                        for t in range(4 * tc + 4, 4 * tc + 8):
                            normalise(t, xt[t % XR][:, :], P)
                    for k in range(KT):
                        n = tc * KT + k
                        cols = slice(tc * CH, (tc + 1) * CH)
                        dve.wait_ge(h_hi, n + 1)
                        nc.vector.tensor_tensor(hL[:, k, cols], hst[n % SR][:, :], hH[:, k, cols].bitcast(F32),
                                                ALU.subtract).then_inc(h_lo, 1)
                normalise(NX, xst[:, :], NS)
                dve.wait_ge(samp_T, 1)
                nc.vector.tensor_tensor(hs_m[:, :, :], xsT, mulT[:, :, 1:NC], ALU.mult).then_inc(samp_step, 1)
                dve.wait_ge(samp_step, 1)
                nc.vector.tensor_tensor(hs_t[:, :, :], hs_m[:, :, :], addT[:, :, 1:NC], ALU.add).then_inc(samp_step, 1)
                dve.wait_ge(samp_hi, 1)
                nc.vector.tensor_tensor(hL[:, :, SEQ:TT], hs_t[:, :, :], hH[:, :, SEQ:TT].bitcast(F32), ALU.subtract)
                dve.wait_ge(bg_landed, 16)
                for j in range(2):
                    dve.wait_ge(gate_done, j + 1)
                    cols = slice(j * 512, (j + 1) * 512)
                    nc.vector.tensor_tensor(gate_sb[:, cols], ps_gate[j][0:NC, :], b_gate[:, cols], ALU.add).then_inc(gate_ready, 1)

            @block.tensor
            def _(pe):
                pe.wait_ge(ident_ready, 1)
                pe.wait_ge(rows_in, 64)
                nc.tensor.transpose(ps_small[:, 0:40], rows[:, :], ident[0:40, 0:40]).then_inc(rows_T, 1)
                pe.wait_ge(c_silu, 1)
                for k in range(KT):
                    last = nc.tensor.transpose(cT[:, k, :], c_sig[:, k * P:(k + 1) * P], ident[0:NC, 0:NC])
                last.then_inc(c_T, 1)
                pe.wait_ge(sc_ready, 1)
                for n in range(4):
                    pe.wait_ge(w_landed[n % WR], 16 * (n // WR) + 16)
                    for f in range(4):
                        for k in range(KT):
                            last = nc.tensor.matmul(mod[:, 4 * n + f, :], w_st[n % WR][:, k, f * P:(f + 1) * P], scT[:, k, :],
                                                    start=(k == 0), stop=(k == KT - 1))
                    last.then_inc(w_used, 1)
                for tc in range(NCH):
                    pe.wait_ge(x_normed, 4 * tc + 4)
                    for k in range(KT):
                        n = tc * KT + k
                        if n >= 4:
                            pe.wait_ge(h_mod, n - 3)
                        for i in range(4):
                            last = nc.tensor.transpose(ps_t[n % 4][:, i * P:(i + 1) * P],
                                                       xt[(4 * tc + i) % XR][:, k * P:(k + 1) * P], ident[:, :])
                        last.then_inc(hT_done, 1)
                pe.wait_ge(x_normed, NX + 1)
                for k in range(KT):
                    last = nc.tensor.transpose(xsT[:, k, :], xst[:, k * P:(k + 1) * P], ident[0:NS, 0:NS])
                last.then_inc(samp_T, 1)
                for j in range(2):
                    n = 4 + j
                    pe.wait_ge(w_landed[n % WR], 16 * (n // WR) + 16)
                    for k in range(KT):
                        last = nc.tensor.matmul(ps_gate[j][0:NC, :], scT[:, k, :], w_st[n % WR][:, k, :],
                                                start=(k == 0), stop=(k == KT - 1))
                    last.then_inc(gate_done, 1)


def branches(nc, scope, v):
    hH, hL, ident, vecT = (v[n] for n in ("hH", "hL", "ident", "vecT"))
    w_in_v, bT_dram, gT_dram, bulk, late = (v[n] for n in ("w_in_v", "bT_dram", "gT_dram", "bulk", "late"))
    pool_p, pool_s, state_pool = v["pool_p"][0, 0], v["pool_s"][0], v["state_pool"][0]
    PAIRS, NF = 4, 28
    stack = ExitStack()
    with stack:
        sb, ps, sem = scope(stack)
        wst = [sb(f"wst{i}", [P, KT, P]) for i in range(2)]
        wH = [sb(f"wH{i}", [P, KT, P], F32R) for i in range(2)]
        wL = [sb(f"wL{i}", [P, KT, P], F32R) for i in range(2)]
        uT = sb("uT", [P, PADU + TT])
        run = [sb(f"run{i}", [P, PADU + SEQ]) for i in range(2)]
        mixed = sb("mixed", [P, TT])
        zS = sb("zS", [P, TT])
        gst = [sb(f"gst{i}", [P, BCH]) for i in range(2)]
        pst = [sb(f"pst{i}", [P, BCH]) for i in range(2)]
        ost = [sb(f"ost{i}", [P, BCH]) for i in range(NBC)]
        wpool = sb("wpool", [P, 4, P])
        recip = sb("recip", [P, PADU])
        sp_rows = sb("sp_rows", [NS * NPS, 4 * P])
        spT = sb("spT", [P, 4, NS * NPS])
        s_sum = sb("s_sum", [P, 2, NS])
        utail = sb("utail", [P, 4, NPS + NS])
        urow = sb("urow", [NPS, 4 * P])
        usrow = sb("usrow", [NS, 4 * P])
        pp = [ps(f"pp{i}", [P, 512]) for i in range(NBC)]
        ppool = [ps(f"ppool{i}", [P, 512]) for i in range(2)]

        w_landed = [sem(f"wb_landed{i}") for i in range(2)]
        w_hi, w_lo, proj_done, evac = (sem(n) for n in ("w_hi", "w_lo", "proj_done", "evac"))
        out_stored = [sem(f"out_stored{i}") for i in range(NBC)]
        wpool_in, sp_in, spT_done, spT_ready, pad_ready = (sem(n) for n in ("wpool_in", "sp_in", "spT_done", "spT_ready", "pad_ready"))
        window, mix_ready, pool_done, biased, gated, tail_saved, tail_T, tail_ready = (
            sem(n) for n in ("window", "mix_ready", "pool_done", "biased", "gated", "tail_saved", "tail_T", "tail_ready"))
        b_stored = [sem(f"b_stored{i}") for i in range(2)]

        def cols_of(c):
            return slice(c * BCH, min((c + 1) * BCH, TT))

        def width(c):
            return cols_of(c).stop - cols_of(c).start

        def column(kind, i):
            return {"u": CU, "zb": CZB, "za": CZA, "g": CGA}[kind] + i * P

        with nc.Block() as block:
            @block.sync
            def _(sp):
                def load(n, slot, col):
                    sp.wait_ge(w_lo, after(n - 2))
                    apart(sp, v["passed"])
                    sp.dma_start(wst[slot][:, :, :], w_in_v[:, :, bass.ds(col, P)]).then_inc(w_landed[slot], 16)

                def store_b(p):
                    for c in range(NBC):
                        m = p * NBC + c
                        sp.wait_ge(gated, m + 1)
                        apart(sp, v["passed"])
                        sp.dma_start(bT_dram[p, :, cols_of(c)], gst[m % 2][:, 0:width(c)]).then_inc(b_stored[m % 2], 16)

                load(0, 0, column("u", 0))
                sp.dma_start(wpool[:, :, :], v["w_pool"][0].rearrange("g c d -> c g d")).then_inc(wpool_in, 16)
                sp.dma_start(sp_rows[:, :], state_pool.rearrange("b j c -> (b j) c")).then_inc(sp_in, 16)
                load(1, 1, column("zb", 0))
                sp.dma_start(pool_s[:, 0:NPS - 1, :], state_pool[:, 1:NPS, :]).then_inc(late, 16)
                for p in range(1, PAIRS):
                    load(2 * p, 0, column("u", p))
                    load(2 * p + 1, 1, column("zb", p))
                    store_b(p - 1)
                with sp.Fori(0, 2) as i:
                    load(i * 2 + 8, 0, i * (2 * P) + CZA)
                    load(i * 2 + 9, 1, i * (2 * P) + (CZA + P))
                store_b(PAIRS - 1)
                with sp.Fori(0, 8) as i:
                    load(i * 2 + 12, 0, i * (2 * P) + CGA)
                    load(i * 2 + 13, 1, i * (2 * P) + (CGA + P))
                    for g in range(2):
                        shifted_copy(sp, v, g, i, bulk)
                sp.wait_ge(tail_ready, 2)
                sp.dma_start(pool_p, urow[:, :]).then_inc(late, 16)
                sp.dma_start(pool_s[:, NPS - 1, :], usrow[:, :]).then_inc(late, 16)
                sp.wait_ge(late, 48)
                for i in range(2):
                    sp.wait_ge(b_stored[i], 16 * PAIRS * NBC // 2)

            @block.gpsimd
            def _(pool):
                nc.gpsimd.memset(uT[:, 0:PADU], 0.0).then_inc(pad_ready, 1)
                for t in range(PADU):
                    nc.gpsimd.memset(recip[:, t:t + 1], 1.0 / (t + 1)).then_inc(pad_ready, 1)

                def split_hi(n, slot, landed):
                    pool.wait_ge(w_landed[slot], landed)
                    pool.wait_ge(proj_done, after((n - 1) * NBC - 1))
                    apart(pool, v["passed"])
                    nc.gpsimd.tensor_copy(wH[slot][:, :, :], wst[slot][:, :, :]).then_inc(w_hi, 1)

                with pool.Fori(0, NF // 2) as i:
                    split_hi(i * 2, 0, i * 16 + 16)
                    split_hi(i * 2 + 1, 1, i * 16 + 16)

            @block.vector
            def _(dve):
                dve.sem_inc(w_lo, LEAD)

                def split_lo(n, slot):
                    dve.wait_ge(w_hi, n + 1)
                    dve.wait_ge(proj_done, after((n - 1) * NBC - 1))
                    nc.vector.tensor_tensor(wL[slot][:, :, :], wst[slot][:, :, :], wH[slot][:, :, :].bitcast(F32),
                                            ALU.subtract).then_inc(w_lo, 1)

                steps = [0]

                def chained(ins):
                    steps[0] += 1
                    ins.then_inc(window, 1)
                    dve.wait_ge(window, steps[0])

                def windows(p):
                    w = POOLS[p]
                    dve.wait_ge(evac, after(2 * p * NBC + NBC - 1))
                    if p:
                        dve.wait_ge(pool_done, NBC * p)
                    src, first = uT, 0
                    for s in range(p + 1):
                        shift = 1 << s
                        first += shift
                        dst = run[s % 2]
                        chained(nc.vector.tensor_tensor(dst[:, first:], src[:, first:PADU + SEQ], src[:, first - shift:PADU + SEQ - shift], ALU.add))
                        src = dst
                    nc.vector.scalar_tensor_tensor(mixed[:, w:SEQ], src[:, PADU + w:], 1.0 / w, uT[:, PADU + w:PADU + SEQ], ALU.mult, ALU.subtract)
                    chained(nc.vector.tensor_tensor(src[:, PADU:PADU + w], src[:, PADU:PADU + w], recip[:, 0:w], ALU.mult))
                    nc.vector.tensor_tensor(mixed[:, 0:w], src[:, PADU:PADU + w], uT[:, PADU:PADU + w], ALU.subtract)
                    nc.vector.tensor_copy(utail[:, p, :], uT[:, PADU + SEQ - NPS:]).then_inc(tail_saved, 1)
                    u_s = uT[:, PADU + SEQ:]
                    carried = spT[:, p, :].rearrange("p (b j) -> p b j", j=NPS)[:, :, NPS - (w - 1):]
                    chained(nc.vector.tensor_reduce(s_sum[:, 0, :], carried, AX.X, ALU.add))
                    chained(nc.vector.tensor_tensor(s_sum[:, 1, :], s_sum[:, 0, :], u_s, ALU.add))
                    nc.vector.scalar_tensor_tensor(mixed[:, SEQ:TT], s_sum[:, 1, :], 1.0 / w, u_s, ALU.mult,
                                                   ALU.subtract).then_inc(mix_ready, 1)

                def gate(p):
                    for c in range(NBC):
                        m = NBC * p + c
                        dve.wait_ge(pool_done, m + 1)
                        t = pst[m % 2][:, 0:width(c)]
                        nc.vector.tensor_scalar(t, ppool[m % 2][:, 0:width(c)], vecT[:, 32 + p:33 + p], vecT[:, 36 + p:37 + p],
                                                ALU.add, ALU.mult).then_inc(biased, 1)
                        dve.wait_ge(biased, m + 1)
                        if m >= 2:
                            dve.wait_ge(b_stored[m % 2], 16 * (m // 2))
                        dve.wait_ge(evac, after((2 * p + 1) * NBC + c))
                        nc.vector.tensor_tensor(gst[m % 2][:, 0:width(c)], t, zS[:, cols_of(c)], ALU.mult).then_inc(gated, 1)

                dve.wait_ge(pad_ready, 1 + PADU)
                for p in range(PAIRS):
                    split_lo(2 * p, 0)
                    split_lo(2 * p + 1, 1)
                    if p == 0:
                        dve.wait_ge(spT_done, 1)
                        chained(nc.vector.tensor_copy(spT[:, :, :].rearrange("p g r -> p (g r)"), ppool[1][:, 0:4 * NS * NPS]))
                        nc.vector.tensor_copy(s_sum[:, 0, :], spT[:, 0, 0:NS]).then_inc(spT_ready, 1)
                    if p:
                        gate(p - 1)
                    windows(p)
                split_lo(2 * PAIRS, 0)
                split_lo(2 * PAIRS + 1, 1)
                gate(PAIRS - 1)
                with dve.Fori(0, NF // 2 - PAIRS - 1) as i:
                    split_lo(i * 2 + (2 * PAIRS + 2), 0)
                    split_lo(i * 2 + (2 * PAIRS + 3), 1)
                dve.wait_ge(tail_T, 1)
                nc.vector.tensor_copy(urow[:, :], ppool[0][0:NPS, :]).then_inc(tail_ready, 1)
                nc.vector.tensor_copy(usrow[:, :], ppool[1][0:NS, :]).then_inc(tail_ready, 1)

            @block.scalar
            def _(act):
                act.sem_inc(evac, LEAD)
                for c in range(NBC):
                    act.sem_inc(out_stored[c], LEAD_DMA)

                def chunk(n, c, out, func):
                    act.wait_ge(proj_done, after(n * NBC + c))
                    nc.scalar.activation(out, pp[c][:, 0:width(c)], func).then_inc(evac, 1)

                for p in range(PAIRS):
                    if p:
                        act.wait_ge(mix_ready, p)
                    for c in range(NBC):
                        chunk(2 * p, c, uT[:, PADU + c * BCH:PADU + c * BCH + width(c)], ACT.Copy)
                    if p:
                        act.wait_ge(gated, NBC * p)
                    for c in range(NBC):
                        chunk(2 * p + 1, c, zS[:, cols_of(c)], ACT.Silu)

                def spilled(n, func):
                    for c in range(NBC):
                        act.wait_ge(out_stored[c], n * 16 + (LEAD_DMA - 16 * 2 * PAIRS))
                        chunk(n, c, ost[c][:, 0:width(c)], func)
                        act.wait_ge(evac, after(n * NBC + c))
                        act.dma_start(gT_dram[bass.ds(n - 2 * PAIRS, 1), :, cols_of(c)].rearrange("a p t -> p (a t)"),
                                      ost[c][:, 0:width(c)]).then_inc(out_stored[c], 16)

                with act.Fori(0, 4) as i:
                    spilled(i + 2 * PAIRS, ACT.Silu)
                with act.Fori(0, 16) as i:
                    spilled(i + (2 * PAIRS + 4), ACT.Sigmoid)
                for c in range(NBC):
                    act.wait_ge(out_stored[c], LEAD_DMA + 16 * (NF - 2 * PAIRS))

            @block.tensor
            def _(pe):
                pe.sem_inc(proj_done, LEAD)

                def project(n, slot):
                    pe.wait_ge(w_lo, after(n))
                    for c in range(NBC):
                        pe.wait_ge(evac, after(n * NBC + (c - NBC)))
                        three_pass(nc, pp[c][:, 0:width(c)], [(wH[slot][:, k, :], wL[slot][:, k, :], hH[:, k, cols_of(c)], hL[:, k, cols_of(c)])
                                                              for k in range(KT)]).then_inc(proj_done, 1)

                pe.wait_ge(sp_in, 16)
                for g in range(4):
                    last = nc.tensor.transpose(ppool[1][:, g * NS * NPS:(g + 1) * NS * NPS], sp_rows[:, g * P:(g + 1) * P],
                                               ident[0:NS * NPS, 0:NS * NPS])
                last.then_inc(spT_done, 1)
                pe.wait_ge(wpool_in, 16)
                for p in range(PAIRS):
                    project(2 * p, 0)
                    project(2 * p + 1, 1)
                    pe.wait_ge(mix_ready, p + 1)
                    pe.wait_ge(spT_ready, 1)
                    for c in range(NBC):
                        m = NBC * p + c
                        if m >= 2:
                            pe.wait_ge(biased, m - 1)
                        nc.tensor.matmul(ppool[m % 2][:, 0:width(c)], wpool[:, p, :], mixed[:, cols_of(c)],
                                         start=True, stop=True).then_inc(pool_done, 1)
                with pe.Fori(0, NF // 2 - PAIRS) as i:
                    project(i * 2 + 2 * PAIRS, 0)
                    project(i * 2 + (2 * PAIRS + 1), 1)
                pe.wait_ge(tail_saved, PAIRS)
                pe.wait_ge(biased, NBC * PAIRS)
                for g in range(4):
                    nc.tensor.transpose(ppool[0][0:NPS, g * P:(g + 1) * P], utail[:, g, 0:NPS], ident[:, :])
                    last = nc.tensor.transpose(ppool[1][0:NS, g * P:(g + 1) * P], utail[:, g, NPS:], ident[:, :])
                last.then_inc(tail_T, 1)


def apart(eng, passed):
    eng.sem_inc(passed[eng.engine], 1)


def three_pass(nc, out, terms):
    last = None
    for i, (sH, sL, mH, mL) in enumerate(terms):
        nc.tensor.matmul(out, sH, mH, start=(i == 0), stop=False)
        nc.tensor.matmul(out, sH, mL, start=False, stop=False)
        last = nc.tensor.matmul(out, sL, mH, start=False, stop=(i == len(terms) - 1))
    return last


def shifted_copy(eng, v, g, b, done, piece=0, pieces=1):
    W = PATTERNS[g][0]
    n = (W - 1) * 2 * HEADS * E // pieces
    rows = (16 * (1 if g == 0 else 8 if g == 1 else 32)) // pieces
    first = piece * n
    def flat(a):
        return a[0].rearrange("b w k h e -> b (w k h e)")
    dst = flat(v["kv_s"][g])[bass.ds(b, 1), first:first + n].rearrange("o (r c) -> (o r) c", r=rows)
    src = flat(v["states"][g])[bass.ds(b, 1), first + 2 * HEADS * E:first + 2 * HEADS * E + n].rearrange("o (r c) -> (o r) c", r=rows)
    eng.dma_start(dst, src).then_inc(done, 16)


def attend(nc, scope, v):
    hH, hL, ident = v["hH"], v["hL"], v["ident"]
    w_in_v, o_dram, samp_dram, bulk = v["w_in_v"], v["o_dram"], v["samp_dram"], v["bulk"]
    SAMP = BLOCKS
    PAIR = 2
    UNITS = PAIR * GROUPS
    STEPS = UNITS * (BLOCKS + 1)
    NB = UNITS * BLOCKS
    ROUNDS = HEADS // PAIR
    plan = [(u, b, u * BLOCKS + b if b < BLOCKS else u) for u in range(UNITS) for b in range(BLOCKS + 1)]
    PIECES = 8
    PACE = STEPS // (NS // ROUNDS * PIECES)
    RKV, RQ, RT, RS, RO = 8, 2, 4, 2, 6

    def stored_rows(g, b):
        t0, d, _ = block_tokens(g, b)
        first = SEQ - PATTERNS[g][0]
        return (t0 - first, d) if t0 >= first else None

    kv_before = []
    kv_slot_total = [0] * RKV
    for u in range(UNITS):
        for b in range(BLOCKS):
            slot = (u * BLOCKS + b) % RKV
            kv_before.append(kv_slot_total[slot])
            if stored_rows(u % GROUPS, b):
                kv_slot_total[slot] += 1

    stack = ExitStack()
    with stack:
        sb, ps, sem = scope(stack)
        wst = sb("a_wst", [P, KT, 3, P])
        wH = [sb(f"a_wH{i}", [P, KT, 3 * P], F32R) for i in range(2)]
        wL = [sb(f"a_wL{i}", [P, KT, 3 * P], F32R) for i in range(2)]
        mask = sb("mask", [P, 2 * P])
        gains = sb("gains", [P, 2, GROUPS, P])
        kv = sb("kv", [P, RKV, 2, P])
        qn = sb("qn", [P, RQ, P])
        qkT = sb("qkT", [P, RT, 2, P])
        sm = sb("sm", [P, RS, 2 * P])
        pr = sb("pr", [P, RS, 2 * P])
        prT = sb("prT", [P, RS, 2 * P])
        ot = sb("ot", [P, RO, OW])
        nm = sb("nm", [P, RS])
        junk = sb("a_junk", [P, P])
        ss = sb("a_ss", [P, 2, 2])
        ms = sb("a_ms", [P, 2, 2])
        rs = sb("a_rs", [P, 2, 2])
        mhalf = sb("a_mhalf", [P, 2])
        sq = sb("sq", [NS, 2, 3, P])
        pp = [ps(f"a_pp{i}", [P, 512]) for i in range(2)]
        pqk = ps("pqk", [P, 512])
        psc = [ps(f"psc{i}", [P, 512]) for i in range(2)]
        ppt = ps("ppt", [P, 512])
        po = [ps(f"po{i}", [P, 512]) for i in range(2)]

        w_landed, gain_in, mask_step, mhalf_ready, gain_ready = (sem(n) for n in ("aw_landed", "gain_in", "mask_step", "mhalf_ready2", "gain_ready"))
        w_hi, w_lo = sem("aw_hi"), sem("aw_lo")
        proj_done, squared, act_read, meaned, powered, qk_normed = (
            sem(n) for n in ("a_proj_done", "a_squared", "act_read", "a_meaned", "a_powered", "qk_normed"))
        t_done, t_evac, s_done, s_masked, max_neg, exp_done, pt_done, pt_evac, pv_done, o_evac = (
            sem(n) for n in ("t_done", "t_evac", "s_done", "s_masked", "max_neg", "exp_done", "pt_done", "pt_evac", "pv_done", "o_evac"))
        kv_stored = [sem(f"kv_stored{i}") for i in range(RKV)]
        o_stored = [sem(f"o_stored{i}") for i in range(RO)]
        samp_stored = [sem(f"samp_stored{i}") for i in range(2)]

        def rounds(eng, body):
            with eng.Fori(0, ROUNDS) as r:
                body(r)

        def head_of(r, u):
            return r * PAIR + u // GROUPS

        def tokens(g, b):
            if b == SAMP:
                return slice(SEQ, TT)
            t0, d, _ = block_tokens(g, b)
            return slice(t0, t0 + (P - 1) * d + 1, d)

        with nc.Block() as block:
            @block.sync
            def _(sp):
                def load(r, u):
                    h, g = head_of(r, u), u % GROUPS
                    sp.wait_ge(w_lo, after((r * UNITS + u) * KT - 1))
                    apart(sp, v["passed"])
                    for i, c0 in enumerate((CQ, CK, CV)):
                        sp.dma_start(wst[:, :, i, :], w_in_v[:, :, bass.ds(h * E + (c0 + g * HEADS * E), E)]).then_inc(w_landed, 16)

                sp.dma_start(gains[:, 0, :, :].rearrange("p g e -> p (g e)"), v["q_gain"].rearrange("o g e -> o (g e)").to_broadcast([P, GROUPS * E])).then_inc(gain_in, 16)
                sp.dma_start(gains[:, 1, :, :].rearrange("p g e -> p (g e)"), v["k_gain"].rearrange("o g e -> o (g e)").to_broadcast([P, GROUPS * E])).then_inc(gain_in, 16)
                load(0, 0)

                def body(r):
                    for s in range(STEPS):
                        u, b, _ = plan[s]
                        if b == 1:
                            load(r, u + 1)
                        piece, at = divmod(s, PACE)
                        if at == 0 and piece < NS // ROUNDS * PIECES:
                            sp.wait_ge(proj_done, after(r * STEPS + s))
                            apart(sp, v["passed"])
                            shifted_copy(sp, v, 2, r * (NS // ROUNDS) + piece // PIECES, bulk, piece % PIECES, PIECES)
                rounds(sp, body)

            @block.gpsimd
            def _(pool):
                pool.sem_inc(w_hi, LEAD)
                pool.sem_inc(powered, LEAD)
                nc.gpsimd.memset(mask[:, :], 0.0).then_inc(mask_step, 1)
                nc.gpsimd.memset(mhalf[:, :], -0.5).then_inc(mhalf_ready, 1)
                pool.wait_ge(mask_step, 1)
                nc.gpsimd.affine_select(out=mask[:, 0:P], in_=mask[:, 0:P], compare_op=ALU.is_ge, fill=-MASKED,
                                        base=0, pattern=[[1, P]], channel_multiplier=-1).then_inc(mask_step, 1)
                nc.gpsimd.affine_select(out=mask[:, P:2 * P], in_=mask[:, P:2 * P], compare_op=ALU.is_ge, fill=-MASKED,
                                        base=0, pattern=[[-1, P]], channel_multiplier=1).then_inc(mask_step, 1)
                pool.wait_ge(mhalf_ready, 1)

                def split_hi(u, slot, k):
                    if k == 0:
                        pool.wait_ge(w_landed, u * 48 + 48)
                    pool.wait_ge(w_lo, after(u * KT + k - 1))
                    apart(pool, v["passed"])
                    nc.gpsimd.tensor_copy(wH[slot][:, k, :], wst[:, k, :, :].rearrange("p i c -> p (i c)")).then_inc(w_hi, 1)

                def power(r, s):
                    n = r * STEPS + s
                    rows = P if plan[s][1] < BLOCKS else NS
                    pool.wait_ge(meaned, after(n))
                    nc.gpsimd.tensor_tensor(rs[0:rows, s % 2, :], ms[0:rows, s % 2, :], mhalf[0:rows, :], ALU.pow).then_inc(powered, 1)

                for k in range(KT):
                    split_hi(0, 0, k)

                def body(r):
                    for s in range(STEPS):
                        power(r, s)
                        u, b, _ = plan[s]
                        if 4 <= b < 4 + KT:
                            split_hi(r * UNITS + (u + 1), (u + 1) % 2, b - 4)
                rounds(pool, body)

            @block.scalar
            def _(act):
                for x in (squared, act_read, t_evac, exp_done, o_evac):
                    act.sem_inc(x, LEAD)
                for x in (*kv_stored, *o_stored, *samp_stored):
                    act.sem_inc(x, LEAD_DMA)

                def project_read(r, s):
                    u, b, j = plan[s]
                    g = u % GROUPS
                    n = r * STEPS + s
                    rows = P if b < BLOCKS else NS
                    src = pp[s % 2]
                    act.wait_ge(proj_done, after(n))
                    act.wait_ge(meaned, after(n - 2))
                    for i in range(2):
                        act.wait_ge(squared, after(2 * n + i - 1))
                        nc.scalar.activation(junk[0:rows, :], src[0:rows, i * P:(i + 1) * P], ACT.Square,
                                             accum_out=ss[0:rows, s % 2, i:i + 1]).then_inc(squared, 1)
                    if b < BLOCKS:
                        jj = r * NB + j
                        act.wait_ge(pv_done, after(jj - RKV + 1))
                        act.wait_ge(kv_stored[j % RKV], r * (16 * kv_slot_total[j % RKV]) + (LEAD_DMA + 16 * kv_before[j]))
                        nc.scalar.activation(kv[:, j % RKV, 1, :], src[:, 2 * P:3 * P], ACT.Copy).then_inc(act_read, 1)
                    else:
                        act.wait_ge(samp_stored[j % 2], r * (32 * UNITS // 2) + (LEAD_DMA + 32 * (j // 2)))
                        nc.scalar.activation(sq[:, j % 2, 2, :], src[0:NS, 2 * P:3 * P], ACT.Copy).then_inc(act_read, 1)

                def store_kv(r, s):
                    u, b, j = plan[s]
                    g, h = u % GROUPS, head_of(r, u)
                    n = r * STEPS + s
                    if b < BLOCKS:
                        at = stored_rows(g, b)
                        if at is None:
                            return
                        act.wait_ge(qk_normed, after(n))
                        act.wait_ge(act_read, after(n))
                        act.dma_start(strided(v["kv_p"][g][0, 0], at[0], P, at[1])[:, :, bass.ds(h, 1), :].rearrange("t k o e -> t k (o e)"),
                                      kv[:, j % RKV, :, :]).then_inc(kv_stored[j % RKV], 16)
                    else:
                        act.wait_ge(qk_normed, after(n))
                        act.wait_ge(act_read, after(n))
                        act.dma_start(samp_dram[:, :, bass.ds(h + g * HEADS, 1), :].rearrange("b i o e -> b i (o e)"),
                                      sq[:, j % 2, :, :]).then_inc(samp_stored[j % 2], 16)
                        act.dma_start(v["kv_s"][g][0, :, PATTERNS[g][0] - 1, :, bass.ds(h, 1), :].rearrange("b k o e -> b k (o e)"),
                                      sq[:, j % 2, 1:3, :]).then_inc(samp_stored[j % 2], 16)

                def evac_T(r, s):
                    u, b, j = plan[s]
                    g = u % GROUPS
                    if b == SAMP:
                        return
                    jj = r * NB + j
                    act.wait_ge(t_done, after(jj))
                    act.wait_ge(s_done, after(jj - RT + 1))
                    nc.scalar.activation(qkT[:, j % RT, :, :].rearrange("p i t -> p (i t)"), pqk[:, 0:2 * P], ACT.Copy).then_inc(t_evac, 1)

                def exponent(r, s):
                    u, b, j = plan[s]
                    g = u % GROUPS
                    if b == SAMP:
                        return
                    jj = r * NB + j
                    lo = 0 if block_tokens(g, b)[2] else P
                    act.wait_ge(max_neg, after(jj))
                    act.wait_ge(pt_done, after(jj - RS))
                    nc.scalar.activation(pr[:, j % RS, lo:], sm[:, j % RS, lo:], ACT.Exp, bias=nm[:, j % RS:j % RS + 1],
                                         accum_out=ot[:, j % RO, E:E + 1]).then_inc(exp_done, 1)

                def output(r, s):
                    u, b, j = plan[s]
                    g, h = u % GROUPS, head_of(r, u)
                    if b == SAMP:
                        return
                    jj = r * NB + j
                    t0, d, _ = block_tokens(g, b)
                    act.wait_ge(pv_done, after(jj))
                    nc.scalar.activation(ot[:, j % RO, 0:E], po[j % 2][:, 0:E], ACT.Copy).then_inc(o_evac, 1)
                    act.wait_ge(o_evac, after(jj))
                    act.dma_start(strided(o_dram, t0, P, d)[:, bass.ds(h + g * HEADS, 1), :].rearrange("t o e -> t (o e)"),
                                  ot[:, j % RO, :]).then_inc(o_stored[j % RO], 16)

                def body(r):
                    for s in range(STEPS + 4):
                        if s < STEPS:
                            project_read(r, s)
                        if 0 <= s - 1 < STEPS:
                            evac_T(r, s - 1)
                            store_kv(r, s - 1)
                        if 0 <= s - 2 < STEPS:
                            exponent(r, s - 2)
                        if 0 <= s - 4 < STEPS:
                            output(r, s - 4)
                rounds(act, body)
                for i in range(RKV):
                    act.wait_ge(kv_stored[i], LEAD_DMA + 16 * ROUNDS * kv_slot_total[i])
                for i in range(RO):
                    act.wait_ge(o_stored[i], LEAD_DMA + 16 * ROUNDS * NB // RO)
                for i in range(2):
                    act.wait_ge(samp_stored[i], LEAD_DMA + 16 * ROUNDS * UNITS)

            @block.vector
            def _(dve):
                for x in (w_lo, meaned, qk_normed, s_masked, max_neg, pt_evac):
                    dve.sem_inc(x, LEAD)
                dve.wait_ge(gain_in, 32)
                nc.vector.tensor_scalar(gains[:, 0, :, :], gains[:, 0, :, :], float(E) ** -0.5, None, ALU.mult).then_inc(gain_ready, 1)

                def split_lo(u, slot, k):
                    dve.wait_ge(w_hi, after(u * KT + k))
                    nc.vector.tensor_tensor(wL[slot][:, k, :], wst[:, k, :, :].rearrange("p i c -> p (i c)"),
                                            wH[slot][:, k, :].bitcast(F32), ALU.subtract).then_inc(w_lo, 1)

                def mean(r, s):
                    u, b, j = plan[s]
                    g = u % GROUPS
                    n = r * STEPS + s
                    rows = P if b < BLOCKS else NS
                    dve.wait_ge(squared, after(2 * n + 1))
                    dve.wait_ge(powered, after(n - 1))
                    nc.vector.tensor_scalar(ms[0:rows, s % 2, :], ss[0:rows, s % 2, :], 1.0 / E, EPS, ALU.mult, ALU.add).then_inc(meaned, 1)

                def normalise(r, s):
                    u, b, j = plan[s]
                    g = u % GROUPS
                    n = r * STEPS + s
                    rows = P if b < BLOCKS else NS
                    src = pp[s % 2]
                    dve.wait_ge(powered, after(n))
                    if b < BLOCKS:
                        jj = r * NB + j
                        dve.wait_ge(t_done, after(jj - RQ))
                        qdst, kdst = qn[:, j % RQ, :], kv[:, j % RKV, 0, :]
                    else:
                        qdst, kdst = sq[:, j % 2, 0, :], sq[:, j % 2, 1, :]
                    dve.wait_ge(act_read, after(n))
                    nc.vector.scalar_tensor_tensor(qdst, src[0:rows, 0:P], rs[0:rows, s % 2, 0:1], gains[0:rows, 0, g, :], ALU.mult, ALU.mult)
                    nc.vector.scalar_tensor_tensor(kdst, src[0:rows, P:2 * P], rs[0:rows, s % 2, 1:2], gains[0:rows, 1, g, :],
                                                   ALU.mult, ALU.mult).then_inc(qk_normed, 1)

                def mask_max(r, s):
                    u, b, j = plan[s]
                    g = u % GROUPS
                    if b == SAMP:
                        return
                    jj = r * NB + j
                    lo = 0 if block_tokens(g, b)[2] else P
                    dve.wait_ge(s_done, after(jj))
                    dve.wait_ge(exp_done, after(jj - RS))
                    dve.wait_ge(o_stored[j % RO], r * (16 * NB // RO) + (LEAD_DMA + 16 * (j // RO)))
                    apart(dve, v["passed"])
                    nc.vector.tensor_tensor_reduce(sm[:, j % RS, lo:], psc[j % 2][:, lo:2 * P], mask[:, lo:], 1.0, -3e38,
                                                   ALU.subtract, ALU.max, ot[:, j % RO, E + 1:E + 2]).then_inc(s_masked, 1)
                    dve.wait_ge(s_masked, after(jj))
                    nc.vector.tensor_scalar(nm[:, j % RS:j % RS + 1], ot[:, j % RO, E + 1:E + 2], -1.0, None, ALU.mult).then_inc(max_neg, 1)

                def evac_PT(r, s):
                    u, b, j = plan[s]
                    g = u % GROUPS
                    if b == SAMP:
                        return
                    jj = r * NB + j
                    lo = 0 if block_tokens(g, b)[2] else P
                    dve.wait_ge(pt_done, after(jj))
                    dve.wait_ge(pv_done, after(jj - RS))
                    nc.vector.tensor_copy(prT[:, j % RS, lo:], ppt[:, lo:2 * P]).then_inc(pt_evac, 1)

                for k in range(KT):
                    split_lo(0, 0, k)
                dve.wait_ge(mask_step, 3)
                dve.wait_ge(gain_ready, 1)

                def body(r):
                    for s in range(STEPS + 4):
                        if s < STEPS:
                            mean(r, s)
                        if 0 <= s - 2 < STEPS:
                            mask_max(r, s - 2)
                        if s < STEPS:
                            normalise(r, s)
                        if 0 <= s - 3 < STEPS:
                            evac_PT(r, s - 3)
                        if s < STEPS:
                            u, b, _ = plan[s]
                            if 4 <= b < 4 + KT:
                                split_lo(r * UNITS + (u + 1), (u + 1) % 2, b - 4)
                rounds(dve, body)

            @block.tensor
            def _(pe):
                for x in (proj_done, t_done, s_done, pt_done, pv_done):
                    pe.sem_inc(x, LEAD)

                def project(r, s, slot):
                    u, b, j = plan[s]
                    g = u % GROUPS
                    n = r * STEPS + s
                    rows = P if b < BLOCKS else NS
                    cols = tokens(g, b)
                    pe.wait_ge(act_read, after(n - 2))
                    pe.wait_ge(qk_normed, after(n - 2))
                    if b == 0:
                        pe.wait_ge(w_lo, after((r * UNITS + u) * KT + KT - 1))
                    three_pass(nc, pp[s % 2][0:rows, 0:3 * P], [(hH[:, k, cols], hL[:, k, cols], wH[slot][:, k, :], wL[slot][:, k, :])
                                                                for k in range(KT)]).then_inc(proj_done, 1)

                def transposes(r, s):
                    u, b, j = plan[s]
                    g = u % GROUPS
                    if b == SAMP:
                        return
                    jj = r * NB + j
                    pe.wait_ge(qk_normed, after(r * STEPS + s))
                    pe.wait_ge(t_evac, after(jj - 1))
                    nc.tensor.transpose(pqk[:, 0:P], qn[:, j % RQ, :], ident[:, :])
                    nc.tensor.transpose(pqk[:, P:2 * P], kv[:, j % RKV, 0, :], ident[:, :]).then_inc(t_done, 1)

                def scores(r, s):
                    u, b, j = plan[s]
                    g = u % GROUPS
                    if b == SAMP:
                        return
                    jj = r * NB + j
                    prev = block_tokens(g, b)[2]
                    pe.wait_ge(t_evac, after(jj))
                    pe.wait_ge(s_masked, after(jj - 2))
                    if prev:
                        nc.tensor.matmul(psc[j % 2][:, 0:P], qkT[:, j % RT, 0, :], qkT[:, (j - 1) % RT, 1, :], start=True, stop=True)
                    nc.tensor.matmul(psc[j % 2][:, P:2 * P], qkT[:, j % RT, 0, :], qkT[:, j % RT, 1, :], start=True, stop=True).then_inc(s_done, 1)

                def probs_T(r, s):
                    u, b, j = plan[s]
                    g = u % GROUPS
                    if b == SAMP:
                        return
                    jj = r * NB + j
                    pe.wait_ge(exp_done, after(jj))
                    pe.wait_ge(pt_evac, after(jj - 1))
                    if block_tokens(g, b)[2]:
                        nc.tensor.transpose(ppt[:, 0:P], pr[:, j % RS, 0:P], ident[:, :])
                    nc.tensor.transpose(ppt[:, P:2 * P], pr[:, j % RS, P:2 * P], ident[:, :]).then_inc(pt_done, 1)

                def values(r, s):
                    u, b, j = plan[s]
                    g = u % GROUPS
                    if b == SAMP:
                        return
                    jj = r * NB + j
                    prev = block_tokens(g, b)[2]
                    pe.wait_ge(pt_evac, after(jj))
                    pe.wait_ge(o_evac, after(jj - 2))
                    if prev:
                        nc.tensor.matmul(po[j % 2][:, 0:E], prT[:, j % RS, 0:P], kv[:, (j - 1) % RKV, 1, :], start=True, stop=False)
                    nc.tensor.matmul(po[j % 2][:, 0:E], prT[:, j % RS, P:2 * P], kv[:, j % RKV, 1, :], start=not prev, stop=True).then_inc(pv_done, 1)

                def body(r):
                    for s in range(STEPS + 4):
                        if s < STEPS:
                            project(r, s, plan[s][0] % 2)
                        if 0 <= s - 1 < STEPS:
                            transposes(r, s - 1)
                        if 0 <= s - 2 < STEPS:
                            scores(r, s - 2)
                        if 0 <= s - 3 < STEPS:
                            probs_T(r, s - 3)
                        if 0 <= s - 4 < STEPS:
                            values(r, s - 4)
                rounds(pe, body)


def merge(nc, scope, v):
    stack = ExitStack()
    with stack:
        sb, _, _ = scope(stack)
        wH = sb("m_wH", [P, 16, D], F32R)
        wL = sb("m_wL", [P, 16, D], F32R)
        aTs = sb("aTs", [P, HEADS, NS])
        decode(nc, scope, v, wH, wL, aTs)
        v["end_phase"]()
        combine(nc, scope, v, wH, wL, aTs)


def decode(nc, scope, v, wH, wL, aTs):
    ident, sampT, bTs, samp_dram, snew_dram, pnew_dram, states = (v[n] for n in ("ident", "sampT", "bTs", "samp_dram", "snew_dram", "pnew_dram", "states"))
    w_a, w_b, w_o = v["w_a_out"][0], v["w_b_out"][0], v["w_out"][0]
    BH = NS * HEADS
    HE = HEADS * E
    stack = ExitStack()
    with stack:
        sb, ps, sem = scope(stack)
        wst = [sb(f"d_wst{i}", [P, D]) for i in range(2)]
        kt = [sb(f"kt{g}", [P, HE]) for g in range(GROUPS)]
        qb = [sb(f"qb{g}", [P, HE]) for g in range(GROUPS)]
        vt = [sb(f"vt{g}", [P, HE]) for g in range(GROUPS)]
        prod = sb("prod", [P, HE])
        sc = sb("sc", [P, GROUPS, BH])
        qkv = sb("qkv", [NS, 3, NO, E])
        nprod = sb("nprod", [NS, NO, E])
        snew = sb("snew", [NS, HEADS, GROUPS])
        scr = sb("scr", [BH, GROUPS * P])
        scn = sb("scn", [BH, GROUPS])
        st = sb("st", [BH, 8])
        pcr = sb("pcr", [BH, GROUPS * P])
        pcn = sb("pcn", [BH, GROUPS])
        pT = sb("pT", [P, GROUPS, BH])
        pn = sb("pn", [NS, NO])
        diag = sb("diag", [NS, NO, NS])
        psT = ps("d_psT", [P, 512])
        psP = ps("d_psP", [P, 512])
        psA = ps("d_psA", [P, 512])
        names = ("d_hi", "d_lo", "qkv_in", "dstep", "scored", "multiplied", "snew_ready", "snew_out", "snew_in", "scT_done", "scr_ready",
                 "max_ready", "dexp", "p_ready", "pn_out", "pn_in", "pT_done", "pT_ready", "diag_ready", "pv_used", "aTs_ready", "samp_cols_in")
        (d_hi, d_lo, qkv_in, dstep, scored, multiplied, snew_ready, snew_out, snew_in, scT_done, scr_ready,
         max_ready, dexp, p_ready, pn_out, pn_in, pT_done, pT_ready, diag_ready, pv_used, aTs_ready, samp_cols_in) = (sem(n) for n in names)
        wd_landed = [sem(f"wd_landed{i}") for i in range(2)]
        k_landed = [sem(f"k_landed{g}") for g in range(GROUPS)]
        q_landed = [sem(f"q_landed{g}") for g in range(GROUPS)]
        v_landed = [sem(f"v_landed{g}") for g in range(GROUPS)]

        def carried(g, b, which):
            W, d = PATTERNS[g]
            rows = states[g][0, bass.ds(b, 1), :, which, :, :].rearrange("o w h e -> (o w) (h e)")
            return strided(rows, 0, P, d)

        with nc.Block() as block:
            @block.sync
            def _(sp):
                sp.dma_start(qkv[:, :, :, :].rearrange("b i n e -> b (i n e)"), samp_dram.rearrange("b i n e -> b (i n e)")).then_inc(qkv_in, 16)
                with sp.Fori(0, NS) as b:
                    for g in range(GROUPS):
                        sp.wait_ge(scored, after(b * GROUPS + (g - GROUPS)))
                        apart(sp, v["passed"])
                        sp.dma_start(kt[g][:, :], carried(g, b, 0)).then_inc(k_landed[g], 16)
                        sp.dma_start(qb[g][:, :], samp_dram[bass.ds(b, 1), 0, g * HEADS:(g + 1) * HEADS, :].rearrange("o h e -> o (h e)")
                                     .to_broadcast([P, HE])).then_inc(q_landed[g], 16)
                sp.dma_start(sampT[:, :, :], v["gT_dram"][:, :, SEQ:TT].rearrange("f p t -> p f t")).then_inc(samp_cols_in, 16)
                sp.dma_start(bTs[:, :, :], v["bT_dram"][:, :, SEQ:TT].rearrange("f p t -> p f t")).then_inc(samp_cols_in, 16)
                sp.wait_ge(snew_ready, 1)
                sp.dma_start(snew_dram.rearrange("b h g -> b (h g)"), snew[:, :, :].rearrange("b h g -> b (h g)")).then_inc(snew_out, 16)
                sp.wait_ge(snew_out, 16)
                sp.dma_start(scn[:, :], snew_dram.rearrange("b h g -> (b h) g")).then_inc(snew_in, 16)
                sp.wait_ge(p_ready, 2)
                sp.dma_start(pnew_dram.rearrange("b h g -> (b h) g"), pcn[:, :]).then_inc(pn_out, 16)
                sp.wait_ge(pn_out, 16)
                sp.dma_start(pn[:, :], pnew_dram.rearrange("b h g -> b (h g)")).then_inc(pn_in, 16)
                with sp.Fori(0, NS) as b:
                    for g in range(GROUPS):
                        sp.wait_ge(pv_used, after(b * GROUPS + (g - GROUPS)))
                        apart(sp, v["passed"])
                        sp.dma_start(vt[g][:, :], carried(g, b, 1)).then_inc(v_landed[g], 16)

            @block.gpsimd
            def _(pool):
                def hi(n, slot, landed):
                    pool.wait_ge(wd_landed[slot], landed)
                    apart(pool, v["passed"])
                    nc.gpsimd.tensor_copy(wH[:, bass.ds(n, 1), :].rearrange("p o c -> p (o c)"), wst[slot][:, :]).then_inc(d_hi, 1)
                with pool.Fori(0, 8) as i:
                    hi(i * 2, 0, i * 16 + 16)
                    hi(i * 2 + 1, 1, i * 16 + 16)

            @block.scalar
            def _(act):
                def load(n, slot, src):
                    act.wait_ge(d_lo, after(n - 2))
                    act.dma_start(wst[slot][:, :], src).then_inc(wd_landed[slot], 16)
                for n0, w, count in ((0, w_a, 2), (4, w_b, 2), (8, w_o, 4)):
                    with act.Fori(0, count) as i:
                        for slot in range(2):
                            load(i * 2 + (n0 + slot), slot, w[bass.ds(i * (2 * P) + slot * P, P), :])
                act.wait_ge(max_ready, 1)
                nc.scalar.activation(pcr[:, :], scr[:, :], ACT.Exp, bias=st[:, 2:3], accum_out=st[:, 3:4]).then_inc(dexp, 1)
                act.wait_ge(snew_in, 16)
                nc.scalar.activation(pcn[:, :], scn[:, :], ACT.Exp, bias=st[:, 2:3], accum_out=st[:, 4:5]).then_inc(dexp, 1)

            @block.vector
            def _(dve):
                dve.sem_inc(d_lo, LEAD)
                dve.sem_inc(scored, LEAD)

                def lo(n, slot):
                    one = bass.ds(n, 1)
                    dve.wait_ge(d_hi, n + 1)
                    nc.vector.tensor_tensor(wL[:, one, :].rearrange("p o c -> p (o c)"), wst[slot][:, :],
                                            wH[:, one, :].bitcast(F32).rearrange("p o c -> p (o c)"), ALU.subtract).then_inc(d_lo, 1)

                with dve.Fori(0, NS) as b:
                    lo(b * 2, 0)
                    lo(b * 2 + 1, 1)
                    for g in range(GROUPS):
                        dve.wait_ge(k_landed[g], b * 16 + 16)
                        dve.wait_ge(q_landed[g], b * 16 + 16)
                        dve.wait_ge(scored, after(b * GROUPS + (g - 1)))
                        nc.vector.tensor_tensor(prod[:, :], kt[g][:, :], qb[g][:, :], ALU.mult).then_inc(multiplied, 1)
                        dve.wait_ge(multiplied, b * GROUPS + (g + 1))
                        nc.vector.tensor_reduce(sc[:, g, bass.ds(b * HEADS, HEADS)], prod[:, :].rearrange("p (h e) -> p h e", e=E),
                                                AX.X, ALU.add).then_inc(scored, 1)

                steps = [0]

                def chained(ins):
                    steps[0] += 1
                    ins.then_inc(dstep, 1)
                    dve.wait_ge(dstep, steps[0])

                dve.wait_ge(qkv_in, 16)
                chained(nc.vector.tensor_tensor(nprod[:, :, :], qkv[:, 0, :, :], qkv[:, 1, :, :], ALU.mult))
                nc.vector.tensor_reduce(snew[:, :, :].rearrange("b h g -> b g h"), nprod[:, :, :].rearrange("b (g h) e -> b g h e", h=HEADS),
                                        AX.X, ALU.add).then_inc(snew_ready, 1)
                dve.wait_ge(scT_done, 1)
                chained(nc.vector.tensor_copy(scr[:, :], psT[0:BH, 0:GROUPS * P]))
                dve.wait_ge(snew_in, 16)
                nc.vector.tensor_reduce(st[:, 0:1], scr[:, :], AX.X, ALU.max)
                chained(nc.vector.tensor_reduce(st[:, 1:2], scn[:, :], AX.X, ALU.max))
                chained(nc.vector.tensor_tensor(st[:, 5:6], st[:, 0:1], st[:, 1:2], ALU.max))
                nc.vector.tensor_scalar(st[:, 2:3], st[:, 5:6], -1.0, None, ALU.mult).then_inc(max_ready, 1)
                dve.wait_ge(dexp, 2)
                chained(nc.vector.tensor_tensor(st[:, 6:7], st[:, 3:4], st[:, 4:5], ALU.add))
                chained(nc.vector.reciprocal(st[:, 7:8], st[:, 6:7]))
                nc.vector.tensor_scalar(pcr[:, :], pcr[:, :], st[:, 7:8], None, ALU.mult).then_inc(p_ready, 1)
                nc.vector.tensor_scalar(pcn[:, :], pcn[:, :], st[:, 7:8], None, ALU.mult).then_inc(p_ready, 1)
                dve.wait_ge(pT_done, 1)
                nc.vector.tensor_copy(pT[:, :, :].rearrange("p g n -> p (g n)"), psP[:, 0:GROUPS * BH]).then_inc(pT_ready, 1)
                dve.wait_ge(pn_in, 16)
                nc.vector.tensor_tensor(diag[:, :, :], pn[:, :].unsqueeze(2).to_broadcast([NS, NO, NS]),
                                        ident[0:NS, 0:NS].unsqueeze(1).to_broadcast([NS, NO, NS]), ALU.mult).then_inc(diag_ready, 1)
                dve.wait_ge(pv_used, after(NS * GROUPS - 1))
                dve.wait_ge(samp_cols_in, 32)
                nc.vector.tensor_tensor(aTs[:, :, :], psA[:, 0:BH].rearrange("p (h b) -> p h b", b=NS), sampT[:, 0:4, :],
                                        ALU.mult).then_inc(aTs_ready, 1)

            @block.tensor
            def _(pe):
                pe.sem_inc(pv_used, LEAD)
                pe.wait_ge(scored, after(NS * GROUPS - 1))
                for g in range(GROUPS):
                    last = nc.tensor.transpose(psT[0:BH, g * P:(g + 1) * P], sc[:, g, :], ident[:, :])
                last.then_inc(scT_done, 1)
                pe.wait_ge(p_ready, 1)
                for g in range(GROUPS):
                    last = nc.tensor.transpose(psP[:, g * BH:(g + 1) * BH], pcr[:, g * P:(g + 1) * P], ident[0:BH, 0:BH])
                last.then_inc(pT_done, 1)
                pe.wait_ge(diag_ready, 1)
                pe.wait_ge(qkv_in, 16)
                for h in range(HEADS):
                    for g in range(GROUPS):
                        nc.tensor.matmul(psA[:, h * NS:(h + 1) * NS], qkv[:, 2, g * HEADS + h, :], diag[:, h * GROUPS + g, :],
                                         start=(h == 0 and g == 0), stop=False, skip_group_check=True)
                pe.wait_ge(pT_ready, 1)
                with pe.Fori(0, NS) as b:
                    for g in range(GROUPS):
                        pe.wait_ge(v_landed[g], b * 16 + 16)
                        for h in range(HEADS):
                            last = nc.tensor.matmul(psA[:, bass.ds(b + h * NS, 1)], vt[g][:, h * E:(h + 1) * E],
                                                    pT[:, g, bass.ds(b * HEADS + h, 1)], start=False, stop=True, skip_group_check=True)
                        last.then_inc(pv_used, 1)


def combine(nc, scope, v, wH, wL, aTs):
    ident, sampT, bTs = v["ident"], v["sampT"], v["bTs"]
    o_dram, bT_dram, gT_dram, gate_dram = v["o_dram"], v["bT_dram"], v["gT_dram"], v["gate_dram"]
    xp, yp, xs, ys = v["xp"], v["yp"], v["xs"], v["ys"]
    NT, CW = 2, 2 * P
    NC = SEQ // CW
    RG, RA = 4, 2
    stack = ExitStack()
    with stack:
        sb, ps, sem = scope(stack)
        ol = [sb(f"ol{i}", [P, NO, OW]) for i in range(NT)]
        bl = sb("bl", [P, 4, CW])
        zl = sb("zl", [P, 4, CW])
        gl = [sb(f"gl{i}", [P, 2, CW]) for i in range(RG)]
        xl = [sb(f"xl{i}", [P, D]) for i in range(NT)]
        yst = [sb(f"yst{i}", [P, D]) for i in range(NT)]
        a32 = sb("a32", [P, 4, CW])
        abH = sb("abH", [P, KT, CW], F32R)
        abL = sb("abL", [P, KT, CW], F32R)
        mH = sb("mH", [P, KT, CW], F32R)
        mL = sb("mL", [P, KT, CW], F32R)
        gm = [sb(f"gm{i}", [P, 2, CW]) for i in range(2)]
        m32 = [sb(f"m32{i}", [P, CW]) for i in range(2)]
        gate_b = sb("gate_b", [P, D])
        cw = sb("cw", [P, NT, 5, NO])
        pT = ps("c_pT", [P, 512])
        pa = [ps(f"c_pa{i}", [P, 512]) for i in range(RA)]
        py = [ps(f"c_py{i}", [P, 512]) for i in range(2)]
        pz = ps("c_pz", [P, 512])

        names = ("cstep", "bl_in", "zl_in", "gate_in", "cexp", "cdiff", "weighted", "a_ready", "aT_done", "aT_gated", "ab_hi", "ab_lo",
                 "pa_done", "gmul", "m_sum", "m_hi", "m_lo", "y_done", "y_mul", "y_ready", "samp_in", "s_hi", "s_lo", "s_done", "s_step", "s_out")
        (cstep, bl_in, zl_in, gate_in, cexp, cdiff, weighted, a_ready, aT_done, aT_gated, ab_hi, ab_lo,
         pa_done, gmul, m_sum, m_hi, m_lo, y_done, y_mul, y_ready, samp_in, s_hi, s_lo, s_done, s_step, s_out) = (sem("c_" + n) for n in names)
        ol_in = [sem(f"ol_in{i}") for i in range(NT)]
        gl_in = [sem(f"gl_in{i}") for i in range(RG)]
        xl_in = [sem(f"xl_in{i}") for i in range(NT)]
        y_out = [sem(f"y_out{i}") for i in range(NT)]

        def chunks(eng, body):
            with eng.Fori(0, NC - 1) as c:
                body(c, False)
            body(NC - 1, True)

        with nc.Block() as block:
            @block.sync
            def _(sp):
                def attention(c):
                    for i in range(NT):
                        sp.wait_ge(aT_gated, after(c * NT + (i - NT)))
                        apart(sp, v["passed"])
                        sp.dma_start(ol[i][:, :, :].rearrange("p n e -> p (n e)"),
                                     o_dram[bass.ds(c * CW + i * P, P), :, :].rearrange("t n e -> t (n e)")).then_inc(ol_in[i], 16)
                    sp.wait_ge(aT_gated, after(c * NT - 1))
                    apart(sp, v["passed"])
                    sp.dma_start(zl[:, :, :], gT_dram[0:4, :, bass.ds(c * CW, CW)].rearrange("f p t -> p f t")).then_inc(zl_in, 16)
                    sp.wait_ge(ab_lo, after(c * 2 - 1))
                    apart(sp, v["passed"])
                    sp.dma_start(bl[:, :, :], bT_dram[:, :, bass.ds(c * CW, CW)].rearrange("f p t -> p f t")).then_inc(bl_in, 16)

                def gates(c, fs):
                    for f in fs:
                        sp.wait_ge(gmul, after(c * KT + (f - RG)))
                        apart(sp, v["passed"])
                        pair = gT_dram[4:20, :, bass.ds(c * CW, CW)].rearrange("(a f) p t -> f p a t", f=KT)
                        sp.dma_start(gl[f % RG][:, :, :], pair[f]).then_inc(gl_in[f % RG], 16)

                sp.dma_start(gate_b[:, :], gate_dram[0:1, :].to_broadcast([P, D])).then_inc(gate_in, 16)
                attention(0)

                def body(c, last):
                    gates(c, range(0, RG))
                    for i in range(NT):
                        sp.wait_ge(y_ready, after((c * NT + (i - NT)) * 2 + 1))
                        apart(sp, v["passed"])
                        sp.dma_start(xl[i][:, :], xp[bass.ds(c * CW + i * P, P), :]).then_inc(xl_in[i], 16)
                    if not last:
                        attention(c + 1)
                    gates(c, range(RG, KT))
                chunks(sp, body)
                sp.wait_ge(y_ready, after(NC * NT * 2 - 1))
                sp.dma_start(xl[0][0:NS, :], xs).then_inc(samp_in, 16)
                sp.dma_start(xl[1][0:NS, :], gate_dram[1:1 + NS, :]).then_inc(samp_in, 16)
                sp.wait_ge(y_ready, after(NC * NT * 2 + 1))
                sp.dma_start(ys, yst[0][0:NS, :]).then_inc(s_out, 16)
                sp.wait_ge(s_out, 16)
                sp.wait_ge(v["bulk"], 16 * (2 * NS + 8 * NS))
                sp.wait_ge(v["late"], 48)

            @block.gpsimd
            def _(pool):
                def split(c):
                    pool.wait_ge(pa_done, after(c * KT - 1))
                    pool.wait_ge(bl_in, c * 16 + 16)
                    apart(pool, v["passed"])
                    nc.gpsimd.tensor_copy(abH[:, 4:8, :], bl[:, :, :]).then_inc(ab_hi, 1)
                    pool.wait_ge(aT_gated, after(c * NT + 1))
                    apart(pool, v["passed"])
                    nc.gpsimd.tensor_copy(abH[:, 0:4, :], a32[:, :, :]).then_inc(ab_hi, 1)
                split(0)

                def body(c, last):
                    if not last:
                        split(c + 1)
                chunks(pool, body)

            @block.scalar
            def _(act):
                act.sem_inc(m_hi, LEAD)
                for x in y_out:
                    act.sem_inc(x, LEAD_DMA)

                def weights(t, i):
                    act.wait_ge(cdiff, t + 1)
                    nc.scalar.activation(cw[:, i, 2, :], cw[:, i, 1, :], ACT.Exp).then_inc(cexp, 1)

                def body(c, last):
                    for f in range(KT):
                        act.wait_ge(m_sum, after(c * KT + f))
                        act.wait_ge(y_done, after(c * (2 * NT) - 1))
                        nc.scalar.activation(mH[:, f, :], m32[f % 2][:, :], ACT.Copy).then_inc(m_hi, 1)
                        if f % 4 == 3 and not last:
                            weights(c * NT + (NT + f // 4), f // 4)
                    for i in range(NT):
                        act.wait_ge(y_ready, after((c * NT + i) * 2 + 1))
                        act.dma_start(yp[bass.ds(c * CW + i * P, P), :], yst[i][:, :]).then_inc(y_out[i], 16)
                weights(0, 0)
                weights(1, 1)
                chunks(act, body)
                for i in range(NT):
                    act.wait_ge(y_out[i], LEAD_DMA + 16 * NC)

            @block.vector
            def _(dve):
                for x in (a_ready, aT_gated, ab_lo, gmul, m_sum, m_lo, y_ready):
                    dve.sem_inc(x, LEAD)
                total = 7

                def groups(c, i):
                    t = c * NT + i
                    o = ol[i][:, :, :]
                    m, l = o[:, :, E + 1:E + 2].rearrange("p n o -> p (n o)"), o[:, :, E:E + 1].rearrange("p n o -> p (n o)")
                    by_head = lambda ap: ap.rearrange("p (g h) -> p h g", h=HEADS)
                    as_groups = lambda ap: ap.rearrange("p (g h) -> p g h", h=HEADS)
                    over = lambda ap: ap.unsqueeze(1).to_broadcast([P, GROUPS, HEADS])
                    row = lambda k: cw[:, i, k, :]
                    at = [0]

                    def chained(ins):
                        at[0] += 1
                        ins.then_inc(cstep, 1)
                        dve.wait_ge(cstep, t * total + at[0])

                    dve.wait_ge(ol_in[i], c * 16 + 16)
                    chained(nc.vector.tensor_reduce(row(0)[:, 0:HEADS], by_head(m), AX.X, ALU.max))
                    nc.vector.tensor_tensor(as_groups(row(1)), as_groups(m), over(row(0)[:, 0:HEADS]), ALU.subtract).then_inc(cdiff, 1)
                    dve.wait_ge(cexp, t + 1)
                    chained(nc.vector.tensor_tensor(row(3), row(2), l, ALU.mult))
                    chained(nc.vector.tensor_reduce(row(0)[:, 4:8], by_head(row(3)), AX.X, ALU.add))
                    chained(nc.vector.reciprocal(row(0)[:, 8:12], row(0)[:, 4:8]))
                    chained(nc.vector.tensor_tensor(as_groups(row(4)), as_groups(row(2)), over(row(0)[:, 8:12]), ALU.mult))
                    chained(nc.vector.tensor_tensor(o[:, :, 0:E], o[:, :, 0:E], row(4).unsqueeze(2).to_broadcast([P, NO, E]), ALU.mult))
                    chained(nc.vector.tensor_tensor(o[:, 0:HEADS, 0:E], o[:, 0:HEADS, 0:E], o[:, HEADS:2 * HEADS, 0:E], ALU.add))
                    nc.vector.tensor_tensor(o[:, 0:HEADS, 0:E], o[:, 0:HEADS, 0:E], o[:, 2 * HEADS:, 0:E], ALU.add).then_inc(a_ready, 1)
                    assert at[0] == total

                def gate_a(c, i):
                    t = c * NT + i
                    if i == 0:
                        dve.wait_ge(zl_in, c * 16 + 16)
                        dve.wait_ge(ab_lo, after(c * 2 - 1))
                    dve.wait_ge(aT_done, t + 1)
                    cols = slice(i * P, (i + 1) * P)
                    nc.vector.tensor_tensor(a32[:, :, cols], pT[:, :].rearrange("p (h t) -> p h t", t=P), zl[:, :, cols],
                                            ALU.mult).then_inc(aT_gated, 1)

                def split(c):
                    dve.wait_ge(ab_hi, c * 2 + 1)
                    nc.vector.tensor_tensor(abL[:, 4:8, :], bl[:, :, :], abH[:, 4:8, :].bitcast(F32), ALU.subtract).then_inc(ab_lo, 1)
                    dve.wait_ge(ab_hi, c * 2 + 2)
                    nc.vector.tensor_tensor(abL[:, 0:4, :], a32[:, :, :], abH[:, 0:4, :].bitcast(F32), ALU.subtract).then_inc(ab_lo, 1)

                def branch(c, f):
                    n = c * KT + f
                    dve.wait_ge(pa_done, after(n))
                    dve.wait_ge(gl_in[f % RG], c * (16 * KT // RG) + 16 * (f // RG + 1))
                    nc.vector.tensor_tensor(gm[f % 2][:, :, :], pa[f % RA][:, :].rearrange("p (a t) -> p a t", a=2),
                                            gl[f % RG][:, :, :], ALU.mult).then_inc(gmul, 1)
                    dve.wait_ge(gmul, after(n))
                    nc.vector.tensor_tensor(m32[f % 2][:, :], gm[f % 2][:, 0, :], gm[f % 2][:, 1, :], ALU.add).then_inc(m_sum, 1)
                    dve.wait_ge(m_hi, after(n))
                    nc.vector.tensor_tensor(mL[:, f, :], m32[f % 2][:, :], mH[:, f, :].bitcast(F32), ALU.subtract).then_inc(m_lo, 1)

                def result(c, i, j):
                    n = (c * NT + i) * 2 + j
                    cols = slice(j * 512, (j + 1) * 512)
                    dve.wait_ge(y_done, after(n))
                    if j == 0:
                        dve.wait_ge(y_out[i], c * 16 + LEAD_DMA)
                        dve.wait_ge(xl_in[i], c * 16 + 16)
                    nc.vector.tensor_tensor(yst[i][:, cols], py[j][:, :], gate_b[:, cols], ALU.mult).then_inc(y_mul, 1)
                    dve.wait_ge(y_mul, n + 1)
                    nc.vector.tensor_tensor(yst[i][:, cols], yst[i][:, cols], xl[i][:, cols], ALU.add).then_inc(y_ready, 1)

                dve.wait_ge(gate_in, 16)
                for i in range(NT):
                    groups(0, i)
                for i in range(NT):
                    gate_a(0, i)
                split(0)

                def body(c, last):
                    for f in range(KT):
                        branch(c, f)
                        if f % 4 == 3 and not last:
                            groups(c + 1, f // 4)
                    for j in range(2):
                        result(c, 0, j)
                    if not last:
                        gate_a(c + 1, 0)
                        gate_a(c + 1, 1)
                        split(c + 1)
                    for j in range(2):
                        result(c, 1, j)
                chunks(dve, body)

                dve.wait_ge(pa_done, after(NC * KT - 1))
                step = [0]

                def chained(ins):
                    step[0] += 1
                    ins.then_inc(s_step, 1)
                    dve.wait_ge(s_step, step[0])

                def split_small(H, L, src):
                    chained(nc.vector.tensor_copy(H, src))
                    nc.vector.tensor_tensor(L, src, H.bitcast(F32), ALU.subtract).then_inc(s_lo, 1)

                dve.wait_ge(y_done, after(NC * NT * 2 - 1))
                split_small(abH[:, 0:4, 0:NS], abL[:, 0:4, 0:NS], aTs[:, :, :])
                split_small(abH[:, 4:8, 0:NS], abL[:, 4:8, 0:NS], bTs[:, :, :])
                dve.wait_ge(s_done, 1)
                g2 = gm[0][:, :, 0:KT * NS].rearrange("p a (f t) -> p a f t", t=NS)
                chained(nc.vector.tensor_tensor(g2, pz[:, 0:2 * KT * NS].rearrange("p (a f t) -> p a f t", f=KT, t=NS),
                                                sampT[:, 4:20, :].rearrange("p (a f) t -> p a f t", f=KT), ALU.mult))
                ms = m32[0][:, 0:KT * NS].rearrange("p (f t) -> p f t", t=NS)
                chained(nc.vector.tensor_tensor(ms, g2[:, 0], g2[:, 1], ALU.add))
                split_small(mH[:, :, 0:NS], mL[:, :, 0:NS], ms)
                dve.wait_ge(samp_in, 32)
                for i in range(NT):
                    dve.wait_ge(y_out[i], LEAD_DMA + 16 * NC)
                for j in range(2):
                    cols = slice(j * 512, (j + 1) * 512)
                    dve.wait_ge(s_done, 2 + j)
                    chained(nc.vector.tensor_tensor(yst[0][0:NS, cols], py[j][0:NS, :], xl[1][0:NS, cols], ALU.mult))
                    nc.vector.tensor_tensor(yst[0][0:NS, cols], yst[0][0:NS, cols], xl[0][0:NS, cols], ALU.add).then_inc(y_ready, 1)

            @block.tensor
            def _(pe):
                pe.sem_inc(pa_done, LEAD)
                pe.sem_inc(y_done, LEAD)

                def transposes(c, i):
                    t = c * NT + i
                    pe.wait_ge(a_ready, after(t))
                    pe.wait_ge(aT_gated, after(t - 1))
                    for h in range(HEADS):
                        last = nc.tensor.transpose(pT[:, h * P:(h + 1) * P], ol[i][:, h, 0:E], ident[:, :])
                    last.then_inc(aT_done, 1)

                def branch(c, f):
                    n = c * KT + f
                    pe.wait_ge(gmul, after(n - RA))
                    for a in range(2):
                        last = three_pass(nc, pa[f % RA][:, a * CW:(a + 1) * CW],
                                          [(wH[:, k, f * P:(f + 1) * P], wL[:, k, f * P:(f + 1) * P], abH[:, k, :], abL[:, k, :])
                                           for k in range(4 * a, 4 * a + 4)])
                    last.then_inc(pa_done, 1)

                def result(c, i, j):
                    n = (c * NT + i) * 2 + j
                    pe.wait_ge(y_ready, after(n - 2))
                    three_pass(nc, py[j][:, :], [(mH[:, k, i * P:(i + 1) * P], mL[:, k, i * P:(i + 1) * P],
                                                  wH[:, 8 + k, j * 512:(j + 1) * 512], wL[:, 8 + k, j * 512:(j + 1) * 512])
                                                 for k in range(KT)]).then_inc(y_done, 1)

                for i in range(NT):
                    transposes(0, i)

                def body(c, last):
                    pe.wait_ge(ab_lo, after(c * 2 + 1))
                    for f in range(KT):
                        branch(c, f)
                    pe.wait_ge(m_lo, after(c * KT + KT - 1))
                    for j in range(2):
                        result(c, 0, j)
                    if not last:
                        transposes(c + 1, 0)
                    result(c, 1, 0)
                    if not last:
                        transposes(c + 1, 1)
                    result(c, 1, 1)
                chunks(pe, body)

                pe.wait_ge(s_lo, 2)
                for a in range(2):
                    for f in range(KT):
                        last = three_pass(nc, pz[:, (a * KT + f) * NS:(a * KT + f + 1) * NS],
                                          [(wH[:, k, f * P:(f + 1) * P], wL[:, k, f * P:(f + 1) * P], abH[:, k, 0:NS], abL[:, k, 0:NS])
                                           for k in range(4 * a, 4 * a + 4)])
                last.then_inc(s_done, 1)
                pe.wait_ge(s_lo, 3)
                pe.wait_ge(y_ready, after(NC * NT * 2 - 1))
                for j in range(2):
                    three_pass(nc, py[j][0:NS, :], [(mH[:, k, 0:NS], mL[:, k, 0:NS], wH[:, 8 + k, j * 512:(j + 1) * 512],
                                                     wL[:, 8 + k, j * 512:(j + 1) * 512]) for k in range(KT)]).then_inc(s_done, 1)


_INS = ["x_prompt", "x_sample", "state_kv_w128", "state_kv_w512", "state_kv_w2048", "state_pool", "c_prompt", "c_sample", "norm_g",
        "w_ada", "b_ada", "w_in", "q_gain", "k_gain", "w_pool", "b_pool", "pool_scale", "w_a_out", "w_b_out", "w_out"]
_OUTS = [(1, SEQ, D), (NS, 1, D), (1, 1, 128, 2, HEADS, E), (1, 1, 512, 2, HEADS, E), (1, 1, 2048, 2, HEADS, E), (1, 1, NPS, 512),
         (1, NS, 128, 2, HEADS, E), (1, NS, 512, 2, HEADS, E), (1, NS, 2048, 2, HEADS, E), (1, NS, NPS, 512)]


def kernel(**inputs):
    import numpy as _np
    import concourse.bacc as _bacc
    from concourse import mybir as _mybir
    from concourse.bass_utils import run_bass_kernel_spmd as _run

    nc = _bacc.Bacc("TRN2", target_bir_lowering=False, num_devices=1, dynamic_dma_scratch_size=1024)
    arrays, args = {}, []
    for name in _INS:
        a = _np.ascontiguousarray(inputs[name])
        arrays[f"in_{name}_dram"] = a
        args.append(nc.dram_tensor(f"in_{name}_dram", a.shape, _mybir.dt.from_np(a.dtype), kind="ExternalInput").ap())
    for i, shape in enumerate(_OUTS):
        args.append(nc.dram_tensor(f"out_{i}_dram", shape, F32, kind="ExternalOutput").ap())
    build(nc, *args)
    r = _run(nc, [arrays], core_ids=[0])
    return tuple(r.results[0][f"out_{i}_dram"] for i in range(len(_OUTS)))
```

```python
from contextlib import ExitStack

import concourse.bass as bass
from concourse import mybir

F32 = mybir.dt.float32
F32R = mybir.dt.float32r
ALU = mybir.AluOpType
ACT = mybir.ActivationFunctionType
AX = mybir.AxisListType

P = 128
D = 1024
KT = D // P
SEQ = 2048
NS = 8
TT = SEQ + NS
HEADS, GROUPS, E = 4, 3, 128
PATTERNS = ((128, 1), (512, 4), (2048, 16))
BLOCKS = SEQ // P
CH = 512
NCH = SEQ // CH
NBC = 5
BCH = -(-TT // NBC)
CQ, CK, CV, CZA, CU, CZB, CGA = 0, 1536, 3072, 4608, 5120, 5632, 6144
POOLS = (2, 4, 8, 16)
PADU = 16
NPS = 15
EPS = 1e-6
MASKED = -1e30
LEAD = 16
LEAD_DMA = 16
OW = E + 2
NO = GROUPS * HEADS


def after(n):
    return n + (LEAD + 1)


def block_tokens(g, b):
    d = PATTERNS[g][1]
    per = BLOCKS // d
    r, n = divmod(b, per)
    return r + d * P * n, d, n > 0


def strided(ap, start, count, step):
    return ap[start:start + (count - 1) * step + 1:step]


def build(nc, x_prompt, x_sample, state_kv_w128, state_kv_w512, state_kv_w2048, state_pool, c_prompt, c_sample,
          norm_g, w_ada, b_ada, w_in, q_gain, k_gain, w_pool, b_pool, pool_scale, w_a_out, w_b_out, w_out,
          y_p, y_s, kv128_p, kv512_p, kv2048_p, pool_p, kv128_s, kv512_s, kv2048_s, pool_s):
    states = (state_kv_w128, state_kv_w512, state_kv_w2048)
    kv_p = (kv128_p, kv512_p, kv2048_p)
    kv_s = (kv128_s, kv512_s, kv2048_s)
    xp, yp = x_prompt[0], y_p[0]
    xs = x_sample.rearrange("b s d -> (b s) d")
    ys = y_s.rearrange("b s d -> (b s) d")
    w_in_v = w_in[0].rearrange("(k p) c -> p k c", p=P)

    o_dram = nc.dram_tensor("o_dram", [SEQ, NO, OW], F32, kind="Internal").ap()
    bT_dram = nc.dram_tensor("bT_dram", [4, P, TT], F32, kind="Internal").ap()
    gT_dram = nc.dram_tensor("gT_dram", [20, P, TT], F32, kind="Internal").ap()
    samp_dram = nc.dram_tensor("samp_dram", [NS, 3, NO, E], F32, kind="Internal").ap()
    gate_dram = nc.dram_tensor("gate_dram", [1 + NS, D], F32, kind="Internal").ap()
    snew_dram = nc.dram_tensor("snew_dram", [NS, HEADS, GROUPS], F32, kind="Internal").ap()
    pnew_dram = nc.dram_tensor("pnew_dram", [NS, HEADS, GROUPS], F32, kind="Internal").ap()

    whole = ExitStack()
    phase_sems = []

    def end_phase():
        nc.clear_and_free_semaphores(phase_sems)
        phase_sems.clear()
        nc.all_engine_barrier()

    with whole:
        def scope(stack):
            def sb(name, shape, dt=F32):
                return stack.enter_context(nc.sbuf_tensor(name, shape, dt))

            def ps(name, shape, dt=F32):
                return stack.enter_context(nc.psum_tensor(name, shape, dt))

            def sem(name):
                one = nc.alloc_semaphore(name=name)
                if stack is not whole:
                    phase_sems.append(one)
                return one
            return sb, ps, sem

        keep_sb, _, keep_sem = scope(whole)
        ident = keep_sb("ident", [P, P])
        vecT = keep_sb("vecT", [P, 40])
        aTs = keep_sb("aTs", [P, HEADS, NS])
        bulk = keep_sem("bulk")
        passed = {e.engine: keep_sem(f"passed{i}") for i, e in enumerate((nc.sync, nc.gpsimd, nc.vector))}
        late = keep_sem("late")

        big = ExitStack()
        whole.enter_context(big)
        big_sb, _, _ = scope(big)
        hH = big_sb("hH", [P, KT, TT], F32R)
        hL = big_sb("hL", [P, KT, TT], F32R)

        prepare(nc, scope, locals())
        end_phase()
        attend(nc, scope, locals())
        end_phase()
        branches(nc, scope, locals())
        end_phase()
        big.close()
        combine(nc, scope, locals())


def prepare(nc, scope, v):
    xp, xs, hH, hL, ident, vecT = v["xp"], v["xs"], v["hH"], v["hL"], v["ident"], v["vecT"]
    w_ada_v = v["w_ada"][0].rearrange("(k p) c -> p k c", p=P)
    gate_dram = v["gate_dram"]
    NC = 1 + NS
    XR, WR, SR = 8, 2, 3
    NX = SEQ // P
    NH = NCH * KT
    stack = ExitStack()
    with stack:
        sb, ps, sem = scope(stack)
        rows = sb("rows", [40, P])
        c_in = sb("c_in", [NC, D])
        c_sig = sb("c_sig", [NC, D])
        scT = sb("scT", [P, KT, NC])
        b_gate = sb("b_gate", [NC, D])
        gate_sb = c_in
        w_st = [sb(f"w_st{i}", [P, KT, 512]) for i in range(WR)]
        xt = [sb(f"xt{i}", [P, D]) for i in range(XR)]
        xst = sb("xst", [NS, D])
        junk = sb("junk", [P, D], mybir.dt.bfloat16)
        ss = sb("ss", [P, NX + 1])
        ms = sb("ms", [P, NX + 1])
        rs = sb("rs", [P, NX + 1])
        mhalf = sb("mhalf", [P, 1])
        addT = sb("addT", [P, KT, NC])
        scl1 = sb("scl1", [P, KT, NC])
        mulT = sb("mulT", [P, KT, NC])
        hst = [sb(f"hst{i}", [P, CH]) for i in range(SR)]
        hs_m = sb("hs_m", [P, KT, NS])
        hs_t = sb("hs_t", [P, KT, NS])
        ps_t = [ps(f"ps_t{i}", [P, CH]) for i in range(4)]
        ps_small = ps("ps_small", [P, 512])
        ps_mod = ps("ps_mod", [P, 512])
        ps_gate = [ps(f"ps_gate{i}", [P, 512]) for i in range(2)]
        mod = ps_mod[:, 0:2 * KT * NC].rearrange("p (f c) -> p f c", c=NC)
        cT = ps_small[:, 64:64 + KT * NC].rearrange("p (k c) -> p k c", c=NC)
        xsT = ps_small[:, 256:256 + KT * NS].rearrange("p (k c) -> p k c", c=NS)

        rows_in, c_landed, bg_landed, xs_landed = (sem(n) for n in ("rows_in", "c_landed", "bg_landed", "xs_landed"))
        w_landed = [sem(f"wa_landed{i}") for i in range(WR)]
        x_landed = [sem(f"x_landed{i}") for i in range(XR)]
        w_used, ident_zero, ident_ready, mhalf_ready = (sem(n) for n in ("wa_used", "ident_zero", "ident_ready", "mhalf_ready"))
        rows_T, vec_ready, c_sigm, c_silu, c_T, sc_ready = (sem(n) for n in ("rows_T", "vec_ready", "c_sigm", "c_silu", "c_T", "sc_ready"))
        mod_step, mod_ready, gate_done, gate_ready = (sem(n) for n in ("mod_step", "mod_ready", "gate_done", "gate_ready"))
        squared, meaned, powered, x_normed = (sem(n) for n in ("squared", "meaned", "powered", "x_normed"))
        hT_done, h_mod, h_hi, h_lo = (sem(n) for n in ("hT_done", "h_mod", "h_hi", "h_lo"))
        samp_T, samp_step, samp_hi, gate_stored = (sem(n) for n in ("samp_T", "samp_step", "samp_hi", "gate_stored"))

        with nc.Block() as block:
            @block.sync
            def _(sp):
                sp.dma_start(rows[0:24, :], v["b_ada"][0].rearrange("(a b) -> a b", b=P)).then_inc(rows_in, 16)
                sp.dma_start(rows[24:32, :], v["norm_g"][0].rearrange("(a b) -> a b", b=P)).then_inc(rows_in, 16)
                sp.dma_start(rows[32:36, :], v["b_pool"][0]).then_inc(rows_in, 16)
                sp.dma_start(rows[36:40, :], v["pool_scale"][0].rearrange("(a b) -> a b", b=P)).then_inc(rows_in, 16)
                sp.dma_start(c_in[0:1, :], v["c_prompt"]).then_inc(c_landed, 16)
                sp.dma_start(c_in[1:NC, :], v["c_sample"]).then_inc(c_landed, 16)
                sp.dma_start(b_gate[:, :], v["b_ada"][0:1, 2 * D:3 * D].to_broadcast([NC, D])).then_inc(bg_landed, 16)
                sp.dma_start(xst[:, :], xs).then_inc(xs_landed, 16)

                def load_w(n):
                    if n >= WR:
                        sp.wait_ge(w_used, n - WR + 1)
                    sp.dma_start(w_st[n % WR][:, :, :], w_ada_v[:, :, n * 512:(n + 1) * 512]).then_inc(w_landed[n % WR], 16)

                def load_x(t):
                    if t >= XR:
                        sp.wait_ge(hT_done, ((t - XR) // 4 + 1) * KT)
                    sp.dma_start(xt[t % XR][:, :], xp[t * P:(t + 1) * P, :]).then_inc(x_landed[t % XR], 16)

                load_w(0)
                load_w(1)
                for t in range(XR):
                    load_x(t)
                load_w(2)
                load_w(3)
                for t in range(XR, NX):
                    load_x(t)
                load_w(4)
                load_w(5)
                sp.wait_ge(gate_ready, 2)
                sp.dma_start(gate_dram, gate_sb[:, :]).then_inc(gate_stored, 16)
                sp.wait_ge(gate_stored, 16)

            @block.gpsimd
            def _(pool):
                nc.gpsimd.memset(ident[:, :], 0.0).then_inc(ident_zero, 1)
                nc.gpsimd.memset(mhalf[:, :], -0.5).then_inc(mhalf_ready, 1)
                pool.wait_ge(ident_zero, 1)
                nc.gpsimd.affine_select(out=ident[:, :], in_=ident[:, :], compare_op=ALU.not_equal, fill=1.0,
                                        base=0, pattern=[[-1, P]], channel_multiplier=1).then_inc(ident_ready, 1)
                pool.wait_ge(mhalf_ready, 1)

                def power(t, rows_n):
                    pool.wait_ge(meaned, t + 1)
                    nc.gpsimd.tensor_tensor(rs[0:rows_n, t:t + 1], ms[0:rows_n, t:t + 1], mhalf[0:rows_n, :],
                                            ALU.pow).then_inc(powered, 1)

                for t in range(4):
                    power(t, P)
                for tc in range(NCH):
                    if tc < NCH - 1:
                        for t in range(4 * tc + 4, 4 * tc + 8):
                            power(t, P)
                    for k in range(KT):
                        n = tc * KT + k
                        pool.wait_ge(h_mod, n + 1)
                        nc.gpsimd.tensor_copy(hH[:, k, tc * CH:(tc + 1) * CH], hst[n % SR][:, :]).then_inc(h_hi, 1)
                power(NX, NS)
                pool.wait_ge(samp_step, 2)
                nc.gpsimd.tensor_copy(hH[:, :, SEQ:TT], hs_t[:, :, :]).then_inc(samp_hi, 1)

            @block.scalar
            def _(act):
                act.wait_ge(c_landed, 32)
                nc.scalar.activation(c_sig[:, :], c_in[:, :], ACT.Sigmoid).then_inc(c_sigm, 1)

                def square(t):
                    act.wait_ge(x_landed[t % XR], 16 * (t // XR) + 16)
                    if t:
                        act.wait_ge(squared, t)
                    nc.scalar.activation(junk[:, :], xt[t % XR][:, :], ACT.Square, accum_out=ss[:, t:t + 1]).then_inc(squared, 1)

                for t in range(4):
                    square(t)
                for tc in range(NCH):
                    if tc < NCH - 1:
                        for t in range(4 * tc + 4, 4 * tc + 8):
                            square(t)
                    for k in range(KT):
                        n = tc * KT + k
                        act.wait_ge(mod_ready, 2)
                        act.wait_ge(hT_done, n + 1)
                        if n >= SR:
                            act.wait_ge(h_lo, n - SR + 1)
                        nc.scalar.activation(hst[n % SR][:, :], ps_t[n % 4][:, :], ACT.Identity,
                                             bias=addT[:, k, 0:1], scale=mulT[:, k, 0:1]).then_inc(h_mod, 1)
                act.wait_ge(xs_landed, 16)
                act.wait_ge(squared, NX)
                nc.scalar.activation(junk[0:NS, :], xst[:, :], ACT.Square, accum_out=ss[0:NS, NX:NX + 1]).then_inc(squared, 1)

            @block.vector
            def _(dve):
                dve.wait_ge(rows_T, 1)
                nc.vector.tensor_copy(vecT[:, :], ps_small[:, 0:40]).then_inc(vec_ready, 1)
                dve.wait_ge(c_sigm, 1)
                nc.vector.tensor_tensor(c_sig[:, :], c_sig[:, :], c_in[:, :], ALU.mult).then_inc(c_silu, 1)
                dve.wait_ge(c_T, 1)
                nc.vector.tensor_copy(scT[:, :, :], cT).then_inc(sc_ready, 1)

                def normalise(t, tile, rows_n):
                    dve.wait_ge(squared, t + 1)
                    nc.vector.tensor_scalar(ms[0:rows_n, t:t + 1], ss[0:rows_n, t:t + 1], 1.0 / D, EPS,
                                            ALU.mult, ALU.add).then_inc(meaned, 1)
                    dve.wait_ge(powered, t + 1)
                    nc.vector.tensor_scalar(tile, tile, rs[0:rows_n, t:t + 1], None, ALU.mult).then_inc(x_normed, 1)

                for t in range(4):
                    normalise(t, xt[t % XR][:, :], P)
                dve.wait_ge(w_used, 4)
                dve.wait_ge(vec_ready, 1)
                nc.vector.tensor_tensor(addT[:, :, :], mod[:, 0:KT, :], vecT[:, 0:KT].unsqueeze(2).to_broadcast([P, KT, NC]),
                                        ALU.add).then_inc(mod_ready, 1)
                nc.vector.tensor_tensor(scl1[:, :, :], mod[:, KT:2 * KT, :],
                                        vecT[:, KT:2 * KT].unsqueeze(2).to_broadcast([P, KT, NC]), ALU.add).then_inc(mod_step, 1)
                dve.wait_ge(mod_step, 1)
                nc.vector.tensor_scalar(scl1[:, :, :], scl1[:, :, :], 1.0, None, ALU.add).then_inc(mod_step, 1)
                dve.wait_ge(mod_step, 2)
                nc.vector.tensor_tensor(mulT[:, :, :], scl1[:, :, :], vecT[:, 24:32].unsqueeze(2).to_broadcast([P, KT, NC]),
                                        ALU.mult).then_inc(mod_ready, 1)
                for tc in range(NCH):
                    if tc < NCH - 1:
                        for t in range(4 * tc + 4, 4 * tc + 8):
                            normalise(t, xt[t % XR][:, :], P)
                    for k in range(KT):
                        n = tc * KT + k
                        cols = slice(tc * CH, (tc + 1) * CH)
                        dve.wait_ge(h_hi, n + 1)
                        nc.vector.tensor_tensor(hL[:, k, cols], hst[n % SR][:, :], hH[:, k, cols].bitcast(F32),
                                                ALU.subtract).then_inc(h_lo, 1)
                normalise(NX, xst[:, :], NS)
                dve.wait_ge(samp_T, 1)
                nc.vector.tensor_tensor(hs_m[:, :, :], xsT, mulT[:, :, 1:NC], ALU.mult).then_inc(samp_step, 1)
                dve.wait_ge(samp_step, 1)
                nc.vector.tensor_tensor(hs_t[:, :, :], hs_m[:, :, :], addT[:, :, 1:NC], ALU.add).then_inc(samp_step, 1)
                dve.wait_ge(samp_hi, 1)
                nc.vector.tensor_tensor(hL[:, :, SEQ:TT], hs_t[:, :, :], hH[:, :, SEQ:TT].bitcast(F32), ALU.subtract)
                dve.wait_ge(bg_landed, 16)
                for j in range(2):
                    dve.wait_ge(gate_done, j + 1)
                    cols = slice(j * 512, (j + 1) * 512)
                    nc.vector.tensor_tensor(gate_sb[:, cols], ps_gate[j][0:NC, :], b_gate[:, cols], ALU.add).then_inc(gate_ready, 1)

            @block.tensor
            def _(pe):
                pe.wait_ge(ident_ready, 1)
                pe.wait_ge(rows_in, 64)
                nc.tensor.transpose(ps_small[:, 0:40], rows[:, :], ident[0:40, 0:40]).then_inc(rows_T, 1)
                pe.wait_ge(c_silu, 1)
                for k in range(KT):
                    last = nc.tensor.transpose(cT[:, k, :], c_sig[:, k * P:(k + 1) * P], ident[0:NC, 0:NC])
                last.then_inc(c_T, 1)
                pe.wait_ge(sc_ready, 1)
                for n in range(4):
                    pe.wait_ge(w_landed[n % WR], 16 * (n // WR) + 16)
                    for f in range(4):
                        for k in range(KT):
                            last = nc.tensor.matmul(mod[:, 4 * n + f, :], w_st[n % WR][:, k, f * P:(f + 1) * P], scT[:, k, :],
                                                    start=(k == 0), stop=(k == KT - 1))
                    last.then_inc(w_used, 1)
                for tc in range(NCH):
                    pe.wait_ge(x_normed, 4 * tc + 4)
                    for k in range(KT):
                        n = tc * KT + k
                        if n >= 4:
                            pe.wait_ge(h_mod, n - 3)
                        for i in range(4):
                            last = nc.tensor.transpose(ps_t[n % 4][:, i * P:(i + 1) * P],
                                                       xt[(4 * tc + i) % XR][:, k * P:(k + 1) * P], ident[:, :])
                        last.then_inc(hT_done, 1)
                pe.wait_ge(x_normed, NX + 1)
                for k in range(KT):
                    last = nc.tensor.transpose(xsT[:, k, :], xst[:, k * P:(k + 1) * P], ident[0:NS, 0:NS])
                last.then_inc(samp_T, 1)
                for j in range(2):
                    n = 4 + j
                    pe.wait_ge(w_landed[n % WR], 16 * (n // WR) + 16)
                    for k in range(KT):
                        last = nc.tensor.matmul(ps_gate[j][0:NC, :], scT[:, k, :], w_st[n % WR][:, k, :],
                                                start=(k == 0), stop=(k == KT - 1))
                    last.then_inc(gate_done, 1)


def branches(nc, scope, v):
    hH, hL, ident, vecT, aTs = (v[n] for n in ("hH", "hL", "ident", "vecT", "aTs"))
    w_in_v, bT_dram, gT_dram, bulk, late = (v[n] for n in ("w_in_v", "bT_dram", "gT_dram", "bulk", "late"))
    samp_dram, snew_dram, pnew_dram, states = (v[n] for n in ("samp_dram", "snew_dram", "pnew_dram", "states"))
    pool_p, pool_s, state_pool = v["pool_p"][0, 0], v["pool_s"][0], v["state_pool"][0]
    PAIRS, NF = 4, 28
    SCORE0, SOFT0, VALUE0, END0 = 12, 20, 22, 26
    BH = NS * HEADS
    HE = HEADS * E
    stack = ExitStack()
    with stack:
        sb, ps, sem = scope(stack)
        wst = [sb(f"wst{i}", [P, KT, P]) for i in range(2)]
        wH = [sb(f"wH{i}", [P, KT, P], F32R) for i in range(2)]
        wL = [sb(f"wL{i}", [P, KT, P], F32R) for i in range(2)]
        gst = [sb(f"gst{i}", [P, BCH]) for i in range(2)]
        pst = [sb(f"pst{i}", [P, BCH]) for i in range(2)]
        ost = [sb(f"ost{i}", [P, BCH]) for i in range(NBC)]
        wpool = sb("wpool", [P, 4, P])
        recip = sb("recip", [P, PADU])
        sp_rows = sb("sp_rows", [NS * NPS, 4 * P])
        spT = sb("spT", [P, 4, NS * NPS])
        s_sum = sb("s_sum", [P, 2, NS])
        utail = sb("utail", [P, 4, NPS + NS])
        urow = sb("urow", [NPS, 4 * P])
        usrow = sb("usrow", [NS, 4 * P])

        pooling = ExitStack()
        with pooling:
            pool_sb, _, _ = scope(pooling)
            uT = pool_sb("uT", [P, PADU + TT])
            run = [pool_sb(f"run{i}", [P, PADU + SEQ]) for i in range(2)]
            mixed = pool_sb("mixed", [P, TT])
            zS = pool_sb("zS", [P, TT])
        kt = [sb(f"kt{g}", [P, HE]) for g in range(GROUPS)]
        qb = [sb(f"qb{g}", [P, HE]) for g in range(GROUPS)]
        vt = (kt, qb)
        prod = sb("prod", [P, HE])
        sc = sb("sc", [P, GROUPS, BH])
        q_new = sb("q_new", [NS, NO, E])
        kv_new = sb("kv_new", [NS, NO, E])
        snew = sb("snew", [NS, HEADS, GROUPS])
        scr = sb("scr", [BH, GROUPS * P])
        scn = sb("scn", [BH, GROUPS])
        st = sb("st", [BH, 8])
        pcr = sb("pcr", [BH, GROUPS * P])
        pcn = sb("pcn", [BH, GROUPS])
        pT = sb("pT", [P, GROUPS, BH])
        pn = sb("pn", [NS, NO])
        diag = sb("diag", [NS, NO, NS])
        zs = sb("zs", [P, 4, NS])

        pp = [ps(f"pp{i}", [P, 512]) for i in range(NBC)]
        ppool = [ps(f"ppool{i}", [P, 512]) for i in range(2)]
        psA = ps("d_psA", [P, 512])

        w_landed = [sem(f"wb_landed{i}") for i in range(2)]
        w_hi, w_lo, proj_done, evac = (sem(n) for n in ("w_hi", "w_lo", "proj_done", "evac"))
        out_stored = [sem(f"out_stored{i}") for i in range(NBC)]
        wpool_in, sp_in, spT_done, spT_ready, pad_ready = (sem(n) for n in ("wpool_in", "sp_in", "spT_done", "spT_ready", "pad_ready"))
        window, mix_ready, pool_done, biased, gated, tail_saved, tail_T, tail_ready = (
            sem(n) for n in ("window", "mix_ready", "pool_done", "biased", "gated", "tail_saved", "tail_T", "tail_ready"))
        b_stored = [sem(f"b_stored{i}") for i in range(2)]
        qk_in, vnew_in, scored, multiplied, snew_ready, snew_out, snew_in, scT_done = (
            sem(n) for n in ("qk_in", "vnew_in", "scored", "multiplied", "snew_ready", "snew_out", "snew_in", "scT_done"))
        max_ready, dexp, p_ready, pn_out, pn_in, pT_done, pT_ready, diag_ready, pv_used, zs_in = (
            sem(n) for n in ("max_ready", "dexp", "p_ready", "pn_out", "pn_in", "pT_done", "pT_ready", "diag_ready", "pv_used", "zs_in"))
        k_landed = [sem(f"k_landed{g}") for g in range(GROUPS)]
        q_landed = [sem(f"q_landed{g}") for g in range(GROUPS)]
        v_landed = [[sem(f"v_landed{i}_{g}") for g in range(GROUPS)] for i in range(2)]

        def cols_of(c):
            return slice(c * BCH, min((c + 1) * BCH, TT))

        def width(c):
            return cols_of(c).stop - cols_of(c).start

        def column(n):
            if n < 2 * PAIRS:
                return (CU, CZB)[n % 2] + n // 2 * P
            return CZA + (n - 2 * PAIRS) * P if n < 2 * PAIRS + 4 else gate_column(n)

        def gate_column(n):
            return n * P + (CGA - (2 * PAIRS + 4) * P)

        def carried(g, b, which):
            W, d = PATTERNS[g]
            rows = states[g][0, bass.ds(b, 1), :, which, :, :].rearrange("o w h e -> (o w) (h e)")
            return strided(rows, 0, P, d)

        with nc.Block() as block:
            @block.sync
            def _(sp):
                def load(n, slot, col):
                    sp.wait_ge(w_lo, after(n - 2))
                    apart(sp, v["passed"])
                    sp.dma_start(wst[slot][:, :, :], w_in_v[:, :, bass.ds(col, P)]).then_inc(w_landed[slot], 16)

                def store_b(p):
                    for c in range(NBC):
                        m = p * NBC + c
                        sp.wait_ge(gated, m + 1)
                        sp.dma_start(bT_dram[p, :, cols_of(c)], gst[m % 2][:, 0:width(c)]).then_inc(b_stored[m % 2], 16)

                def keys(b):
                    for g in range(GROUPS):
                        sp.wait_ge(scored, after(b * GROUPS + (g - GROUPS)))
                        apart(sp, v["passed"])
                        sp.dma_start(kt[g][:, :], carried(g, b, 0)).then_inc(k_landed[g], 16)
                        sp.dma_start(qb[g][:, :], samp_dram[bass.ds(b, 1), 0, g * HEADS:(g + 1) * HEADS, :].rearrange("o h e -> o (h e)")
                                     .to_broadcast([P, HE])).then_inc(q_landed[g], 16)

                def values(b, i):
                    for g in range(GROUPS):
                        sp.wait_ge(pv_used, after(b * GROUPS + (g - 2 * GROUPS)))
                        apart(sp, v["passed"])
                        sp.dma_start(vt[i][g][:, :], carried(g, b, 1)).then_inc(v_landed[i][g], 16)

                load(0, 0, column(0))
                sp.dma_start(sp_rows[:, :], state_pool.rearrange("b j c -> (b j) c")).then_inc(sp_in, 16)
                load(1, 1, column(1))
                sp.dma_start(wpool[:, :, :], v["w_pool"][0].rearrange("g c d -> c g d")).then_inc(wpool_in, 16)
                sp.dma_start(pool_s[:, 0:NPS - 1, :], state_pool[:, 1:NPS, :]).then_inc(late, 16)
                for p in range(PAIRS):
                    load(2 * p + 2, 0, column(2 * p + 2))
                    shifted_copy(sp, v, 1, 2 * p, bulk)
                    if p:
                        store_b(p - 1)
                    load(2 * p + 3, 1, column(2 * p + 3))
                    shifted_copy(sp, v, 1, 2 * p + 1, bulk)
                load(2 * PAIRS + 2, 0, column(2 * PAIRS + 2))
                store_b(PAIRS - 1)
                load(2 * PAIRS + 3, 1, column(2 * PAIRS + 3))
                rows = lambda ap: ap.rearrange("b n e -> b (n e)")
                sp.dma_start(rows(q_new[:, :, :]), rows(samp_dram[:, 0])).then_inc(qk_in, 16)
                sp.dma_start(rows(kv_new[:, :, :]), rows(samp_dram[:, 1])).then_inc(qk_in, 16)
                sp.wait_ge(snew_ready, 1)
                sp.dma_start(rows(kv_new[:, :, :]), rows(samp_dram[:, 2])).then_inc(vnew_in, 16)
                sp.dma_start(snew_dram.rearrange("b h g -> b (h g)"), snew[:, :, :].rearrange("b h g -> b (h g)")).then_inc(snew_out, 16)
                sp.wait_ge(snew_out, 16)
                sp.dma_start(scn[:, :], snew_dram.rearrange("b h g -> (b h) g")).then_inc(snew_in, 16)
                sp.wait_ge(tail_ready, 2)
                sp.dma_start(pool_p, urow[:, :]).then_inc(late, 16)
                sp.dma_start(pool_s[:, NPS - 1, :], usrow[:, :]).then_inc(late, 16)
                with sp.Fori(0, NS // 2) as i:
                    n = i * 2 + SCORE0
                    for j in range(2):
                        load(n + j, j, gate_column(n + j))
                        keys(i * 2 + j)
                        shifted_copy(sp, v, 0, i * 2 + j, bulk)
                load(SOFT0, 0, gate_column(SOFT0))
                load(SOFT0 + 1, 1, gate_column(SOFT0 + 1))
                sp.wait_ge(out_stored[NBC - 1], LEAD_DMA + 16 * 4)
                sp.dma_start(zs[:, :, :], gT_dram[0:4, :, SEQ:TT].rearrange("f p t -> p f t")).then_inc(zs_in, 16)
                sp.wait_ge(p_ready, 2)
                sp.dma_start(pnew_dram.rearrange("b h g -> (b h) g"), pcn[:, :]).then_inc(pn_out, 16)
                sp.wait_ge(pn_out, 16)
                sp.dma_start(pn[:, :], pnew_dram.rearrange("b h g -> b (h g)")).then_inc(pn_in, 16)
                with sp.Fori(0, 2) as i:
                    n = i * 2 + VALUE0
                    for j in range(2):
                        load(n + j, j, gate_column(n + j))
                    for j in range(4):
                        values(i * 4 + j, j % 2)
                load(END0, 0, gate_column(END0))
                load(END0 + 1, 1, gate_column(END0 + 1))
                sp.wait_ge(late, 48)
                for i in range(2):
                    sp.wait_ge(b_stored[i], 16 * PAIRS * NBC // 2)

            @block.gpsimd
            def _(pool):
                nc.gpsimd.memset(uT[:, 0:PADU], 0.0).then_inc(pad_ready, 1)
                for t in range(PADU):
                    nc.gpsimd.memset(recip[:, t:t + 1], 1.0 / (t + 1)).then_inc(pad_ready, 1)

                def split_hi(n, slot, landed):
                    pool.wait_ge(w_landed[slot], landed)
                    pool.wait_ge(proj_done, after((n - 1) * NBC - 1))
                    apart(pool, v["passed"])
                    nc.gpsimd.tensor_copy(wH[slot][:, :, :], wst[slot][:, :, :]).then_inc(w_hi, 1)

                with pool.Fori(0, NF // 2) as i:
                    split_hi(i * 2, 0, i * 16 + 16)
                    split_hi(i * 2 + 1, 1, i * 16 + 16)

            @block.vector
            def _(dve):
                dve.sem_inc(w_lo, LEAD)
                dve.sem_inc(scored, LEAD)

                def split_lo(n, slot):
                    dve.wait_ge(w_hi, n + 1)
                    dve.wait_ge(proj_done, after((n - 1) * NBC - 1))
                    nc.vector.tensor_tensor(wL[slot][:, :, :], wst[slot][:, :, :], wH[slot][:, :, :].bitcast(F32),
                                            ALU.subtract).then_inc(w_lo, 1)

                steps = [0]

                def chained(ins):
                    steps[0] += 1
                    ins.then_inc(window, 1)
                    dve.wait_ge(window, steps[0])

                def windows(p):
                    w = POOLS[p]
                    dve.wait_ge(evac, after(2 * p * NBC + NBC - 1))
                    if p:
                        dve.wait_ge(pool_done, NBC * p)
                    src, first = uT, 0
                    for s in range(p + 1):
                        shift = 1 << s
                        first += shift
                        dst = run[s % 2]
                        chained(nc.vector.tensor_tensor(dst[:, first:], src[:, first:PADU + SEQ], src[:, first - shift:PADU + SEQ - shift], ALU.add))
                        src = dst
                    nc.vector.scalar_tensor_tensor(mixed[:, w:SEQ], src[:, PADU + w:], 1.0 / w, uT[:, PADU + w:PADU + SEQ], ALU.mult, ALU.subtract)
                    chained(nc.vector.tensor_tensor(src[:, PADU:PADU + w], src[:, PADU:PADU + w], recip[:, 0:w], ALU.mult))
                    nc.vector.tensor_tensor(mixed[:, 0:w], src[:, PADU:PADU + w], uT[:, PADU:PADU + w], ALU.subtract)
                    nc.vector.tensor_copy(utail[:, p, :], uT[:, PADU + SEQ - NPS:]).then_inc(tail_saved, 1)
                    u_s = uT[:, PADU + SEQ:]
                    rows = spT[:, p, :].rearrange("p (b j) -> p b j", j=NPS)[:, :, NPS - (w - 1):]
                    chained(nc.vector.tensor_reduce(s_sum[:, 0, :], rows, AX.X, ALU.add))
                    chained(nc.vector.tensor_tensor(s_sum[:, 1, :], s_sum[:, 0, :], u_s, ALU.add))
                    nc.vector.scalar_tensor_tensor(mixed[:, SEQ:TT], s_sum[:, 1, :], 1.0 / w, u_s, ALU.mult,
                                                   ALU.subtract).then_inc(mix_ready, 1)

                def gate(p):
                    for c in range(NBC):
                        m = NBC * p + c
                        dve.wait_ge(pool_done, m + 1)
                        t = pst[m % 2][:, 0:width(c)]
                        nc.vector.tensor_scalar(t, ppool[m % 2][:, 0:width(c)], vecT[:, 32 + p:33 + p], vecT[:, 36 + p:37 + p],
                                                ALU.add, ALU.mult).then_inc(biased, 1)
                        dve.wait_ge(biased, m + 1)
                        if m >= 2:
                            dve.wait_ge(b_stored[m % 2], 16 * (m // 2))
                        dve.wait_ge(evac, after((2 * p + 1) * NBC + c))
                        nc.vector.tensor_tensor(gst[m % 2][:, 0:width(c)], t, zS[:, cols_of(c)], ALU.mult).then_inc(gated, 1)

                def score(b):
                    for g in range(GROUPS):
                        dve.wait_ge(k_landed[g], b * 16 + 16)
                        dve.wait_ge(q_landed[g], b * 16 + 16)
                        dve.wait_ge(scored, after(b * GROUPS + (g - 1)))
                        nc.vector.tensor_tensor(prod[:, :], kt[g][:, :], qb[g][:, :], ALU.mult).then_inc(multiplied, 1)
                        dve.wait_ge(multiplied, b * GROUPS + (g + 1))
                        nc.vector.tensor_reduce(sc[:, g, bass.ds(b * HEADS, HEADS)], prod[:, :].rearrange("p (h e) -> p h e", e=E),
                                                AX.X, ALU.add).then_inc(scored, 1)

                split_lo(0, 0)
                split_lo(1, 1)
                dve.wait_ge(spT_done, 1)
                nc.vector.tensor_copy(spT[:, :, :].rearrange("p g r -> p (g r)"), ppool[1][:, 0:4 * NS * NPS]).then_inc(spT_ready, 1)
                dve.wait_ge(spT_ready, 1)
                dve.wait_ge(pad_ready, 1 + PADU)
                for p in range(PAIRS):
                    if p:
                        gate(p - 1)
                    split_lo(2 * p + 2, 0)
                    windows(p)
                    split_lo(2 * p + 3, 1)
                gate(PAIRS - 1)
                split_lo(2 * PAIRS + 2, 0)
                split_lo(2 * PAIRS + 3, 1)
                dve.wait_ge(tail_T, 1)
                nc.vector.tensor_copy(urow[:, :], ppool[0][0:NPS, :]).then_inc(tail_ready, 1)
                nc.vector.tensor_copy(usrow[:, :], ppool[1][0:NS, :]).then_inc(tail_ready, 1)
                dve.wait_ge(qk_in, 32)
                chained(nc.vector.tensor_tensor(q_new[:, :, :], q_new[:, :, :], kv_new[:, :, :], ALU.mult))
                nc.vector.tensor_reduce(snew[:, :, :].rearrange("b h g -> b g h"), q_new[:, :, :].rearrange("b (g h) e -> b g h e", h=HEADS),
                                        AX.X, ALU.add).then_inc(snew_ready, 1)
                with dve.Fori(0, NS // 2) as i:
                    for j in range(2):
                        split_lo(i * 2 + (SCORE0 + j), j)
                        score(i * 2 + j)
                split_lo(SOFT0, 0)
                split_lo(SOFT0 + 1, 1)
                dve.wait_ge(scT_done, 1)
                chained(nc.vector.tensor_copy(scr[:, :], ppool[0][0:BH, 0:GROUPS * P]))
                dve.wait_ge(snew_in, 16)
                nc.vector.tensor_reduce(st[:, 0:1], scr[:, :], AX.X, ALU.max)
                chained(nc.vector.tensor_reduce(st[:, 1:2], scn[:, :], AX.X, ALU.max))
                chained(nc.vector.tensor_tensor(st[:, 5:6], st[:, 0:1], st[:, 1:2], ALU.max))
                nc.vector.tensor_scalar(st[:, 2:3], st[:, 5:6], -1.0, None, ALU.mult).then_inc(max_ready, 1)
                dve.wait_ge(dexp, 2)
                chained(nc.vector.tensor_tensor(st[:, 6:7], st[:, 3:4], st[:, 4:5], ALU.add))
                chained(nc.vector.reciprocal(st[:, 7:8], st[:, 6:7]))
                nc.vector.tensor_scalar(pcr[:, :], pcr[:, :], st[:, 7:8], None, ALU.mult).then_inc(p_ready, 1)
                nc.vector.tensor_scalar(pcn[:, :], pcn[:, :], st[:, 7:8], None, ALU.mult).then_inc(p_ready, 1)
                dve.wait_ge(pn_in, 16)
                nc.vector.tensor_tensor(diag[:, :, :], pn[:, :].unsqueeze(2).to_broadcast([NS, NO, NS]),
                                        ident[0:NS, 0:NS].unsqueeze(1).to_broadcast([NS, NO, NS]), ALU.mult).then_inc(diag_ready, 1)
                dve.wait_ge(pT_done, 1)
                nc.vector.tensor_copy(pT[:, :, :].rearrange("p g n -> p (g n)"), ppool[1][:, 0:GROUPS * BH]).then_inc(pT_ready, 1)
                with dve.Fori(0, 2) as i:
                    for j in range(2):
                        split_lo(i * 2 + (VALUE0 + j), j)
                split_lo(END0, 0)
                split_lo(END0 + 1, 1)
                dve.wait_ge(pv_used, after(NS * GROUPS - 1))
                dve.wait_ge(zs_in, 16)
                nc.vector.tensor_tensor(aTs[:, :, :], psA[:, 0:BH].rearrange("p (h b) -> p h b", b=NS), zs[:, :, :], ALU.mult)

            @block.scalar
            def _(act):
                act.sem_inc(evac, LEAD)
                for c in range(NBC):
                    act.sem_inc(out_stored[c], LEAD_DMA)

                def chunk(n, c, out, func):
                    act.wait_ge(proj_done, after(n * NBC + c))
                    nc.scalar.activation(out, pp[c][:, 0:width(c)], func).then_inc(evac, 1)

                for p in range(PAIRS):
                    if p:
                        act.wait_ge(mix_ready, p)
                    for c in range(NBC):
                        chunk(2 * p, c, uT[:, PADU + c * BCH:PADU + c * BCH + width(c)], ACT.Copy)
                    if p:
                        act.wait_ge(gated, NBC * p)
                    for c in range(NBC):
                        chunk(2 * p + 1, c, zS[:, cols_of(c)], ACT.Silu)

                def spilled(n, func):
                    for c in range(NBC):
                        act.wait_ge(out_stored[c], n * 16 + (LEAD_DMA - 16 * 2 * PAIRS))
                        chunk(n, c, ost[c][:, 0:width(c)], func)
                        act.wait_ge(evac, after(n * NBC + c))
                        act.dma_start(gT_dram[bass.ds(n - 2 * PAIRS, 1), :, cols_of(c)].rearrange("a p t -> p (a t)"),
                                      ost[c][:, 0:width(c)]).then_inc(out_stored[c], 16)

                with act.Fori(0, 4) as i:
                    spilled(i + 2 * PAIRS, ACT.Silu)
                with act.Fori(0, 8) as i:
                    spilled(i + SCORE0, ACT.Sigmoid)
                act.wait_ge(max_ready, 1)
                nc.scalar.activation(pcr[:, :], scr[:, :], ACT.Exp, bias=st[:, 2:3], accum_out=st[:, 3:4]).then_inc(dexp, 1)
                nc.scalar.activation(pcn[:, :], scn[:, :], ACT.Exp, bias=st[:, 2:3], accum_out=st[:, 4:5]).then_inc(dexp, 1)
                with act.Fori(0, 8) as i:
                    spilled(i + SOFT0, ACT.Sigmoid)
                for c in range(NBC):
                    act.wait_ge(out_stored[c], LEAD_DMA + 16 * (NF - 2 * PAIRS))

            @block.tensor
            def _(pe):
                pe.sem_inc(proj_done, LEAD)
                pe.sem_inc(pv_used, LEAD)

                def project(n, slot):
                    pe.wait_ge(w_lo, after(n))
                    for c in range(NBC):
                        pe.wait_ge(evac, after(n * NBC + (c - NBC)))
                        three_pass(nc, pp[c][:, 0:width(c)], [(wH[slot][:, k, :], wL[slot][:, k, :], hH[:, k, cols_of(c)], hL[:, k, cols_of(c)])
                                                              for k in range(KT)]).then_inc(proj_done, 1)

                def pooled(p):
                    pe.wait_ge(mix_ready, p + 1)
                    for c in range(NBC):
                        m = NBC * p + c
                        if m >= 2:
                            pe.wait_ge(biased, m - 1)
                        nc.tensor.matmul(ppool[m % 2][:, 0:width(c)], wpool[:, p, :], mixed[:, cols_of(c)],
                                         start=True, stop=True).then_inc(pool_done, 1)

                def values(b, i):
                    for g in range(GROUPS):
                        pe.wait_ge(v_landed[i][g], (b - i) * 8 + 16)
                        for h in range(HEADS):
                            last = nc.tensor.matmul(psA[:, bass.ds(b + h * NS, 1)], vt[i][g][:, h * E:(h + 1) * E],
                                                    pT[:, g, bass.ds(b * HEADS + h, 1)], start=False, stop=True, skip_group_check=True)
                        last.then_inc(pv_used, 1)

                pe.wait_ge(sp_in, 16)
                for g in range(4):
                    last = nc.tensor.transpose(ppool[1][:, g * NS * NPS:(g + 1) * NS * NPS], sp_rows[:, g * P:(g + 1) * P],
                                               ident[0:NS * NPS, 0:NS * NPS])
                last.then_inc(spT_done, 1)
                for p in range(PAIRS):
                    project(2 * p, 0)
                    if p:
                        pooled(p - 1)
                    else:
                        pe.wait_ge(wpool_in, 16)
                        pe.wait_ge(spT_ready, 1)
                    project(2 * p + 1, 1)
                project(2 * PAIRS, 0)
                pooled(PAIRS - 1)
                project(2 * PAIRS + 1, 1)
                pe.wait_ge(tail_saved, PAIRS)
                pe.wait_ge(biased, NBC * PAIRS)
                for g in range(4):
                    nc.tensor.transpose(ppool[0][0:NPS, g * P:(g + 1) * P], utail[:, g, 0:NPS], ident[:, :])
                    last = nc.tensor.transpose(ppool[1][0:NS, g * P:(g + 1) * P], utail[:, g, NPS:], ident[:, :])
                last.then_inc(tail_T, 1)
                project(2 * PAIRS + 2, 0)
                project(2 * PAIRS + 3, 1)
                with pe.Fori(0, NS // 2) as i:
                    project(i * 2 + SCORE0, 0)
                    project(i * 2 + (SCORE0 + 1), 1)
                pe.wait_ge(scored, after(NS * GROUPS - 1))
                pe.wait_ge(tail_ready, 2)
                for g in range(GROUPS):
                    last = nc.tensor.transpose(ppool[0][0:BH, g * P:(g + 1) * P], sc[:, g, :], ident[:, :])
                last.then_inc(scT_done, 1)
                project(SOFT0, 0)
                pe.wait_ge(p_ready, 1)
                for g in range(GROUPS):
                    last = nc.tensor.transpose(ppool[1][:, g * BH:(g + 1) * BH], pcr[:, g * P:(g + 1) * P], ident[0:BH, 0:BH])
                last.then_inc(pT_done, 1)
                pe.wait_ge(diag_ready, 1)
                pe.wait_ge(vnew_in, 16)
                for h in range(HEADS):
                    for g in range(GROUPS):
                        nc.tensor.matmul(psA[:, h * NS:(h + 1) * NS], kv_new[:, g * HEADS + h, :], diag[:, h * GROUPS + g, :],
                                         start=(h == 0 and g == 0), stop=False, skip_group_check=True)
                project(SOFT0 + 1, 1)
                pe.wait_ge(pT_ready, 1)
                with pe.Fori(0, 2) as i:
                    for j in range(2):
                        project(i * 2 + (VALUE0 + j), j)
                        values(i * 4 + 2 * j, 0)
                        values(i * 4 + (2 * j + 1), 1)
                project(END0, 0)
                project(END0 + 1, 1)


def apart(eng, passed):
    eng.sem_inc(passed[eng.engine], 1)


def three_pass(nc, out, terms, before=None):
    last = None
    for i, (sH, sL, mH, mL) in enumerate(terms):
        if before:
            before(i)
        nc.tensor.matmul(out, sH, mH, start=(i == 0), stop=False)
        nc.tensor.matmul(out, sH, mL, start=False, stop=False)
        last = nc.tensor.matmul(out, sL, mH, start=False, stop=(i == len(terms) - 1))
    return last


def shifted_copy(eng, v, g, b, done, piece=0, pieces=1):
    W = PATTERNS[g][0]
    n = (W - 1) * 2 * HEADS * E // pieces
    rows = (16 * (1 if g == 0 else 8 if g == 1 else 32)) // pieces
    first = piece * n
    def flat(a):
        return a[0].rearrange("b w k h e -> b (w k h e)")
    dst = flat(v["kv_s"][g])[bass.ds(b, 1), first:first + n].rearrange("o (r c) -> (o r) c", r=rows)
    src = flat(v["states"][g])[bass.ds(b, 1), first + 2 * HEADS * E:first + 2 * HEADS * E + n].rearrange("o (r c) -> (o r) c", r=rows)
    eng.dma_start(dst, src).then_inc(done, 16)


def attend(nc, scope, v):
    hH, hL, ident = v["hH"], v["hL"], v["ident"]
    w_in_v, o_dram, samp_dram, bulk = v["w_in_v"], v["o_dram"], v["samp_dram"], v["bulk"]
    SAMP = BLOCKS
    PAIR = 2
    UNITS = PAIR * GROUPS
    STEPS = UNITS * (BLOCKS + 1)
    NB = UNITS * BLOCKS
    ROUNDS = HEADS // PAIR
    plan = [(u, b, u * BLOCKS + b if b < BLOCKS else u) for u in range(UNITS) for b in range(BLOCKS + 1)]
    PIECES = 8
    PACE = STEPS // (NS // ROUNDS * PIECES)
    RKV, RQ, RT, RS, RO = 8, 2, 4, 2, 6

    def stored_rows(g, b):
        t0, d, _ = block_tokens(g, b)
        first = SEQ - PATTERNS[g][0]
        return (t0 - first, d) if t0 >= first else None

    kv_before = []
    kv_slot_total = [0] * RKV
    for u in range(UNITS):
        for b in range(BLOCKS):
            slot = (u * BLOCKS + b) % RKV
            kv_before.append(kv_slot_total[slot])
            if stored_rows(u % GROUPS, b):
                kv_slot_total[slot] += 1

    stack = ExitStack()
    with stack:
        sb, ps, sem = scope(stack)
        wst = sb("a_wst", [P, KT, 3, P])
        wH = [sb(f"a_wH{i}", [P, KT, 3 * P], F32R) for i in range(2)]
        wL = [sb(f"a_wL{i}", [P, KT, 3 * P], F32R) for i in range(2)]
        mask = sb("mask", [P, 2 * P])
        gains = sb("gains", [P, 2, GROUPS, P])
        kv = sb("kv", [P, RKV, 2, P])
        qn = sb("qn", [P, RQ, P])
        qkT = sb("qkT", [P, RT, 2, P])
        sm = sb("sm", [P, RS, 2 * P])
        pr = sb("pr", [P, RS, 2 * P])
        prT = sb("prT", [P, RS, 2 * P])
        ot = sb("ot", [P, RO, OW])
        nm = sb("nm", [P, RS])
        junk = sb("a_junk", [P, P])
        ss = sb("a_ss", [P, 2, 2])
        ms = sb("a_ms", [P, 2, 2])
        rs = sb("a_rs", [P, 2, 2])
        mhalf = sb("a_mhalf", [P, 2])
        sq = sb("sq", [NS, 2, 3, P])
        pp = [ps(f"a_pp{i}", [P, 512]) for i in range(2)]
        pqk = ps("pqk", [P, 512])
        psc = [ps(f"psc{i}", [P, 512]) for i in range(2)]
        ppt = ps("ppt", [P, 512])
        po = [ps(f"po{i}", [P, 512]) for i in range(2)]

        w_landed, gain_in, mask_step, mhalf_ready, gain_ready = (sem(n) for n in ("aw_landed", "gain_in", "mask_step", "mhalf_ready2", "gain_ready"))
        w_hi, w_lo = sem("aw_hi"), sem("aw_lo")
        proj_done, squared, act_read, meaned, powered, qk_normed = (
            sem(n) for n in ("a_proj_done", "a_squared", "act_read", "a_meaned", "a_powered", "qk_normed"))
        t_done, t_evac, s_done, s_masked, max_neg, exp_done, pt_done, pt_evac, pv_done, o_evac = (
            sem(n) for n in ("t_done", "t_evac", "s_done", "s_masked", "max_neg", "exp_done", "pt_done", "pt_evac", "pv_done", "o_evac"))
        kv_stored = [sem(f"kv_stored{i}") for i in range(RKV)]
        o_stored = [sem(f"o_stored{i}") for i in range(RO)]
        samp_stored = [sem(f"samp_stored{i}") for i in range(2)]

        def rounds(eng, body):
            with eng.Fori(0, ROUNDS) as r:
                body(r)

        def head_of(r, u):
            return r * PAIR + u // GROUPS

        def tokens(g, b):
            if b == SAMP:
                return slice(SEQ, TT)
            t0, d, _ = block_tokens(g, b)
            return slice(t0, t0 + (P - 1) * d + 1, d)

        with nc.Block() as block:
            @block.sync
            def _(sp):
                def load(r, u):
                    h, g = head_of(r, u), u % GROUPS
                    sp.wait_ge(w_lo, after((r * UNITS + u) * KT - 1))
                    apart(sp, v["passed"])
                    for i, c0 in enumerate((CQ, CK, CV)):
                        sp.dma_start(wst[:, :, i, :], w_in_v[:, :, bass.ds(h * E + (c0 + g * HEADS * E), E)]).then_inc(w_landed, 16)

                sp.dma_start(gains[:, 0, :, :].rearrange("p g e -> p (g e)"), v["q_gain"].rearrange("o g e -> o (g e)").to_broadcast([P, GROUPS * E])).then_inc(gain_in, 16)
                sp.dma_start(gains[:, 1, :, :].rearrange("p g e -> p (g e)"), v["k_gain"].rearrange("o g e -> o (g e)").to_broadcast([P, GROUPS * E])).then_inc(gain_in, 16)
                load(0, 0)

                def body(r):
                    for s in range(STEPS):
                        u, b, _ = plan[s]
                        if b == 1:
                            load(r, u + 1)
                        piece, at = divmod(s, PACE)
                        if at == 0 and piece < NS // ROUNDS * PIECES:
                            sp.wait_ge(proj_done, after(r * STEPS + s))
                            apart(sp, v["passed"])
                            shifted_copy(sp, v, 2, r * (NS // ROUNDS) + piece // PIECES, bulk, piece % PIECES, PIECES)
                rounds(sp, body)

            @block.gpsimd
            def _(pool):
                pool.sem_inc(w_hi, LEAD)
                pool.sem_inc(powered, LEAD)
                nc.gpsimd.memset(mask[:, :], 0.0).then_inc(mask_step, 1)
                nc.gpsimd.memset(mhalf[:, :], -0.5).then_inc(mhalf_ready, 1)
                pool.wait_ge(mask_step, 1)
                nc.gpsimd.affine_select(out=mask[:, 0:P], in_=mask[:, 0:P], compare_op=ALU.is_ge, fill=-MASKED,
                                        base=0, pattern=[[1, P]], channel_multiplier=-1).then_inc(mask_step, 1)
                nc.gpsimd.affine_select(out=mask[:, P:2 * P], in_=mask[:, P:2 * P], compare_op=ALU.is_ge, fill=-MASKED,
                                        base=0, pattern=[[-1, P]], channel_multiplier=1).then_inc(mask_step, 1)
                pool.wait_ge(mhalf_ready, 1)

                def split_hi(u, slot, k):
                    if k == 0:
                        pool.wait_ge(w_landed, u * 48 + 48)
                    pool.wait_ge(w_lo, after(u * KT + k - 1))
                    apart(pool, v["passed"])
                    nc.gpsimd.tensor_copy(wH[slot][:, k, :], wst[:, k, :, :].rearrange("p i c -> p (i c)")).then_inc(w_hi, 1)

                def power(r, s):
                    n = r * STEPS + s
                    rows = P if plan[s][1] < BLOCKS else NS
                    pool.wait_ge(meaned, after(n))
                    nc.gpsimd.tensor_tensor(rs[0:rows, s % 2, :], ms[0:rows, s % 2, :], mhalf[0:rows, :], ALU.pow).then_inc(powered, 1)

                for k in range(KT):
                    split_hi(0, 0, k)

                def body(r):
                    for s in range(STEPS):
                        power(r, s)
                        u, b, _ = plan[s]
                        if 4 <= b < 4 + KT:
                            split_hi(r * UNITS + (u + 1), (u + 1) % 2, b - 4)
                rounds(pool, body)

            @block.scalar
            def _(act):
                for x in (squared, act_read, t_evac, exp_done, o_evac):
                    act.sem_inc(x, LEAD)
                for x in (*kv_stored, *o_stored, *samp_stored):
                    act.sem_inc(x, LEAD_DMA)

                def project_read(r, s):
                    u, b, j = plan[s]
                    g = u % GROUPS
                    n = r * STEPS + s
                    rows = P if b < BLOCKS else NS
                    src = pp[s % 2]
                    act.wait_ge(proj_done, after(n))
                    act.wait_ge(meaned, after(n - 2))
                    for i in range(2):
                        act.wait_ge(squared, after(2 * n + i - 1))
                        nc.scalar.activation(junk[0:rows, :], src[0:rows, i * P:(i + 1) * P], ACT.Square,
                                             accum_out=ss[0:rows, s % 2, i:i + 1]).then_inc(squared, 1)
                    if b < BLOCKS:
                        jj = r * NB + j
                        act.wait_ge(pv_done, after(jj - RKV + 1))
                        act.wait_ge(kv_stored[j % RKV], r * (16 * kv_slot_total[j % RKV]) + (LEAD_DMA + 16 * kv_before[j]))
                        nc.scalar.activation(kv[:, j % RKV, 1, :], src[:, 2 * P:3 * P], ACT.Copy).then_inc(act_read, 1)
                    else:
                        act.wait_ge(samp_stored[j % 2], r * (32 * UNITS // 2) + (LEAD_DMA + 32 * (j // 2)))
                        nc.scalar.activation(sq[:, j % 2, 2, :], src[0:NS, 2 * P:3 * P], ACT.Copy).then_inc(act_read, 1)

                def store_kv(r, s):
                    u, b, j = plan[s]
                    g, h = u % GROUPS, head_of(r, u)
                    n = r * STEPS + s
                    if b < BLOCKS:
                        at = stored_rows(g, b)
                        if at is None:
                            return
                        act.wait_ge(qk_normed, after(n))
                        act.wait_ge(act_read, after(n))
                        act.dma_start(strided(v["kv_p"][g][0, 0], at[0], P, at[1])[:, :, bass.ds(h, 1), :].rearrange("t k o e -> t k (o e)"),
                                      kv[:, j % RKV, :, :]).then_inc(kv_stored[j % RKV], 16)
                    else:
                        act.wait_ge(qk_normed, after(n))
                        act.wait_ge(act_read, after(n))
                        act.dma_start(samp_dram[:, :, bass.ds(h + g * HEADS, 1), :].rearrange("b i o e -> b i (o e)"),
                                      sq[:, j % 2, :, :]).then_inc(samp_stored[j % 2], 16)
                        act.dma_start(v["kv_s"][g][0, :, PATTERNS[g][0] - 1, :, bass.ds(h, 1), :].rearrange("b k o e -> b k (o e)"),
                                      sq[:, j % 2, 1:3, :]).then_inc(samp_stored[j % 2], 16)

                def evac_T(r, s):
                    u, b, j = plan[s]
                    g = u % GROUPS
                    if b == SAMP:
                        return
                    jj = r * NB + j
                    act.wait_ge(t_done, after(jj))
                    act.wait_ge(s_done, after(jj - RT + 1))
                    nc.scalar.activation(qkT[:, j % RT, :, :].rearrange("p i t -> p (i t)"), pqk[:, 0:2 * P], ACT.Copy).then_inc(t_evac, 1)

                def exponent(r, s):
                    u, b, j = plan[s]
                    g = u % GROUPS
                    if b == SAMP:
                        return
                    jj = r * NB + j
                    lo = 0 if block_tokens(g, b)[2] else P
                    act.wait_ge(max_neg, after(jj))
                    act.wait_ge(pt_done, after(jj - RS))
                    nc.scalar.activation(pr[:, j % RS, lo:], sm[:, j % RS, lo:], ACT.Exp, bias=nm[:, j % RS:j % RS + 1],
                                         accum_out=ot[:, j % RO, E:E + 1]).then_inc(exp_done, 1)

                def output(r, s):
                    u, b, j = plan[s]
                    g, h = u % GROUPS, head_of(r, u)
                    if b == SAMP:
                        return
                    jj = r * NB + j
                    t0, d, _ = block_tokens(g, b)
                    act.wait_ge(pv_done, after(jj))
                    nc.scalar.activation(ot[:, j % RO, 0:E], po[j % 2][:, 0:E], ACT.Copy).then_inc(o_evac, 1)
                    act.wait_ge(o_evac, after(jj))
                    act.dma_start(strided(o_dram, t0, P, d)[:, bass.ds(h + g * HEADS, 1), :].rearrange("t o e -> t (o e)"),
                                  ot[:, j % RO, :]).then_inc(o_stored[j % RO], 16)

                def body(r):
                    for s in range(STEPS + 4):
                        if s < STEPS:
                            project_read(r, s)
                        if 0 <= s - 1 < STEPS:
                            evac_T(r, s - 1)
                            store_kv(r, s - 1)
                        if 0 <= s - 2 < STEPS:
                            exponent(r, s - 2)
                        if 0 <= s - 4 < STEPS:
                            output(r, s - 4)
                rounds(act, body)
                for i in range(RKV):
                    act.wait_ge(kv_stored[i], LEAD_DMA + 16 * ROUNDS * kv_slot_total[i])
                for i in range(RO):
                    act.wait_ge(o_stored[i], LEAD_DMA + 16 * ROUNDS * NB // RO)
                for i in range(2):
                    act.wait_ge(samp_stored[i], LEAD_DMA + 16 * ROUNDS * UNITS)

            @block.vector
            def _(dve):
                for x in (w_lo, meaned, qk_normed, s_masked, max_neg, pt_evac):
                    dve.sem_inc(x, LEAD)
                dve.wait_ge(gain_in, 32)
                nc.vector.tensor_scalar(gains[:, 0, :, :], gains[:, 0, :, :], float(E) ** -0.5, None, ALU.mult).then_inc(gain_ready, 1)

                def split_lo(u, slot, k):
                    dve.wait_ge(w_hi, after(u * KT + k))
                    nc.vector.tensor_tensor(wL[slot][:, k, :], wst[:, k, :, :].rearrange("p i c -> p (i c)"),
                                            wH[slot][:, k, :].bitcast(F32), ALU.subtract).then_inc(w_lo, 1)

                def mean(r, s):
                    u, b, j = plan[s]
                    g = u % GROUPS
                    n = r * STEPS + s
                    rows = P if b < BLOCKS else NS
                    dve.wait_ge(squared, after(2 * n + 1))
                    dve.wait_ge(powered, after(n - 1))
                    nc.vector.tensor_scalar(ms[0:rows, s % 2, :], ss[0:rows, s % 2, :], 1.0 / E, EPS, ALU.mult, ALU.add).then_inc(meaned, 1)

                def normalise(r, s):
                    u, b, j = plan[s]
                    g = u % GROUPS
                    n = r * STEPS + s
                    rows = P if b < BLOCKS else NS
                    src = pp[s % 2]
                    dve.wait_ge(powered, after(n))
                    if b < BLOCKS:
                        jj = r * NB + j
                        dve.wait_ge(t_done, after(jj - RQ))
                        qdst, kdst = qn[:, j % RQ, :], kv[:, j % RKV, 0, :]
                    else:
                        qdst, kdst = sq[:, j % 2, 0, :], sq[:, j % 2, 1, :]
                    dve.wait_ge(act_read, after(n))
                    nc.vector.scalar_tensor_tensor(qdst, src[0:rows, 0:P], rs[0:rows, s % 2, 0:1], gains[0:rows, 0, g, :], ALU.mult, ALU.mult)
                    nc.vector.scalar_tensor_tensor(kdst, src[0:rows, P:2 * P], rs[0:rows, s % 2, 1:2], gains[0:rows, 1, g, :],
                                                   ALU.mult, ALU.mult).then_inc(qk_normed, 1)

                def mask_max(r, s):
                    u, b, j = plan[s]
                    g = u % GROUPS
                    if b == SAMP:
                        return
                    jj = r * NB + j
                    lo = 0 if block_tokens(g, b)[2] else P
                    dve.wait_ge(s_done, after(jj))
                    dve.wait_ge(exp_done, after(jj - RS))
                    dve.wait_ge(o_stored[j % RO], r * (16 * NB // RO) + (LEAD_DMA + 16 * (j // RO)))
                    apart(dve, v["passed"])
                    nc.vector.tensor_tensor_reduce(sm[:, j % RS, lo:], psc[j % 2][:, lo:2 * P], mask[:, lo:], 1.0, -3e38,
                                                   ALU.subtract, ALU.max, ot[:, j % RO, E + 1:E + 2]).then_inc(s_masked, 1)
                    dve.wait_ge(s_masked, after(jj))
                    nc.vector.tensor_scalar(nm[:, j % RS:j % RS + 1], ot[:, j % RO, E + 1:E + 2], -1.0, None, ALU.mult).then_inc(max_neg, 1)

                def evac_PT(r, s):
                    u, b, j = plan[s]
                    g = u % GROUPS
                    if b == SAMP:
                        return
                    jj = r * NB + j
                    lo = 0 if block_tokens(g, b)[2] else P
                    dve.wait_ge(pt_done, after(jj))
                    dve.wait_ge(pv_done, after(jj - RS))
                    nc.vector.tensor_copy(prT[:, j % RS, lo:], ppt[:, lo:2 * P]).then_inc(pt_evac, 1)

                for k in range(KT):
                    split_lo(0, 0, k)
                dve.wait_ge(mask_step, 3)
                dve.wait_ge(gain_ready, 1)

                def body(r):
                    for s in range(STEPS + 4):
                        if s < STEPS:
                            mean(r, s)
                        if 0 <= s - 2 < STEPS:
                            mask_max(r, s - 2)
                        if s < STEPS:
                            normalise(r, s)
                        if 0 <= s - 3 < STEPS:
                            evac_PT(r, s - 3)
                        if s < STEPS:
                            u, b, _ = plan[s]
                            if 4 <= b < 4 + KT:
                                split_lo(r * UNITS + (u + 1), (u + 1) % 2, b - 4)
                rounds(dve, body)

            @block.tensor
            def _(pe):
                for x in (proj_done, t_done, s_done, pt_done, pv_done):
                    pe.sem_inc(x, LEAD)

                def project(r, s, slot):
                    u, b, j = plan[s]
                    g = u % GROUPS
                    n = r * STEPS + s
                    rows = P if b < BLOCKS else NS
                    cols = tokens(g, b)
                    pe.wait_ge(act_read, after(n - 2))
                    pe.wait_ge(qk_normed, after(n - 2))
                    if b == 0:
                        pe.wait_ge(w_lo, after((r * UNITS + u) * KT + KT - 1))
                    three_pass(nc, pp[s % 2][0:rows, 0:3 * P], [(hH[:, k, cols], hL[:, k, cols], wH[slot][:, k, :], wL[slot][:, k, :])
                                                                for k in range(KT)]).then_inc(proj_done, 1)

                def transposes(r, s):
                    u, b, j = plan[s]
                    g = u % GROUPS
                    if b == SAMP:
                        return
                    jj = r * NB + j
                    pe.wait_ge(qk_normed, after(r * STEPS + s))
                    pe.wait_ge(t_evac, after(jj - 1))
                    nc.tensor.transpose(pqk[:, 0:P], qn[:, j % RQ, :], ident[:, :])
                    nc.tensor.transpose(pqk[:, P:2 * P], kv[:, j % RKV, 0, :], ident[:, :]).then_inc(t_done, 1)

                def scores(r, s):
                    u, b, j = plan[s]
                    g = u % GROUPS
                    if b == SAMP:
                        return
                    jj = r * NB + j
                    prev = block_tokens(g, b)[2]
                    pe.wait_ge(t_evac, after(jj))
                    pe.wait_ge(s_masked, after(jj - 2))
                    if prev:
                        nc.tensor.matmul(psc[j % 2][:, 0:P], qkT[:, j % RT, 0, :], qkT[:, (j - 1) % RT, 1, :], start=True, stop=True)
                    nc.tensor.matmul(psc[j % 2][:, P:2 * P], qkT[:, j % RT, 0, :], qkT[:, j % RT, 1, :], start=True, stop=True).then_inc(s_done, 1)

                def probs_T(r, s):
                    u, b, j = plan[s]
                    g = u % GROUPS
                    if b == SAMP:
                        return
                    jj = r * NB + j
                    pe.wait_ge(exp_done, after(jj))
                    pe.wait_ge(pt_evac, after(jj - 1))
                    if block_tokens(g, b)[2]:
                        nc.tensor.transpose(ppt[:, 0:P], pr[:, j % RS, 0:P], ident[:, :])
                    nc.tensor.transpose(ppt[:, P:2 * P], pr[:, j % RS, P:2 * P], ident[:, :]).then_inc(pt_done, 1)

                def values(r, s):
                    u, b, j = plan[s]
                    g = u % GROUPS
                    if b == SAMP:
                        return
                    jj = r * NB + j
                    prev = block_tokens(g, b)[2]
                    pe.wait_ge(pt_evac, after(jj))
                    pe.wait_ge(o_evac, after(jj - 2))
                    if prev:
                        nc.tensor.matmul(po[j % 2][:, 0:E], prT[:, j % RS, 0:P], kv[:, (j - 1) % RKV, 1, :], start=True, stop=False)
                    nc.tensor.matmul(po[j % 2][:, 0:E], prT[:, j % RS, P:2 * P], kv[:, j % RKV, 1, :], start=not prev, stop=True).then_inc(pv_done, 1)

                def body(r):
                    for s in range(STEPS + 4):
                        if s < STEPS:
                            project(r, s, plan[s][0] % 2)
                        if 0 <= s - 1 < STEPS:
                            transposes(r, s - 1)
                        if 0 <= s - 2 < STEPS:
                            scores(r, s - 2)
                        if 0 <= s - 3 < STEPS:
                            probs_T(r, s - 3)
                        if 0 <= s - 4 < STEPS:
                            values(r, s - 4)
                rounds(pe, body)


def combine(nc, scope, v):
    ident, aTs = v["ident"], v["aTs"]
    w_a, w_b, w_o = v["w_a_out"][0], v["w_b_out"][0], v["w_out"][0]
    o_dram, bT_dram, gT_dram, gate_dram = v["o_dram"], v["bT_dram"], v["gT_dram"], v["gate_dram"]
    xp, yp, xs, ys = v["xp"], v["yp"], v["xs"], v["ys"]
    NT, CW = 2, 2 * P
    CS = CW + NS
    NC = SEQ // CW
    RG, RA = 4, 4
    stack = ExitStack()
    with stack:
        sb, ps, sem = scope(stack)
        NW = 16
        wH = sb("m_wH", [P, NW, D], F32R)
        with ExitStack() as whole_weights:
            w_whole = scope(whole_weights)[0]("w_whole", [P, NW, D])
        wL = sb("m_wL", [P, NW, D], F32R)
        ol = [sb(f"ol{i}", [P, NO, OW]) for i in range(NT)]
        bl = sb("bl", [P, 4, CS])
        zl = sb("zl", [P, 4, CW])
        gl = [sb(f"gl{i}", [P, 2, CS]) for i in range(RG)]
        xl = [sb(f"xl{i}", [P, D]) for i in range(NT)]
        yst = [sb(f"yst{i}", [P, D]) for i in range(NT)]
        a32 = sb("a32", [P, 4, CS])
        abH = sb("abH", [P, KT, CS], F32R)
        abL = sb("abL", [P, KT, CS], F32R)
        mH = sb("mH", [P, KT, CS], F32R)
        mL = sb("mL", [P, KT, CS], F32R)
        gm = [sb(f"gm{i}", [P, 2, CS]) for i in range(2)]
        m32 = [sb(f"m32{i}", [P, CS]) for i in range(2)]
        gate_b = sb("gate_b", [P, D])
        cw = sb("cw", [P, NT, 5, NO])
        pT = ps("c_pT", [P, 512])
        pa = ps("c_pa", [P, RA, 512])
        py = [ps(f"c_py{i}", [P, 512]) for i in range(2)]

        names = ("cstep", "bl_in", "zl_in", "gate_in", "cexp", "cdiff", "weighted", "a_ready", "aT_done", "aT_gated", "ab_hi", "ab_lo",
                 "pa_done", "gmul", "m_sum", "m_hi", "m_lo", "y_done", "y_mul", "y_ready", "samp_in", "s_done", "s_step", "s_out", "a_hi", "w_whole_hi", "w_split")
        (cstep, bl_in, zl_in, gate_in, cexp, cdiff, weighted, a_ready, aT_done, aT_gated, ab_hi, ab_lo,
         pa_done, gmul, m_sum, m_hi, m_lo, y_done, y_mul, y_ready, samp_in, s_done, s_step, s_out, a_hi, w_whole_hi, w_split) = (sem("c_" + n) for n in names)
        ol_in = [sem(f"ol_in{i}") for i in range(NT)]
        gl_in = [sem(f"gl_in{i}") for i in range(RG)]
        xl_in = [sem(f"xl_in{i}") for i in range(NT)]
        y_out = [sem(f"y_out{i}") for i in range(NT)]
        wo_landed = [sem(f"wo_landed{i}") for i in range(NW // 2)]

        def chunks(eng, body):
            with eng.Fori(0, NC - 1) as c:
                body(c, False)
            body(NC - 1, True)

        def branch_banks(f, last):
            if last:
                return pa[:, 2 * (f % 2):2 * (f % 2) + 2, 0:CS]
            return pa[:, f % RA, :].rearrange("p (a t) -> p a t", a=2)

        with nc.Block() as block:
            @block.sync
            def _(sp):
                def attention(c):
                    for i in range(NT):
                        sp.wait_ge(aT_gated, after(c * NT + (i - NT)))
                        apart(sp, v["passed"])
                        sp.dma_start(ol[i][:, :, :].rearrange("p n e -> p (n e)"),
                                     o_dram[bass.ds(c * CW + i * P, P), :, :].rearrange("t n e -> t (n e)")).then_inc(ol_in[i], 16)
                    sp.wait_ge(aT_gated, after(c * NT - 1))
                    apart(sp, v["passed"])
                    sp.dma_start(zl[:, :, :], gT_dram[0:4, :, bass.ds(c * CW, CW)].rearrange("f p t -> p f t")).then_inc(zl_in, 16)
                    sp.wait_ge(ab_lo, after(c * 2 - 1))
                    apart(sp, v["passed"])
                    sp.dma_start(bl[:, :, :], bT_dram[:, :, bass.ds(c * CW, CS)].rearrange("f p t -> p f t")).then_inc(bl_in, 16)

                def gates(c, fs, last):
                    cols = CS if last else CW
                    for f in fs:
                        sp.wait_ge(gmul, after(c * KT + (f - RG)))
                        apart(sp, v["passed"])
                        pair = gT_dram[4:20, :, bass.ds(c * CW, cols)].rearrange("(a f) p t -> f p a t", f=KT)
                        sp.dma_start(gl[f % RG][:, :, 0:cols], pair[f]).then_inc(gl_in[f % RG], 16)

                sp.dma_start(gate_b[:, :], gate_dram[0:1, :].to_broadcast([P, D])).then_inc(gate_in, 16)
                attention(0)

                def body(c, last):
                    gates(c, range(0, RG), last)
                    for i in range(NT):
                        sp.wait_ge(y_ready, after((c * NT + (i - NT)) * 2 + 1))
                        apart(sp, v["passed"])
                        sp.dma_start(xl[i][:, :], xp[bass.ds(c * CW + i * P, P), :]).then_inc(xl_in[i], 16)
                    if not last:
                        attention(c + 1)
                    gates(c, range(RG, KT), last)
                chunks(sp, body)
                sp.wait_ge(aT_gated, after(NC * NT - 1))
                sp.dma_start(ol[0][0:NS, :, :].rearrange("p n e -> p (n e)")[:, 0:D], xs).then_inc(samp_in, 16)
                sp.dma_start(ol[1][0:NS, :, :].rearrange("p n e -> p (n e)")[:, 0:D], gate_dram[1:1 + NS, :]).then_inc(samp_in, 16)
                sp.wait_ge(s_step, 4)
                sp.dma_start(ys, ol[1][0:NS, :, :].rearrange("p n e -> p (n e)")[:, 0:D]).then_inc(s_out, 16)
                sp.wait_ge(s_out, 16)
                sp.wait_ge(v["bulk"], 16 * (2 * NS + 8 * NS))
                sp.wait_ge(v["late"], 48)

            @block.gpsimd
            def _(pool):
                def split(c):
                    pool.wait_ge(pa_done, after(c * KT - 1))
                    pool.wait_ge(bl_in, c * 16 + 16)
                    apart(pool, v["passed"])
                    nc.gpsimd.tensor_copy(abH[:, 4:8, :], bl[:, :, :]).then_inc(ab_hi, 1)
                split(0)

                def body(c, last):
                    if not last:
                        split(c + 1)
                chunks(pool, body)

            @block.scalar
            def _(act):
                act.sem_inc(m_hi, LEAD)
                for x in y_out:
                    act.sem_inc(x, LEAD_DMA)

                def weights(t, i):
                    act.wait_ge(cdiff, t + 1)
                    nc.scalar.activation(cw[:, i, 2, :], cw[:, i, 1, :], ACT.Exp).then_inc(cexp, 1)

                def attention_hi(c):
                    act.wait_ge(pa_done, after(c * KT - 1))
                    act.wait_ge(aT_gated, after(c * NT + 1))
                    nc.scalar.activation(abH[:, 0:4, :], a32[:, :, :], ACT.Copy).then_inc(a_hi, 1)

                def body(c, last):
                    cols = CS if last else CW
                    for f in range(KT):
                        act.wait_ge(m_sum, after(c * KT + f))
                        act.wait_ge(y_done, after(c * (2 * NT) - 1))
                        nc.scalar.activation(mH[:, f, 0:cols], m32[f % 2][:, 0:cols], ACT.Copy).then_inc(m_hi, 1)
                        if f % 4 == 3 and not last:
                            weights(c * NT + (NT + f // 4), f // 4)
                    for i in range(NT):
                        act.wait_ge(y_ready, after((c * NT + i) * 2 + 1))
                        act.dma_start(yp[bass.ds(c * CW + i * P, P), :], yst[i][:, :]).then_inc(y_out[i], 16)
                        if i == 0 and not last:
                            attention_hi(c + 1)

                for n in range(0, NW, 2):
                    w, at = ((w_a, n) if n < 4 else (w_b, n - 4) if n < 8 else (w_o, n - 8))
                    act.dma_start(w_whole[:, n:n + 2, :], w[at * P:(at + 2) * P, :].rearrange("(k p) c -> p k c", p=P)).then_inc(wo_landed[n // 2], 16)
                weights(0, 0)
                weights(1, 1)
                for n in range(NW):
                    if n == KT:
                        attention_hi(0)
                    act.wait_ge(wo_landed[n // 2], 16)
                    nc.scalar.activation(wH[:, n, :], w_whole[:, n, :], ACT.Copy).then_inc(w_whole_hi, 1)
                chunks(act, body)
                for i in range(NT):
                    act.wait_ge(y_out[i], LEAD_DMA + 16 * NC)

            @block.vector
            def _(dve):
                for x in (a_ready, aT_gated, ab_lo, gmul, m_sum, m_lo, y_ready):
                    dve.sem_inc(x, LEAD)
                total = 7

                def groups(c, i):
                    t = c * NT + i
                    o = ol[i][:, :, :]
                    m, l = o[:, :, E + 1:E + 2].rearrange("p n o -> p (n o)"), o[:, :, E:E + 1].rearrange("p n o -> p (n o)")
                    by_head = lambda ap: ap.rearrange("p (g h) -> p h g", h=HEADS)
                    as_groups = lambda ap: ap.rearrange("p (g h) -> p g h", h=HEADS)
                    over = lambda ap: ap.unsqueeze(1).to_broadcast([P, GROUPS, HEADS])
                    row = lambda k: cw[:, i, k, :]
                    at = [0]

                    def chained(ins):
                        at[0] += 1
                        ins.then_inc(cstep, 1)
                        dve.wait_ge(cstep, t * total + at[0])

                    dve.wait_ge(ol_in[i], c * 16 + 16)
                    chained(nc.vector.tensor_reduce(row(0)[:, 0:HEADS], by_head(m), AX.X, ALU.max))
                    nc.vector.tensor_tensor(as_groups(row(1)), as_groups(m), over(row(0)[:, 0:HEADS]), ALU.subtract).then_inc(cdiff, 1)
                    dve.wait_ge(cexp, t + 1)
                    chained(nc.vector.tensor_tensor(row(3), row(2), l, ALU.mult))
                    chained(nc.vector.tensor_reduce(row(0)[:, 4:8], by_head(row(3)), AX.X, ALU.add))
                    chained(nc.vector.reciprocal(row(0)[:, 8:12], row(0)[:, 4:8]))
                    chained(nc.vector.tensor_tensor(as_groups(row(4)), as_groups(row(2)), over(row(0)[:, 8:12]), ALU.mult))
                    chained(nc.vector.tensor_tensor(o[:, :, 0:E], o[:, :, 0:E], row(4).unsqueeze(2).to_broadcast([P, NO, E]), ALU.mult))
                    chained(nc.vector.tensor_tensor(o[:, 0:HEADS, 0:E], o[:, 0:HEADS, 0:E], o[:, HEADS:2 * HEADS, 0:E], ALU.add))
                    nc.vector.tensor_tensor(o[:, 0:HEADS, 0:E], o[:, 0:HEADS, 0:E], o[:, 2 * HEADS:, 0:E], ALU.add).then_inc(a_ready, 1)
                    assert at[0] == total

                def gate_a(c, i):
                    t = c * NT + i
                    if i == 0:
                        dve.wait_ge(zl_in, c * 16 + 16)
                        dve.wait_ge(ab_lo, after(c * 2 - 1))
                    dve.wait_ge(aT_done, t + 1)
                    cols = slice(i * P, (i + 1) * P)
                    nc.vector.tensor_tensor(a32[:, :, cols], pT[:, :].rearrange("p (h t) -> p h t", t=P), zl[:, :, cols],
                                            ALU.mult).then_inc(aT_gated, 1)

                def split(c):
                    dve.wait_ge(ab_hi, c + 1)
                    nc.vector.tensor_tensor(abL[:, 4:8, :], bl[:, :, :], abH[:, 4:8, :].bitcast(F32), ALU.subtract).then_inc(ab_lo, 1)
                    dve.wait_ge(a_hi, c + 1)
                    nc.vector.tensor_tensor(abL[:, 0:4, :], a32[:, :, :], abH[:, 0:4, :].bitcast(F32), ALU.subtract).then_inc(ab_lo, 1)

                def branch(c, f, last):
                    n = c * KT + f
                    cols = CS if last else CW
                    dve.wait_ge(pa_done, after(n))
                    dve.wait_ge(gl_in[f % RG], c * (16 * KT // RG) + 16 * (f // RG + 1))
                    nc.vector.tensor_tensor(gm[f % 2][:, :, 0:cols], branch_banks(f, last), gl[f % RG][:, :, 0:cols], ALU.mult).then_inc(gmul, 1)
                    dve.wait_ge(gmul, after(n))
                    nc.vector.tensor_tensor(m32[f % 2][:, 0:cols], gm[f % 2][:, 0, 0:cols], gm[f % 2][:, 1, 0:cols], ALU.add).then_inc(m_sum, 1)
                    dve.wait_ge(m_hi, after(n))
                    nc.vector.tensor_tensor(mL[:, f, 0:cols], m32[f % 2][:, 0:cols], mH[:, f, 0:cols].bitcast(F32), ALU.subtract).then_inc(m_lo, 1)

                def result(c, i, j):
                    n = (c * NT + i) * 2 + j
                    cols = slice(j * 512, (j + 1) * 512)
                    dve.wait_ge(y_done, after(n))
                    if j == 0:
                        dve.wait_ge(y_out[i], c * 16 + LEAD_DMA)
                        dve.wait_ge(xl_in[i], c * 16 + 16)
                    nc.vector.tensor_tensor(yst[i][:, cols], py[j][:, :], gate_b[:, cols], ALU.mult).then_inc(y_mul, 1)
                    dve.wait_ge(y_mul, n + 1)
                    nc.vector.tensor_tensor(yst[i][:, cols], yst[i][:, cols], xl[i][:, cols], ALU.add).then_inc(y_ready, 1)

                def samples():
                    dve.wait_ge(samp_in, 32)
                    x_s, gate_s = (ol[i][0:NS, :, :].rearrange("p n e -> p (n e)") for i in range(NT))
                    for j in range(2):
                        cols = slice(j * 512, (j + 1) * 512)
                        dve.wait_ge(s_done, 1 + j)
                        nc.vector.tensor_tensor(gate_s[:, cols], py[j][0:NS, :], gate_s[:, cols], ALU.mult).then_inc(s_step, 1)
                        dve.wait_ge(s_step, 2 * j + 1)
                        nc.vector.tensor_tensor(gate_s[:, cols], gate_s[:, cols], x_s[:, cols], ALU.add).then_inc(s_step, 1)

                def weights_lo(n):
                    dve.wait_ge(w_whole_hi, n + 1)
                    nc.vector.tensor_tensor(wL[:, n, :], w_whole[:, n, :], wH[:, n, :].bitcast(F32), ALU.subtract).then_inc(w_split, 1)

                nc.vector.tensor_copy(a32[:, :, CW:], aTs[:, :, :])
                dve.wait_ge(gate_in, 16)
                for i in range(NT):
                    groups(0, i)
                for i in range(NT):
                    gate_a(0, i)
                for n in range(KT):
                    weights_lo(n)
                split(0)
                for n in range(KT, NW):
                    weights_lo(n)

                def body(c, last):
                    for f in range(KT):
                        branch(c, f, last)
                        if f % 4 == 3 and not last:
                            groups(c + 1, f // 4)
                    if last:
                        samples()
                    for j in range(2):
                        result(c, 0, j)
                    if not last:
                        gate_a(c + 1, 0)
                        gate_a(c + 1, 1)
                        split(c + 1)
                    for j in range(2):
                        result(c, 1, j)
                chunks(dve, body)

            @block.tensor
            def _(pe):
                pe.sem_inc(pa_done, LEAD)
                pe.sem_inc(y_done, LEAD)

                def transposes(c, i):
                    t = c * NT + i
                    pe.wait_ge(a_ready, after(t))
                    pe.wait_ge(aT_gated, after(t - 1))
                    for h in range(HEADS):
                        last = nc.tensor.transpose(pT[:, h * P:(h + 1) * P], ol[i][:, h, 0:E], ident[:, :])
                    last.then_inc(aT_done, 1)

                def branch(c, f, last):
                    n = c * KT + f
                    cols = CS if last else CW
                    pe.wait_ge(gmul, after(n - (2 if last else RA)))
                    for a in range(2):
                        done = three_pass(nc, branch_banks(f, last)[:, a, :],
                                          [(wH[:, k, f * P:(f + 1) * P], wL[:, k, f * P:(f + 1) * P], abH[:, k, 0:cols], abL[:, k, 0:cols])
                                           for k in range(4 * a, 4 * a + 4)])
                    done.then_inc(pa_done, 1)

                def out_terms(cols, j):
                    return [(mH[:, k, cols], mL[:, k, cols], wH[:, KT + k, j * 512:(j + 1) * 512], wL[:, KT + k, j * 512:(j + 1) * 512])
                            for k in range(KT)]

                def result(c, i, j, last):
                    n = (c * NT + i) * 2 + j
                    pe.wait_ge(y_ready, after(n - 2))
                    if last and i == 0:
                        pe.wait_ge(s_step, 2 * j + 1)
                    before = (lambda k: pe.wait_ge(m_lo, after(c * KT + k))) if i == 0 and j == 0 and not last else None
                    three_pass(nc, py[j][:, :], out_terms(slice(i * P, (i + 1) * P), j), before).then_inc(y_done, 1)

                def samples(c, j):
                    pe.wait_ge(y_ready, after((c * NT - 1) * 2 + j))
                    before = (lambda k: pe.wait_ge(m_lo, after(c * KT + k))) if j == 0 else None
                    three_pass(nc, py[j][0:NS, :], out_terms(slice(CW, CS), j), before).then_inc(s_done, 1)

                for i in range(NT):
                    transposes(0, i)

                def body(c, last):
                    pe.wait_ge(ab_lo, after(c * 2 + 1))
                    pe.wait_ge(w_split, KT)
                    for f in range(KT):
                        branch(c, f, last)
                    pe.wait_ge(w_split, NW)
                    if last:
                        for j in range(2):
                            samples(c, j)
                    for j in range(2):
                        result(c, 0, j, last)
                    if not last:
                        transposes(c + 1, 0)
                    result(c, 1, 0, last)
                    if not last:
                        transposes(c + 1, 1)
                    result(c, 1, 1, last)
                chunks(pe, body)


_INS = ["x_prompt", "x_sample", "state_kv_w128", "state_kv_w512", "state_kv_w2048", "state_pool", "c_prompt", "c_sample", "norm_g",
        "w_ada", "b_ada", "w_in", "q_gain", "k_gain", "w_pool", "b_pool", "pool_scale", "w_a_out", "w_b_out", "w_out"]
_OUTS = [(1, SEQ, D), (NS, 1, D), (1, 1, 128, 2, HEADS, E), (1, 1, 512, 2, HEADS, E), (1, 1, 2048, 2, HEADS, E), (1, 1, NPS, 512),
         (1, NS, 128, 2, HEADS, E), (1, NS, 512, 2, HEADS, E), (1, NS, 2048, 2, HEADS, E), (1, NS, NPS, 512)]


def kernel(**inputs):
    import numpy as _np
    import concourse.bacc as _bacc
    from concourse import mybir as _mybir
    from concourse.bass_utils import run_bass_kernel_spmd as _run

    nc = _bacc.Bacc("TRN2", target_bir_lowering=False, num_devices=1, dynamic_dma_scratch_size=1024)
    arrays, args = {}, []
    for name in _INS:
        a = _np.ascontiguousarray(inputs[name])
        arrays[f"in_{name}_dram"] = a
        args.append(nc.dram_tensor(f"in_{name}_dram", a.shape, _mybir.dt.from_np(a.dtype), kind="ExternalInput").ap())
    for i, shape in enumerate(_OUTS):
        args.append(nc.dram_tensor(f"out_{i}_dram", shape, F32, kind="ExternalOutput").ap())
    build(nc, *args)
    r = _run(nc, [arrays], core_ids=[0])
    return tuple(r.results[0][f"out_{i}_dram"] for i in range(len(_OUTS)))
```

```python
from contextlib import ExitStack

import concourse.bass as bass
from concourse import mybir

F32 = mybir.dt.float32
F32R = mybir.dt.float32r
ALU = mybir.AluOpType
ACT = mybir.ActivationFunctionType
AX = mybir.AxisListType

P = 128
D = 1024
KT = D // P
SEQ = 2048
NS = 8
TT = SEQ + NS
HEADS, GROUPS, E = 4, 3, 128
PATTERNS = ((128, 1), (512, 4), (2048, 16))
BLOCKS = SEQ // P
CH = 512
NCH = SEQ // CH
NBC = 5
BCH = -(-TT // NBC)
CQ, CK, CV, CZA, CU, CZB, CGA = 0, 1536, 3072, 4608, 5120, 5632, 6144
POOLS = (2, 4, 8, 16)
PADU = 16
NPS = 15
EPS = 1e-6
MASKED = -1e30
LEAD = 16
LEAD_DMA = 16
OW = E + 2
NO = GROUPS * HEADS


def after(n):
    return n + (LEAD + 1)


def block_tokens(g, b):
    d = PATTERNS[g][1]
    per = BLOCKS // d
    r, n = divmod(b, per)
    return r + d * P * n, d, n > 0


def strided(ap, start, count, step):
    return ap[start:start + (count - 1) * step + 1:step]


def build(nc, x_prompt, x_sample, state_kv_w128, state_kv_w512, state_kv_w2048, state_pool, c_prompt, c_sample,
          norm_g, w_ada, b_ada, w_in, q_gain, k_gain, w_pool, b_pool, pool_scale, w_a_out, w_b_out, w_out,
          y_p, y_s, kv128_p, kv512_p, kv2048_p, pool_p, kv128_s, kv512_s, kv2048_s, pool_s):
    states = (state_kv_w128, state_kv_w512, state_kv_w2048)
    kv_p = (kv128_p, kv512_p, kv2048_p)
    kv_s = (kv128_s, kv512_s, kv2048_s)
    xp, yp = x_prompt[0], y_p[0]
    xs = x_sample.rearrange("b s d -> (b s) d")
    ys = y_s.rearrange("b s d -> (b s) d")
    w_in_v = w_in[0].rearrange("(k p) c -> p k c", p=P)

    o_dram = nc.dram_tensor("o_dram", [SEQ, NO, OW], F32, kind="Internal").ap()
    bT_dram = nc.dram_tensor("bT_dram", [4, P, TT], F32, kind="Internal").ap()
    gT_dram = nc.dram_tensor("gT_dram", [20, P, TT], F32, kind="Internal").ap()
    samp_dram = nc.dram_tensor("samp_dram", [NS, 3, NO, E], F32, kind="Internal").ap()
    gate_dram = nc.dram_tensor("gate_dram", [1 + NS, D], F32, kind="Internal").ap()
    snew_dram = nc.dram_tensor("snew_dram", [NS, HEADS, GROUPS], F32, kind="Internal").ap()
    pnew_dram = nc.dram_tensor("pnew_dram", [NS, HEADS, GROUPS], F32, kind="Internal").ap()

    whole = ExitStack()
    phase_sems = []

    def end_phase():
        nc.clear_and_free_semaphores(phase_sems)
        phase_sems.clear()
        nc.all_engine_barrier()

    with whole:
        def scope(stack):
            def sb(name, shape, dt=F32, side=None):
                return stack.enter_context(nc.sbuf_tensor(name, shape, dt, side=side))

            def ps(name, shape, dt=F32):
                return stack.enter_context(nc.psum_tensor(name, shape, dt))

            def sem(name):
                one = nc.alloc_semaphore(name=name)
                if stack is not whole:
                    phase_sems.append(one)
                return one
            return sb, ps, sem

        keep_sb, _, keep_sem = scope(whole)
        ident = keep_sb("ident", [P, P])
        vecT = keep_sb("vecT", [P, 40])
        aTs = keep_sb("aTs", [P, HEADS, NS])
        bulk = keep_sem("bulk")
        passed = {e.engine: keep_sem(f"passed{i}") for i, e in enumerate((nc.sync, nc.gpsimd, nc.vector))}
        late = keep_sem("late")

        big = ExitStack()
        whole.enter_context(big)
        big_sb, _, _ = scope(big)
        hH = big_sb("hH", [P, KT, TT], F32R)
        hL = big_sb("hL", [P, KT, TT], F32R)

        w_first = prepare(nc, scope, locals())
        end_phase()
        attend(nc, scope, locals())
        end_phase()
        ol, cw = branches(nc, scope, locals())
        end_phase()
        big.close()
        combine(nc, scope, locals())


def prepare(nc, scope, v):
    xp, xs, hH, hL, ident, vecT = v["xp"], v["xs"], v["hH"], v["hL"], v["ident"], v["vecT"]
    w_ada_v = v["w_ada"][0].rearrange("(k p) c -> p k c", p=P)
    gate_dram = v["gate_dram"]
    NC = 1 + NS
    XR, WR, SR = 8, 2, 4
    NX = SEQ // P
    stack = ExitStack()
    with stack:
        sb, ps, sem = scope(stack)
        with ExitStack() as same_place:
            w_first = scope(same_place)[0]("w_first", [P, 3, KT, P])
        w_st0 = sb("w_st0", [P, KT, 512])
        rows = sb("rows", [40, P])
        c_in = sb("c_in", [NC, D])
        c_sig = sb("c_sig", [NC, D])
        scT = sb("scT", [P, KT, NC])
        b_gate = sb("b_gate", [NC, D])
        gate_sb = c_in
        rows_sb = c_sig
        w_st = [w_st0] + [sb(f"w_st{i}", [P, KT, 512]) for i in range(1, WR)]
        xt = [sb(f"xt{i}", [P, D]) for i in range(XR)]
        xst = sb("xst", [NS, D])
        junk = sb("junk", [P, D], mybir.dt.bfloat16)
        ss = sb("ss", [P, NX + 1])
        ms = sb("ms", [P, NX + 1])
        rs = sb("rs", [P, NX + 1])
        mhalf = sb("mhalf", [P, 1])
        addT = sb("addT", [P, KT, NC])
        scl1 = sb("scl1", [P, KT, NC])
        mulT = sb("mulT", [P, KT, NC])
        hst = [sb(f"hst{i}", [P, CH]) for i in range(SR)]
        hs_m = sb("hs_m", [P, KT, NS])
        hs_t = sb("hs_t", [P, KT, NS])
        ps_t = [ps(f"ps_t{i}", [P, CH]) for i in range(4)]
        ps_small = ps("ps_small", [P, 512])
        ps_mod = ps("ps_mod", [P, 512])
        ps_row = [ps(f"ps_row{i}", [P, 512]) for i in range(2)]
        mod = ps_mod[:, 0:2 * KT * NC].rearrange("p (f c) -> p f c", c=NC)
        cT = ps_small[:, 64:64 + KT * NC].rearrange("p (k c) -> p k c", c=NC)
        xsT = ps_small[:, 256:256 + KT * NS].rearrange("p (k c) -> p k c", c=NS)

        rows_in, c_landed, bg_landed, xs_landed = (sem(n) for n in ("rows_in", "c_landed", "bg_landed", "xs_landed"))
        w_landed = [sem(f"wa_landed{i}") for i in range(WR)]
        x_landed = [sem(f"x_landed{i}") for i in range(XR)]
        w_used, ident_zero, ident_ready, mhalf_ready = (sem(n) for n in ("wa_used", "ident_zero", "ident_ready", "mhalf_ready"))
        rows_T, vec_ready, c_sigm, c_silu, c_T, sc_ready = (sem(n) for n in ("rows_T", "vec_ready", "c_sigm", "c_silu", "c_T", "sc_ready"))
        mod_step, mod_ready, row_evac, mod_T, gate_ready = (sem(n) for n in ("mod_step", "mod_ready", "row_evac", "mod_T", "gate_ready"))
        squared, x_normed, xs_normed = (sem(n) for n in ("squared", "x_normed", "xs_normed"))
        mean_ready = [sem(n) for n in ("mean_ready", "mean_s_ready")]
        powered = [sem(n) for n in ("powered", "powered_s")]
        hT_done, h_mod, h_lo = (sem(n) for n in ("hT_done", "h_mod", "h_lo"))
        h_hi = {who: sem(f"h_hi_{who}") for who in ("act", "dve")}
        samp_T, samp_step, samp_hi, gate_stored, first_in = (sem(n) for n in ("samp_T", "samp_step", "samp_hi", "gate_stored", "first_in"))

        def squares_before(t):
            return t if t < 3 else t + 1

        HI = ("dve", "dve", "dve", "act")

        def hi_count(who, n):
            return sum(HI[m % len(HI)] == who for m in range(n + 1))

        with nc.Block() as block:
            @block.sync
            def _(sp):
                sp.dma_start(c_in[0:1, :], v["c_prompt"]).then_inc(c_landed, 16)
                sp.dma_start(c_in[1:NC, :], v["c_sample"]).then_inc(c_landed, 16)

                def load_w(n):
                    if n >= WR:
                        sp.wait_ge(w_used, n - WR + 1)
                    sp.dma_start(w_st[n % WR][:, :, :], w_ada_v[:, :, n * 512:(n + 1) * 512]).then_inc(w_landed[n % WR], 16)

                def load_x(t):
                    if t >= XR:
                        sp.wait_ge(hT_done, ((t - XR) // 4 + 1) * KT)
                    sp.dma_start(xt[t % XR][:, :], xp[t * P:(t + 1) * P, :]).then_inc(x_landed[t % XR], 16)

                load_w(0)
                load_w(1)
                load_x(0)
                load_x(1)
                load_w(2)
                load_x(2)
                load_x(3)
                load_w(3)
                for t in range(4, XR):
                    load_x(t)
                load_w(4)
                load_w(5)
                for t in range(XR, NX):
                    load_x(t)
                sp.wait_ge(w_used, 5)
                for i, c0 in enumerate((CQ, CK, CV)):
                    sp.dma_start(w_first[:, i, :, :], v["w_in_v"][:, :, c0:c0 + P]).then_inc(first_in, 16)
                sp.wait_ge(first_in, 48)
                sp.wait_ge(gate_ready, 2)
                sp.dma_start(gate_dram, gate_sb[:, :]).then_inc(gate_stored, 16)
                sp.wait_ge(gate_stored, 16)

            @block.gpsimd
            def _(pool):
                nc.gpsimd.memset(ident[:, :], 0.0).then_inc(ident_zero, 1)
                nc.gpsimd.memset(mhalf[:, :], -0.5).then_inc(mhalf_ready, 1)
                pool.wait_ge(ident_zero, 1)
                nc.gpsimd.affine_select(out=ident[:, :], in_=ident[:, :], compare_op=ALU.not_equal, fill=1.0,
                                        base=0, pattern=[[-1, P]], channel_multiplier=1).then_inc(ident_ready, 1)
                pool.wait_ge(mhalf_ready, 1)

                def power(t):
                    rows_n = P if t < NX else NS
                    pool.wait_ge(mean_ready[t == NX], t + 1 if t < NX else 1)
                    nc.gpsimd.tensor_tensor(rs[0:rows_n, t:t + 1], ms[0:rows_n, t:t + 1], mhalf[0:rows_n, :],
                                            ALU.pow).then_inc(powered[t == NX], 1)

                for t in (*range(XR), NX):
                    power(t)
                pool.wait_ge(samp_step, 2)
                nc.gpsimd.tensor_copy(hH[:, :, SEQ:TT], hs_t[:, :, :]).then_inc(samp_hi, 1)
                for t in range(XR, NX):
                    power(t)

            @block.scalar
            def _(act):
                act.dma_start(rows[0:24, :], v["b_ada"][0].rearrange("(a b) -> a b", b=P)).then_inc(rows_in, 16)
                act.dma_start(rows[24:32, :], v["norm_g"][0].rearrange("(a b) -> a b", b=P)).then_inc(rows_in, 16)
                act.wait_ge(c_landed, 32)
                nc.scalar.activation(c_sig[:, :], c_in[:, :], ACT.Sigmoid).then_inc(c_sigm, 1)
                act.dma_start(rows[32:36, :], v["b_pool"][0]).then_inc(rows_in, 16)
                act.dma_start(rows[36:40, :], v["pool_scale"][0].rearrange("(a b) -> a b", b=P)).then_inc(rows_in, 16)
                act.dma_start(b_gate[:, :], v["b_ada"][0:1, 2 * D:3 * D].to_broadcast([NC, D])).then_inc(bg_landed, 16)
                act.dma_start(xst[:, :], xs).then_inc(xs_landed, 16)

                def square(t):
                    act.wait_ge(x_landed[t % XR], 16 * (t // XR) + 16)
                    if t:
                        act.wait_ge(squared, squares_before(t))
                    nc.scalar.activation(junk[:, :], xt[t % XR][:, :], ACT.Square, accum_out=ss[:, t:t + 1]).then_inc(squared, 1)

                for t in range(3):
                    square(t)
                act.wait_ge(xs_landed, 16)
                act.wait_ge(squared, 3)
                nc.scalar.activation(junk[0:NS, :], xst[:, :], ACT.Square, accum_out=ss[0:NS, NX:NX + 1]).then_inc(squared, 1)
                for t in range(3, XR):
                    square(t)
                act.wait_ge(mod_ready, 2)
                for tc in range(NCH):
                    for k in range(KT):
                        n = tc * KT + k
                        if 0 < tc < NCH - 1 and k % 2 == 0:
                            square(4 * (tc + 1) + k // 2)
                        act.wait_ge(hT_done, n + 1)
                        if n >= SR:
                            act.wait_ge(h_lo, n - SR + 1)
                        nc.scalar.activation(hst[n % SR][:, :], ps_t[n % 4][:, :], ACT.Identity, bias=addT[:, k, 0:1],
                                             scale=mulT[:, k, 0:1]).then_inc(h_mod, 1)
                        if HI[n % 4] == "act":
                            act.wait_ge(h_mod, n + 1)
                            nc.scalar.activation(hH[:, k, tc * CH:(tc + 1) * CH], hst[n % SR][:, :], ACT.Copy).then_inc(h_hi["act"], 1)

            @block.vector
            def _(dve):
                dve.wait_ge(c_sigm, 1)
                nc.vector.tensor_tensor(c_sig[:, :], c_sig[:, :], c_in[:, :], ALU.mult).then_inc(c_silu, 1)
                dve.wait_ge(c_T, 1)
                nc.vector.tensor_copy(scT[:, :, :], cT).then_inc(sc_ready, 1)

                def tile_of(t):
                    return (xst, NS) if t == NX else (xt[t % XR], P)

                def normalise(t):
                    mean(t)
                    scale(t)

                def mean(t):
                    samp, (tile, rows_n) = t == NX, tile_of(t)
                    dve.wait_ge(squared, 4 if samp else squares_before(t) + 1)
                    nc.vector.tensor_scalar(ms[0:rows_n, t:t + 1], ss[0:rows_n, t:t + 1], 1.0 / D, EPS,
                                            ALU.mult, ALU.add).then_inc(mean_ready[samp], 1)

                def scale(t):
                    samp, (tile, rows_n) = t == NX, tile_of(t)
                    dve.wait_ge(powered[samp], 1 if samp else t + 1)
                    nc.vector.tensor_scalar(tile[:, :], tile[:, :], rs[0:rows_n, t:t + 1], None,
                                            ALU.mult).then_inc(xs_normed if samp else x_normed, 1)

                def row_out(n):
                    dve.wait_ge(w_used, n + 1)
                    if n >= 2:
                        dve.wait_ge(mod_T, n - 1)
                    nc.vector.tensor_copy(rows_sb[:, (n % 2) * 512:(n % 2 + 1) * 512], ps_row[n % 2][0:NC, :]).then_inc(row_evac, 1)

                def gate_out(j):
                    dve.wait_ge(w_used, 5 + j)
                    cols = slice(j * 512, (j + 1) * 512)
                    nc.vector.tensor_tensor(gate_sb[:, cols], ps_row[j][0:NC, :], b_gate[:, cols], ALU.add).then_inc(gate_ready, 1)

                row_out(0)
                normalise(0)
                normalise(1)
                row_out(1)
                normalise(2)
                dve.wait_ge(rows_T, 1)
                nc.vector.tensor_copy(vecT[:, :], ps_small[:, 0:40]).then_inc(vec_ready, 1)
                normalise(3)
                row_out(2)
                for t in range(4, XR - 1):
                    normalise(t)
                row_out(3)
                dve.wait_ge(mod_T, 4)
                dve.wait_ge(vec_ready, 1)
                nc.vector.tensor_tensor(addT[:, :, :], mod[:, 0:KT, :], vecT[:, 0:KT].unsqueeze(2).to_broadcast([P, KT, NC]),
                                        ALU.add).then_inc(mod_ready, 1)
                nc.vector.tensor_tensor(scl1[:, :, :], mod[:, KT:2 * KT, :],
                                        vecT[:, KT:2 * KT].unsqueeze(2).to_broadcast([P, KT, NC]), ALU.add).then_inc(mod_step, 1)
                dve.wait_ge(mod_step, 1)
                nc.vector.tensor_scalar(scl1[:, :, :], scl1[:, :, :], 1.0, None, ALU.add).then_inc(mod_step, 1)
                dve.wait_ge(mod_step, 2)
                nc.vector.tensor_tensor(mulT[:, :, :], scl1[:, :, :], vecT[:, 24:32].unsqueeze(2).to_broadcast([P, KT, NC]),
                                        ALU.mult).then_inc(mod_ready, 1)
                normalise(XR - 1)
                normalise(NX)
                dve.wait_ge(bg_landed, 16)
                for tc in range(NCH):
                    for k in range(KT):
                        n = tc * KT + k
                        cols = slice(tc * CH, (tc + 1) * CH)
                        if 0 < tc < NCH - 1:
                            (mean if k % 2 == 0 else scale)(4 * (tc + 1) + k // 2)
                        if HI[n % 4] == "dve":
                            dve.wait_ge(h_mod, n + 1)
                            nc.vector.tensor_copy(hH[:, k, cols], hst[n % SR][:, :]).then_inc(h_hi["dve"], 1)
                        dve.wait_ge(h_hi[HI[n % 4]], hi_count(HI[n % 4], n))
                        nc.vector.tensor_tensor(hL[:, k, cols], hst[n % SR][:, :], hH[:, k, cols].bitcast(F32),
                                                ALU.subtract).then_inc(h_lo, 1)
                    if tc == 0:
                        dve.wait_ge(mod_ready, 2)
                        dve.wait_ge(samp_T, 1)
                        nc.vector.tensor_tensor(hs_m[:, :, :], xsT, mulT[:, :, 1:NC], ALU.mult).then_inc(samp_step, 1)
                        dve.wait_ge(samp_step, 1)
                        nc.vector.tensor_tensor(hs_t[:, :, :], hs_m[:, :, :], addT[:, :, 1:NC], ALU.add).then_inc(samp_step, 1)
                    elif tc < NCH - 1:
                        gate_out(tc - 1)
                dve.wait_ge(samp_hi, 1)
                nc.vector.tensor_tensor(hL[:, :, SEQ:TT], hs_t[:, :, :], hH[:, :, SEQ:TT].bitcast(F32), ALU.subtract)

            @block.tensor
            def _(pe):
                pe.wait_ge(ident_ready, 1)
                pe.wait_ge(c_silu, 1)
                for k in range(KT):
                    last = nc.tensor.transpose(cT[:, k, :], c_sig[:, k * P:(k + 1) * P], ident[0:NC, 0:NC])
                last.then_inc(c_T, 1)
                pe.wait_ge(sc_ready, 1)

                def row(n):
                    pe.wait_ge(w_landed[n % WR], 16 * (n // WR) + 16)
                    if n >= 2:
                        pe.wait_ge(row_evac, n - 1)
                    for k in range(KT):
                        last = nc.tensor.matmul(ps_row[n % 2][0:NC, :], scT[:, k, :], w_st[n % WR][:, k, :],
                                                start=(k == 0), stop=(k == KT - 1))
                    last.then_inc(w_used, 1)

                def row_T(n):
                    pe.wait_ge(row_evac, n + 1)
                    for f in range(4):
                        last = nc.tensor.transpose(mod[:, 4 * n + f, :], rows_sb[:, (n % 2) * 512 + f * P:(n % 2) * 512 + (f + 1) * P],
                                                   ident[0:NC, 0:NC])
                    last.then_inc(mod_T, 1)

                row(0)
                row(1)
                row_T(0)
                pe.wait_ge(rows_in, 64)
                nc.tensor.transpose(ps_small[:, 0:40], rows[:, :], ident[0:40, 0:40]).then_inc(rows_T, 1)
                row(2)
                row_T(1)
                row(3)
                row_T(2)
                row_T(3)
                for tc in range(NCH):
                    pe.wait_ge(x_normed, 4 * tc + 4)
                    for k in range(KT):
                        n = tc * KT + k
                        if n >= 4:
                            pe.wait_ge(h_mod, n - 3)
                        for i in range(4):
                            last = nc.tensor.transpose(ps_t[n % 4][:, i * P:(i + 1) * P],
                                                       xt[(4 * tc + i) % XR][:, k * P:(k + 1) * P], ident[:, :])
                        last.then_inc(hT_done, 1)
                    if tc == 0:
                        pe.wait_ge(xs_normed, 1)
                        for k in range(KT):
                            last = nc.tensor.transpose(xsT[:, k, :], xst[:, k * P:(k + 1) * P], ident[0:NS, 0:NS])
                        last.then_inc(samp_T, 1)
                    elif tc < NCH - 1:
                        row(3 + tc)
    return w_first


def branches(nc, scope, v):
    hH, hL, ident, vecT, aTs = (v[n] for n in ("hH", "hL", "ident", "vecT", "aTs"))
    w_in_v, bT_dram, gT_dram, bulk, late = (v[n] for n in ("w_in_v", "bT_dram", "gT_dram", "bulk", "late"))
    o_dram, samp_dram, snew_dram, pnew_dram, states = (v[n] for n in ("o_dram", "samp_dram", "snew_dram", "pnew_dram", "states"))
    pool_p, pool_s, state_pool = v["pool_p"][0, 0], v["pool_s"][0], v["state_pool"][0]
    PAIRS, NF = 4, 28
    SCORE0, SOFT0, VALUE0, END0 = 12, 20, 22, 26
    BH = NS * HEADS
    HE = HEADS * E
    stack = ExitStack()
    with stack:
        sb, ps, sem = scope(stack)
        sb("wst", [P, 2, KT, P])
        wst = [v["w_first"][:, i, :, :] for i in range(2)]
        wH = [sb(f"wH{i}", [P, KT, P], F32R) for i in range(2)]
        wL = [sb(f"wL{i}", [P, KT, P], F32R) for i in range(2)]
        gst = [sb(f"gst{i}", [P, BCH]) for i in range(2)]
        pst = [sb(f"pst{i}", [P, BCH]) for i in range(2)]
        ost = [sb(f"ost{i}", [P, BCH]) for i in range(NBC)]
        wpool = sb("wpool", [P, 4, P])
        recip = sb("recip", [P, PADU])
        sp_rows = sb("sp_rows", [NS * NPS, 4 * P])
        spT = sb("spT", [P, 4, NS * NPS])
        s_sum = sb("s_sum", [P, 2, NS])
        utail = sb("utail", [P, 4, NPS + NS])
        urow = sb("urow", [NPS, 4 * P])
        usrow = sb("usrow", [NS, 4 * P])

        pooling = ExitStack()
        with pooling:
            pool_sb, _, _ = scope(pooling)
            uT = pool_sb("uT", [P, PADU + TT], side="right")
            run = [pool_sb(f"run{i}", [P, PADU + SEQ], side="right") for i in range(2)]
            mixed = pool_sb("mixed", [P, TT], side="right")
            zS = pool_sb("zS", [P, TT], side="right")
        ol, cw = combine_tiles(sb)
        kt = [sb(f"kt{g}", [P, HE]) for g in range(GROUPS)]
        qb = [sb(f"qb{g}", [P, HE]) for g in range(GROUPS)]
        vt = (kt, qb)
        prod = sb("prod", [P, HE])
        sc = sb("sc", [P, GROUPS, BH])
        q_new = sb("q_new", [NS, NO, E])
        kv_new = sb("kv_new", [NS, NO, E])
        snew = sb("snew", [NS, HEADS, GROUPS])
        scr = sb("scr", [BH, GROUPS * P])
        scn = sb("scn", [BH, GROUPS])
        st = sb("st", [BH, 8])
        pcr = sb("pcr", [BH, GROUPS * P])
        pcn = sb("pcn", [BH, GROUPS])
        pT = sb("pT", [P, GROUPS, BH])
        pn = sb("pn", [NS, NO])
        diag = sb("diag", [NS, NO, NS])
        zs = sb("zs", [P, 4, NS])

        pp = [ps(f"pp{i}", [P, 512]) for i in range(NBC)]
        ppool = [ps(f"ppool{i}", [P, 512]) for i in range(2)]
        psA = ps("d_psA", [P, 512])

        w_landed = [sem(f"wb_landed{i}") for i in range(2)]
        w_hi, w_lo, proj_done, evac = (sem(n) for n in ("w_hi", "w_lo", "proj_done", "evac"))
        out_stored = [sem(f"out_stored{i}") for i in range(NBC)]
        wpool_in, sp_in, spT_done, spT_ready, pad_ready = (sem(n) for n in ("wpool_in", "sp_in", "spT_done", "spT_ready", "pad_ready"))
        window, mix_ready, pool_done, biased, gated, tail_saved, tail_T, tail_ready = (
            sem(n) for n in ("window", "mix_ready", "pool_done", "biased", "gated", "tail_saved", "tail_T", "tail_ready"))
        b_stored = [sem(f"b_stored{i}") for i in range(2)]
        ol_landed, ol_diff, ol_exp = (sem(n) for n in ("ol_landed", "ol_diff", "ol_exp"))
        qk_in, vnew_in, scored, multiplied, snew_ready, snew_out, snew_in, scT_done = (
            sem(n) for n in ("qk_in", "vnew_in", "scored", "multiplied", "snew_ready", "snew_out", "snew_in", "scT_done"))
        max_ready, dexp, p_ready, pn_out, pn_in, pT_done, pT_ready, diag_ready, pv_used, zs_in = (
            sem(n) for n in ("max_ready", "dexp", "p_ready", "pn_out", "pn_in", "pT_done", "pT_ready", "diag_ready", "pv_used", "zs_in"))
        k_landed = [sem(f"k_landed{g}") for g in range(GROUPS)]
        q_landed = [sem(f"q_landed{g}") for g in range(GROUPS)]
        v_landed = [[sem(f"v_landed{i}_{g}") for g in range(GROUPS)] for i in range(2)]

        def cols_of(c):
            return slice(c * BCH, min((c + 1) * BCH, TT))

        def width(c):
            return cols_of(c).stop - cols_of(c).start

        def column(n):
            if n < 2 * PAIRS:
                return (CU, CZB)[n % 2] + n // 2 * P
            return CZA + (n - 2 * PAIRS) * P if n < 2 * PAIRS + 4 else gate_column(n)

        def gate_column(n):
            return n * P + (CGA - (2 * PAIRS + 4) * P)

        def carried(g, b, which):
            W, d = PATTERNS[g]
            rows = states[g][0, bass.ds(b, 1), :, which, :, :].rearrange("o w h e -> (o w) (h e)")
            return strided(rows, 0, P, d)

        with nc.Block() as block:
            @block.sync
            def _(sp):
                def load(n, slot, col):
                    sp.wait_ge(w_lo, after(n - 2))
                    apart(sp, v["passed"])
                    sp.dma_start(wst[slot][:, :, :], w_in_v[:, :, bass.ds(col, P)]).then_inc(w_landed[slot], 16)

                def store_b(p):
                    for c in range(NBC):
                        m = p * NBC + c
                        sp.wait_ge(gated, m + 1)
                        sp.dma_start(bT_dram[p, :, cols_of(c)], gst[m % 2][:, 0:width(c)]).then_inc(b_stored[m % 2], 16)

                def keys(b):
                    for g in range(GROUPS):
                        sp.wait_ge(scored, after(b * GROUPS + (g - GROUPS)))
                        apart(sp, v["passed"])
                        sp.dma_start(kt[g][:, :], carried(g, b, 0)).then_inc(k_landed[g], 16)
                        sp.dma_start(qb[g][:, :], samp_dram[bass.ds(b, 1), 0, g * HEADS:(g + 1) * HEADS, :].rearrange("o h e -> o (h e)")
                                     .to_broadcast([P, HE])).then_inc(q_landed[g], 16)

                def values(b, i):
                    for g in range(GROUPS):
                        sp.wait_ge(pv_used, after(b * GROUPS + (g - 2 * GROUPS)))
                        apart(sp, v["passed"])
                        sp.dma_start(vt[i][g][:, :], carried(g, b, 1)).then_inc(v_landed[i][g], 16)

                for i in range(2):
                    sp.sem_inc(w_landed[i], 16)
                sp.dma_start(sp_rows[:, :], state_pool.rearrange("b j c -> (b j) c")).then_inc(sp_in, 16)
                sp.dma_start(wpool[:, :, :], v["w_pool"][0].rearrange("g c d -> c g d")).then_inc(wpool_in, 16)
                sp.dma_start(pool_s[:, 0:NPS - 1, :], state_pool[:, 1:NPS, :]).then_inc(late, 16)
                for p in range(PAIRS):
                    load(2 * p + 2, 0, column(2 * p + 2))
                    shifted_copy(sp, v, 1, 2 * p, bulk)
                    if p:
                        store_b(p - 1)
                    load(2 * p + 3, 1, column(2 * p + 3))
                    shifted_copy(sp, v, 1, 2 * p + 1, bulk)
                load(2 * PAIRS + 2, 0, column(2 * PAIRS + 2))
                store_b(PAIRS - 1)
                load(2 * PAIRS + 3, 1, column(2 * PAIRS + 3))
                for i in range(2):
                    sp.dma_start(ol[i][:, :, :], o_dram[i * P:(i + 1) * P, :, :]).then_inc(ol_landed, 16)
                rows = lambda ap: ap.rearrange("b n e -> b (n e)")
                sp.dma_start(rows(q_new[:, :, :]), rows(samp_dram[:, 0])).then_inc(qk_in, 16)
                sp.dma_start(rows(kv_new[:, :, :]), rows(samp_dram[:, 1])).then_inc(qk_in, 16)
                sp.wait_ge(snew_ready, 1)
                sp.dma_start(rows(kv_new[:, :, :]), rows(samp_dram[:, 2])).then_inc(vnew_in, 16)
                sp.dma_start(snew_dram.rearrange("b h g -> b (h g)"), snew[:, :, :].rearrange("b h g -> b (h g)")).then_inc(snew_out, 16)
                sp.wait_ge(snew_out, 16)
                sp.dma_start(scn[:, :], snew_dram.rearrange("b h g -> (b h) g")).then_inc(snew_in, 16)
                sp.wait_ge(tail_ready, 2)
                sp.dma_start(pool_p, urow[:, :]).then_inc(late, 16)
                sp.dma_start(pool_s[:, NPS - 1, :], usrow[:, :]).then_inc(late, 16)
                with sp.Fori(0, NS // 2) as i:
                    n = i * 2 + SCORE0
                    for j in range(2):
                        load(n + j, j, gate_column(n + j))
                        keys(i * 2 + j)
                        shifted_copy(sp, v, 0, i * 2 + j, bulk)
                load(SOFT0, 0, gate_column(SOFT0))
                load(SOFT0 + 1, 1, gate_column(SOFT0 + 1))
                sp.wait_ge(out_stored[NBC - 1], LEAD_DMA + 16 * 4)
                sp.dma_start(zs[:, :, :], gT_dram[0:4, :, SEQ:TT].rearrange("f p t -> p f t")).then_inc(zs_in, 16)
                sp.wait_ge(p_ready, 2)
                sp.dma_start(pnew_dram.rearrange("b h g -> (b h) g"), pcn[:, :]).then_inc(pn_out, 16)
                sp.wait_ge(pn_out, 16)
                sp.dma_start(pn[:, :], pnew_dram.rearrange("b h g -> b (h g)")).then_inc(pn_in, 16)
                with sp.Fori(0, 2) as i:
                    n = i * 2 + VALUE0
                    for j in range(2):
                        load(n + j, j, gate_column(n + j))
                    for j in range(4):
                        values(i * 4 + j, j % 2)
                load(END0, 0, gate_column(END0))
                load(END0 + 1, 1, gate_column(END0 + 1))
                sp.wait_ge(late, 48)
                for i in range(2):
                    sp.wait_ge(b_stored[i], 16 * PAIRS * NBC // 2)

            @block.gpsimd
            def _(pool):
                nc.gpsimd.memset(uT[:, 0:PADU], 0.0).then_inc(pad_ready, 1)
                for t in range(PADU):
                    nc.gpsimd.memset(recip[:, t:t + 1], 1.0 / (t + 1)).then_inc(pad_ready, 1)

                def split_hi(n, slot, landed):
                    pool.wait_ge(w_landed[slot], landed)
                    pool.wait_ge(proj_done, after((n - 1) * NBC - 1))
                    apart(pool, v["passed"])
                    nc.gpsimd.tensor_copy(wH[slot][:, :, :], wst[slot][:, :, :]).then_inc(w_hi, 1)

                pool.wait_ge(w_hi, 1)
                split_hi(1, 1, 16)
                with pool.Fori(1, NF // 2) as i:
                    split_hi(i * 2, 0, i * 16 + 16)
                    split_hi(i * 2 + 1, 1, i * 16 + 16)

            @block.vector
            def _(dve):
                dve.sem_inc(w_lo, LEAD)
                dve.sem_inc(scored, LEAD)

                def split_lo(n, slot):
                    dve.wait_ge(w_hi, n + 1)
                    dve.wait_ge(proj_done, after((n - 1) * NBC - 1))
                    nc.vector.tensor_tensor(wL[slot][:, :, :], wst[slot][:, :, :], wH[slot][:, :, :].bitcast(F32),
                                            ALU.subtract).then_inc(w_lo, 1)

                steps = [0]

                def chained(ins):
                    steps[0] += 1
                    ins.then_inc(window, 1)
                    dve.wait_ge(window, steps[0])

                def windows(p):
                    w = POOLS[p]
                    dve.wait_ge(evac, after(2 * p * NBC + NBC - 1))
                    if p:
                        dve.wait_ge(pool_done, NBC * p)
                    src, first = uT, 0
                    for s in range(p + 1):
                        shift = 1 << s
                        first += shift
                        dst = run[s % 2]
                        chained(nc.vector.tensor_tensor(dst[:, first:], src[:, first:PADU + SEQ], src[:, first - shift:PADU + SEQ - shift], ALU.add))
                        src = dst
                    nc.vector.scalar_tensor_tensor(mixed[:, w:SEQ], src[:, PADU + w:], 1.0 / w, uT[:, PADU + w:PADU + SEQ], ALU.mult, ALU.subtract)
                    chained(nc.vector.tensor_tensor(src[:, PADU:PADU + w], src[:, PADU:PADU + w], recip[:, 0:w], ALU.mult))
                    nc.vector.tensor_tensor(mixed[:, 0:w], src[:, PADU:PADU + w], uT[:, PADU:PADU + w], ALU.subtract)
                    nc.vector.tensor_copy(utail[:, p, :], uT[:, PADU + SEQ - NPS:]).then_inc(tail_saved, 1)
                    u_s = uT[:, PADU + SEQ:]
                    rows = spT[:, p, :].rearrange("p (b j) -> p b j", j=NPS)[:, :, NPS - (w - 1):]
                    chained(nc.vector.tensor_reduce(s_sum[:, 0, :], rows, AX.X, ALU.add))
                    chained(nc.vector.tensor_tensor(s_sum[:, 1, :], s_sum[:, 0, :], u_s, ALU.add))
                    nc.vector.scalar_tensor_tensor(mixed[:, SEQ:TT], s_sum[:, 1, :], 1.0 / w, u_s, ALU.mult,
                                                   ALU.subtract).then_inc(mix_ready, 1)

                def gate(p):
                    for c in range(NBC):
                        m = NBC * p + c
                        dve.wait_ge(pool_done, m + 1)
                        t = pst[m % 2][:, 0:width(c)]
                        nc.vector.tensor_scalar(t, ppool[m % 2][:, 0:width(c)], vecT[:, 32 + p:33 + p], vecT[:, 36 + p:37 + p],
                                                ALU.add, ALU.mult).then_inc(biased, 1)
                        dve.wait_ge(biased, m + 1)
                        if m >= 2:
                            dve.wait_ge(b_stored[m % 2], 16 * (m // 2))
                        dve.wait_ge(evac, after((2 * p + 1) * NBC + c))
                        nc.vector.tensor_tensor(gst[m % 2][:, 0:width(c)], t, zS[:, cols_of(c)], ALU.mult).then_inc(gated, 1)

                def score(b):
                    for g in range(GROUPS):
                        dve.wait_ge(k_landed[g], b * 16 + 16)
                        dve.wait_ge(q_landed[g], b * 16 + 16)
                        dve.wait_ge(scored, after(b * GROUPS + (g - 1)))
                        nc.vector.tensor_tensor(prod[:, :], kt[g][:, :], qb[g][:, :], ALU.mult).then_inc(multiplied, 1)
                        dve.wait_ge(multiplied, b * GROUPS + (g + 1))
                        nc.vector.tensor_reduce(sc[:, g, bass.ds(b * HEADS, HEADS)], prod[:, :].rearrange("p (h e) -> p h e", e=E),
                                                AX.X, ALU.add).then_inc(scored, 1)

                split_lo(0, 0)
                split_lo(1, 1)
                dve.wait_ge(spT_done, 1)
                nc.vector.tensor_copy(spT[:, :, :].rearrange("p g r -> p (g r)"), ppool[1][:, 0:4 * NS * NPS]).then_inc(spT_ready, 1)
                dve.wait_ge(spT_ready, 1)
                dve.wait_ge(pad_ready, 1 + PADU)
                for p in range(PAIRS):
                    if p:
                        gate(p - 1)
                    split_lo(2 * p + 2, 0)
                    windows(p)
                    split_lo(2 * p + 3, 1)
                gate(PAIRS - 1)
                split_lo(2 * PAIRS + 2, 0)
                split_lo(2 * PAIRS + 3, 1)
                dve.wait_ge(tail_T, 1)
                nc.vector.tensor_copy(urow[:, :], ppool[0][0:NPS, :]).then_inc(tail_ready, 1)
                nc.vector.tensor_copy(usrow[:, :], ppool[1][0:NS, :]).then_inc(tail_ready, 1)
                dve.wait_ge(qk_in, 32)
                chained(nc.vector.tensor_tensor(q_new[:, :, :], q_new[:, :, :], kv_new[:, :, :], ALU.mult))
                nc.vector.tensor_reduce(snew[:, :, :].rearrange("b h g -> b g h"), q_new[:, :, :].rearrange("b (g h) e -> b g h e", h=HEADS),
                                        AX.X, ALU.add).then_inc(snew_ready, 1)
                with dve.Fori(0, NS // 2) as i:
                    for j in range(2):
                        split_lo(i * 2 + (SCORE0 + j), j)
                        score(i * 2 + j)
                split_lo(SOFT0, 0)
                split_lo(SOFT0 + 1, 1)
                dve.wait_ge(scT_done, 1)
                chained(nc.vector.tensor_copy(scr[:, :], ppool[0][0:BH, 0:GROUPS * P]))
                dve.wait_ge(snew_in, 16)
                nc.vector.tensor_reduce(st[:, 0:1], scr[:, :], AX.X, ALU.max)
                chained(nc.vector.tensor_reduce(st[:, 1:2], scn[:, :], AX.X, ALU.max))
                chained(nc.vector.tensor_tensor(st[:, 5:6], st[:, 0:1], st[:, 1:2], ALU.max))
                nc.vector.tensor_scalar(st[:, 2:3], st[:, 5:6], -1.0, None, ALU.mult).then_inc(max_ready, 1)
                dve.wait_ge(dexp, 2)
                chained(nc.vector.tensor_tensor(st[:, 6:7], st[:, 3:4], st[:, 4:5], ALU.add))
                chained(nc.vector.reciprocal(st[:, 7:8], st[:, 6:7]))
                nc.vector.tensor_scalar(pcr[:, :], pcr[:, :], st[:, 7:8], None, ALU.mult).then_inc(p_ready, 1)
                nc.vector.tensor_scalar(pcn[:, :], pcn[:, :], st[:, 7:8], None, ALU.mult).then_inc(p_ready, 1)
                dve.wait_ge(pn_in, 16)
                nc.vector.tensor_tensor(diag[:, :, :], pn[:, :].unsqueeze(2).to_broadcast([NS, NO, NS]),
                                        ident[0:NS, 0:NS].unsqueeze(1).to_broadcast([NS, NO, NS]), ALU.mult).then_inc(diag_ready, 1)
                dve.wait_ge(pT_done, 1)
                nc.vector.tensor_copy(pT[:, :, :].rearrange("p g n -> p (g n)"), ppool[1][:, 0:GROUPS * BH]).then_inc(pT_ready, 1)
                with dve.Fori(0, 2) as i:
                    for j in range(2):
                        split_lo(i * 2 + (VALUE0 + j), j)
                dve.wait_ge(ol_landed, 32)
                for i in range(2):
                    sum_groups(nc, ol[i][:, :, :], cw[:, i], chained, ol_diff, lambda: dve.wait_ge(ol_exp, i + 1))
                split_lo(END0, 0)
                split_lo(END0 + 1, 1)
                dve.wait_ge(pv_used, after(NS * GROUPS - 1))
                dve.wait_ge(zs_in, 16)
                nc.vector.tensor_tensor(aTs[:, :, :], psA[:, 0:BH].rearrange("p (h b) -> p h b", b=NS), zs[:, :, :], ALU.mult)

            @block.scalar
            def _(act):
                act.sem_inc(evac, LEAD)
                for c in range(NBC):
                    act.sem_inc(out_stored[c], LEAD_DMA)
                act.wait_ge(w_landed[0], 16)
                nc.scalar.activation(wH[0][:, :, :], wst[0], ACT.Copy).then_inc(w_hi, 1)

                def chunk(n, c, out, func):
                    act.wait_ge(proj_done, after(n * NBC + c))
                    nc.scalar.activation(out, pp[c][:, 0:width(c)], func).then_inc(evac, 1)

                for p in range(PAIRS):
                    if p:
                        act.wait_ge(mix_ready, p)
                    for c in range(NBC):
                        chunk(2 * p, c, uT[:, PADU + c * BCH:PADU + c * BCH + width(c)], ACT.Copy)
                    if p:
                        act.wait_ge(gated, NBC * p)
                    for c in range(NBC):
                        chunk(2 * p + 1, c, zS[:, cols_of(c)], ACT.Silu)

                def spilled(n, func):
                    for c in range(NBC):
                        act.wait_ge(out_stored[c], n * 16 + (LEAD_DMA - 16 * 2 * PAIRS))
                        chunk(n, c, ost[c][:, 0:width(c)], func)
                        act.wait_ge(evac, after(n * NBC + c))
                        act.dma_start(gT_dram[bass.ds(n - 2 * PAIRS, 1), :, cols_of(c)].rearrange("a p t -> p (a t)"),
                                      ost[c][:, 0:width(c)]).then_inc(out_stored[c], 16)

                with act.Fori(0, 4) as i:
                    spilled(i + 2 * PAIRS, ACT.Silu)
                with act.Fori(0, 8) as i:
                    spilled(i + SCORE0, ACT.Sigmoid)
                act.wait_ge(max_ready, 1)
                nc.scalar.activation(pcr[:, :], scr[:, :], ACT.Exp, bias=st[:, 2:3], accum_out=st[:, 3:4]).then_inc(dexp, 1)
                nc.scalar.activation(pcn[:, :], scn[:, :], ACT.Exp, bias=st[:, 2:3], accum_out=st[:, 4:5]).then_inc(dexp, 1)
                with act.Fori(0, 4) as i:
                    spilled(i + SOFT0, ACT.Sigmoid)
                for i in range(2):
                    act.wait_ge(ol_diff, i + 1)
                    nc.scalar.activation(cw[:, i, 2, :], cw[:, i, 1, :], ACT.Exp).then_inc(ol_exp, 1)
                with act.Fori(0, 4) as i:
                    spilled(i + (SOFT0 + 4), ACT.Sigmoid)
                for c in range(NBC):
                    act.wait_ge(out_stored[c], LEAD_DMA + 16 * (NF - 2 * PAIRS))

            @block.tensor
            def _(pe):
                pe.sem_inc(proj_done, LEAD)
                pe.sem_inc(pv_used, LEAD)

                def project(n, slot):
                    pe.wait_ge(w_lo, after(n))
                    for c in range(NBC):
                        pe.wait_ge(evac, after(n * NBC + (c - NBC)))
                        three_pass(nc, pp[c][:, 0:width(c)], [(wH[slot][:, k, :], wL[slot][:, k, :], hH[:, k, cols_of(c)], hL[:, k, cols_of(c)])
                                                              for k in range(KT)]).then_inc(proj_done, 1)

                def pooled(p):
                    if p == 0:
                        pe.wait_ge(wpool_in, 16)
                        pe.wait_ge(spT_ready, 1)
                    pe.wait_ge(mix_ready, p + 1)
                    for c in range(NBC):
                        m = NBC * p + c
                        if m >= 2:
                            pe.wait_ge(biased, m - 1)
                        nc.tensor.matmul(ppool[m % 2][:, 0:width(c)], wpool[:, p, :], mixed[:, cols_of(c)],
                                         start=True, stop=True).then_inc(pool_done, 1)

                def values(b, i):
                    for g in range(GROUPS):
                        pe.wait_ge(v_landed[i][g], (b - i) * 8 + 16)
                        for h in range(HEADS):
                            last = nc.tensor.matmul(psA[:, bass.ds(b + h * NS, 1)], vt[i][g][:, h * E:(h + 1) * E],
                                                    pT[:, g, bass.ds(b * HEADS + h, 1)], start=False, stop=True, skip_group_check=True)
                        last.then_inc(pv_used, 1)

                for p in range(PAIRS):
                    project(2 * p, 0)
                    if p:
                        pooled(p - 1)
                    else:
                        pe.wait_ge(sp_in, 16)
                        for g in range(4):
                            last = nc.tensor.transpose(ppool[1][:, g * NS * NPS:(g + 1) * NS * NPS], sp_rows[:, g * P:(g + 1) * P],
                                                       ident[0:NS * NPS, 0:NS * NPS])
                        last.then_inc(spT_done, 1)
                    project(2 * p + 1, 1)
                project(2 * PAIRS, 0)
                pooled(PAIRS - 1)
                project(2 * PAIRS + 1, 1)
                pe.wait_ge(tail_saved, PAIRS)
                pe.wait_ge(biased, NBC * PAIRS)
                for g in range(4):
                    nc.tensor.transpose(ppool[0][0:NPS, g * P:(g + 1) * P], utail[:, g, 0:NPS], ident[:, :])
                    last = nc.tensor.transpose(ppool[1][0:NS, g * P:(g + 1) * P], utail[:, g, NPS:], ident[:, :])
                last.then_inc(tail_T, 1)
                project(2 * PAIRS + 2, 0)
                project(2 * PAIRS + 3, 1)
                with pe.Fori(0, NS // 2) as i:
                    project(i * 2 + SCORE0, 0)
                    project(i * 2 + (SCORE0 + 1), 1)
                pe.wait_ge(scored, after(NS * GROUPS - 1))
                pe.wait_ge(tail_ready, 2)
                for g in range(GROUPS):
                    last = nc.tensor.transpose(ppool[0][0:BH, g * P:(g + 1) * P], sc[:, g, :], ident[:, :])
                last.then_inc(scT_done, 1)
                project(SOFT0, 0)
                pe.wait_ge(p_ready, 1)
                for g in range(GROUPS):
                    last = nc.tensor.transpose(ppool[1][:, g * BH:(g + 1) * BH], pcr[:, g * P:(g + 1) * P], ident[0:BH, 0:BH])
                last.then_inc(pT_done, 1)
                pe.wait_ge(diag_ready, 1)
                pe.wait_ge(vnew_in, 16)
                for h in range(HEADS):
                    for g in range(GROUPS):
                        nc.tensor.matmul(psA[:, h * NS:(h + 1) * NS], kv_new[:, g * HEADS + h, :], diag[:, h * GROUPS + g, :],
                                         start=(h == 0 and g == 0), stop=False, skip_group_check=True)
                project(SOFT0 + 1, 1)
                pe.wait_ge(pT_ready, 1)
                with pe.Fori(0, 2) as i:
                    for j in range(2):
                        project(i * 2 + (VALUE0 + j), j)
                        values(i * 4 + 2 * j, 0)
                        values(i * 4 + (2 * j + 1), 1)
                project(END0, 0)
                project(END0 + 1, 1)
    return ol, cw


def combine_tiles(sb):
    return [sb(f"ol{i}", [P, NO, OW], side="right") for i in range(2)], sb("cw", [P, 2, 5, NO], side="right")


def sum_groups(nc, o, cw, chained, diff_ready, wait_exp):
    m, l = o[:, :, E + 1:E + 2].rearrange("p n o -> p (n o)"), o[:, :, E:E + 1].rearrange("p n o -> p (n o)")
    by_head = lambda ap: ap.rearrange("p (g h) -> p h g", h=HEADS)
    as_groups = lambda ap: ap.rearrange("p (g h) -> p g h", h=HEADS)
    over = lambda ap: ap.unsqueeze(1).to_broadcast([P, GROUPS, HEADS])
    row = lambda k: cw[:, k, :]
    chained(nc.vector.tensor_reduce(row(0)[:, 0:HEADS], by_head(m), AX.X, ALU.max))
    nc.vector.tensor_tensor(as_groups(row(1)), as_groups(m), over(row(0)[:, 0:HEADS]), ALU.subtract).then_inc(diff_ready, 1)
    wait_exp()
    chained(nc.vector.tensor_tensor(row(3), row(2), l, ALU.mult))
    chained(nc.vector.tensor_reduce(row(0)[:, 4:8], by_head(row(3)), AX.X, ALU.add))
    chained(nc.vector.reciprocal(row(0)[:, 8:12], row(0)[:, 4:8]))
    chained(nc.vector.tensor_tensor(as_groups(row(4)), as_groups(row(2)), over(row(0)[:, 8:12]), ALU.mult))
    chained(nc.vector.tensor_tensor(o[:, :, 0:E], o[:, :, 0:E], row(4).unsqueeze(2).to_broadcast([P, NO, E]), ALU.mult))
    chained(nc.vector.tensor_tensor(o[:, 0:HEADS, 0:E], o[:, 0:HEADS, 0:E], o[:, HEADS:2 * HEADS, 0:E], ALU.add))
    return nc.vector.tensor_tensor(o[:, 0:HEADS, 0:E], o[:, 0:HEADS, 0:E], o[:, 2 * HEADS:, 0:E], ALU.add)


def apart(eng, passed):
    eng.sem_inc(passed[eng.engine], 1)


def three_pass(nc, out, terms, before=None):
    last = None
    for i, (sH, sL, mH, mL) in enumerate(terms):
        if before:
            before(i)
        nc.tensor.matmul(out, sH, mH, start=(i == 0), stop=False)
        nc.tensor.matmul(out, sH, mL, start=False, stop=False)
        last = nc.tensor.matmul(out, sL, mH, start=False, stop=(i == len(terms) - 1))
    return last


def shifted_copy(eng, v, g, b, done, piece=0, pieces=1):
    W = PATTERNS[g][0]
    n = (W - 1) * 2 * HEADS * E // pieces
    rows = (16 * (1 if g == 0 else 8 if g == 1 else 32)) // pieces
    first = piece * n
    def flat(a):
        return a[0].rearrange("b w k h e -> b (w k h e)")
    dst = flat(v["kv_s"][g])[bass.ds(b, 1), first:first + n].rearrange("o (r c) -> (o r) c", r=rows)
    src = flat(v["states"][g])[bass.ds(b, 1), first + 2 * HEADS * E:first + 2 * HEADS * E + n].rearrange("o (r c) -> (o r) c", r=rows)
    eng.dma_start(dst, src).then_inc(done, 16)


def attend(nc, scope, v):
    hH, hL, ident = v["hH"], v["hL"], v["ident"]
    w_in_v, o_dram, samp_dram, bulk = v["w_in_v"], v["o_dram"], v["samp_dram"], v["bulk"]
    SAMP = BLOCKS
    PAIR = 2
    UNITS = PAIR * GROUPS
    STEPS = UNITS * (BLOCKS + 1)
    NB = UNITS * BLOCKS
    ROUNDS = HEADS // PAIR
    plan = [(u, b, u * BLOCKS + b if b < BLOCKS else u) for u in range(UNITS) for b in range(BLOCKS + 1)]
    PIECES = 8
    PACE = STEPS // (NS // ROUNDS * PIECES)
    RKV, RQ, RT, RS, RO = 8, 2, 4, 2, 6

    def stored_rows(g, b):
        t0, d, _ = block_tokens(g, b)
        first = SEQ - PATTERNS[g][0]
        return (t0 - first, d) if t0 >= first else None

    kv_before = []
    kv_slot_total = [0] * RKV
    for u in range(UNITS):
        for b in range(BLOCKS):
            slot = (u * BLOCKS + b) % RKV
            kv_before.append(kv_slot_total[slot])
            if stored_rows(u % GROUPS, b):
                kv_slot_total[slot] += 1

    stack = ExitStack()
    with stack:
        sb, ps, sem = scope(stack)
        sb("a_wst", [P, 3, KT, P])
        wst = v["w_first"]
        wH = [sb(f"a_wH{i}", [P, KT, 3 * P], F32R) for i in range(2)]
        wL = [sb(f"a_wL{i}", [P, KT, 3 * P], F32R) for i in range(2)]
        mask = sb("mask", [P, 2 * P])
        gains = sb("gains", [P, 2, GROUPS, P])
        kv = sb("kv", [P, RKV, 2, P])
        qn = sb("qn", [P, RQ, P])
        qkT = sb("qkT", [P, RT, 2, P])
        sm = sb("sm", [P, RS, 2 * P])
        pr = sb("pr", [P, RS, 2 * P])
        prT = sb("prT", [P, RS, 2 * P])
        ot = sb("ot", [P, RO, OW])
        nm = sb("nm", [P, RS])
        junk = sb("a_junk", [P, P])
        ss = sb("a_ss", [P, 2, 2])
        ms = sb("a_ms", [P, 2, 2])
        rs = sb("a_rs", [P, 2, 2])
        mhalf = sb("a_mhalf", [P, 2])
        sq = sb("sq", [NS, 2, 3, P])
        pp = [ps(f"a_pp{i}", [P, 512]) for i in range(2)]
        pqk = ps("pqk", [P, 512])
        psc = [ps(f"psc{i}", [P, 512]) for i in range(2)]
        ppt = ps("ppt", [P, 512])
        po = [ps(f"po{i}", [P, 512]) for i in range(2)]

        w_landed, gain_in, mask_step, mhalf_ready, gain_ready = (sem(n) for n in ("aw_landed", "gain_in", "mask_step", "mhalf_ready2", "gain_ready"))
        w_hi, w_lo, next_in = sem("aw_hi"), sem("aw_lo"), sem("next_in")
        proj_done, squared, act_read, meaned, powered, qk_normed = (
            sem(n) for n in ("a_proj_done", "a_squared", "act_read", "a_meaned", "a_powered", "qk_normed"))
        t_done, t_evac, s_done, s_masked, max_neg, exp_done, pt_done, pt_evac, pv_done, o_evac = (
            sem(n) for n in ("t_done", "t_evac", "s_done", "s_masked", "max_neg", "exp_done", "pt_done", "pt_evac", "pv_done", "o_evac"))
        kv_stored = [sem(f"kv_stored{i}") for i in range(RKV)]
        o_stored = [sem(f"o_stored{i}") for i in range(RO)]
        samp_stored = [sem(f"samp_stored{i}") for i in range(2)]

        def rounds(eng, body):
            with eng.Fori(0, ROUNDS) as r:
                body(r)

        def three(ap):
            return ap.rearrange("p (i c) -> p i c", c=P)

        def head_of(r, u):
            return r * PAIR + u // GROUPS

        def tokens(g, b):
            if b == SAMP:
                return slice(SEQ, TT)
            t0, d, _ = block_tokens(g, b)
            return slice(t0, t0 + (P - 1) * d + 1, d)

        with nc.Block() as block:
            @block.sync
            def _(sp):
                def load(r, u):
                    h, g = head_of(r, u), u % GROUPS
                    sp.wait_ge(w_lo, after((r * UNITS + u) * KT - 1))
                    apart(sp, v["passed"])
                    for i, c0 in enumerate((CQ, CK, CV)):
                        sp.dma_start(wst[:, i, :, :], w_in_v[:, :, bass.ds(h * E + (c0 + g * HEADS * E), E)]).then_inc(w_landed, 16)

                sp.dma_start(gains[:, 0, :, :].rearrange("p g e -> p (g e)"), v["q_gain"].rearrange("o g e -> o (g e)").to_broadcast([P, GROUPS * E])).then_inc(gain_in, 16)
                sp.dma_start(gains[:, 1, :, :].rearrange("p g e -> p (g e)"), v["k_gain"].rearrange("o g e -> o (g e)").to_broadcast([P, GROUPS * E])).then_inc(gain_in, 16)
                sp.sem_inc(w_landed, 48)

                def body(r):
                    for s in range(STEPS):
                        u, b, _ = plan[s]
                        if b == 1:
                            load(r, u + 1)
                        piece, at = divmod(s, PACE)
                        if at == 0 and piece < NS // ROUNDS * PIECES:
                            sp.wait_ge(proj_done, after(r * STEPS + s))
                            apart(sp, v["passed"])
                            shifted_copy(sp, v, 2, r * (NS // ROUNDS) + piece // PIECES, bulk, piece % PIECES, PIECES)
                rounds(sp, body)
                sp.wait_ge(w_lo, after((ROUNDS * UNITS + 1) * KT - 1))
                for i, c0 in enumerate((CU, CZB)):
                    sp.dma_start(wst[:, i, :, :], w_in_v[:, :, c0:c0 + P]).then_inc(next_in, 16)
                sp.wait_ge(next_in, 32)

            @block.gpsimd
            def _(pool):
                pool.sem_inc(w_hi, LEAD)
                pool.sem_inc(powered, LEAD)
                nc.gpsimd.memset(mask[:, :], 0.0).then_inc(mask_step, 1)
                nc.gpsimd.memset(mhalf[:, :], -0.5).then_inc(mhalf_ready, 1)
                pool.wait_ge(mask_step, 1)
                nc.gpsimd.affine_select(out=mask[:, 0:P], in_=mask[:, 0:P], compare_op=ALU.is_ge, fill=-MASKED,
                                        base=0, pattern=[[1, P]], channel_multiplier=-1).then_inc(mask_step, 1)
                nc.gpsimd.affine_select(out=mask[:, P:2 * P], in_=mask[:, P:2 * P], compare_op=ALU.is_ge, fill=-MASKED,
                                        base=0, pattern=[[-1, P]], channel_multiplier=1).then_inc(mask_step, 1)
                pool.wait_ge(mhalf_ready, 1)

                def split_hi(u, slot, k):
                    if k == 0:
                        pool.wait_ge(w_landed, u * 48 + 48)
                    pool.wait_ge(w_lo, after(u * KT + k - 1))
                    apart(pool, v["passed"])
                    nc.gpsimd.tensor_copy(three(wH[slot][:, k, :]), wst[:, :, k, :]).then_inc(w_hi, 1)

                def power(r, s):
                    n = r * STEPS + s
                    rows = P if plan[s][1] < BLOCKS else NS
                    pool.wait_ge(meaned, after(n))
                    nc.gpsimd.tensor_tensor(rs[0:rows, s % 2, :], ms[0:rows, s % 2, :], mhalf[0:rows, :], ALU.pow).then_inc(powered, 1)

                def body(r):
                    for s in range(STEPS):
                        power(r, s)
                        u, b, _ = plan[s]
                        if 4 <= b < 4 + KT:
                            split_hi(r * UNITS + (u + 1), (u + 1) % 2, b - 4)
                rounds(pool, body)

            @block.scalar
            def _(act):
                for x in (squared, act_read, t_evac, exp_done, o_evac):
                    act.sem_inc(x, LEAD)
                for x in (*kv_stored, *o_stored, *samp_stored):
                    act.sem_inc(x, LEAD_DMA)

                act.wait_ge(w_hi, LEAD)
                act.wait_ge(w_landed, 48)
                for k in range(KT):
                    nc.scalar.activation(three(wH[0][:, k, :]), wst[:, :, k, :], ACT.Copy).then_inc(w_hi, 1)

                def project_read(r, s):
                    u, b, j = plan[s]
                    g = u % GROUPS
                    n = r * STEPS + s
                    rows = P if b < BLOCKS else NS
                    src = pp[s % 2]
                    act.wait_ge(proj_done, after(n))
                    act.wait_ge(meaned, after(n - 2))
                    for i in range(2):
                        act.wait_ge(squared, after(2 * n + i - 1))
                        nc.scalar.activation(junk[0:rows, :], src[0:rows, i * P:(i + 1) * P], ACT.Square,
                                             accum_out=ss[0:rows, s % 2, i:i + 1]).then_inc(squared, 1)
                    if b < BLOCKS:
                        jj = r * NB + j
                        act.wait_ge(pv_done, after(jj - RKV + 1))
                        act.wait_ge(kv_stored[j % RKV], r * (16 * kv_slot_total[j % RKV]) + (LEAD_DMA + 16 * kv_before[j]))
                        nc.scalar.activation(kv[:, j % RKV, 1, :], src[:, 2 * P:3 * P], ACT.Copy).then_inc(act_read, 1)
                    else:
                        act.wait_ge(samp_stored[j % 2], r * (32 * UNITS // 2) + (LEAD_DMA + 32 * (j // 2)))
                        nc.scalar.activation(sq[:, j % 2, 2, :], src[0:NS, 2 * P:3 * P], ACT.Copy).then_inc(act_read, 1)

                def store_kv(r, s):
                    u, b, j = plan[s]
                    g, h = u % GROUPS, head_of(r, u)
                    n = r * STEPS + s
                    if b < BLOCKS:
                        at = stored_rows(g, b)
                        if at is None:
                            return
                        act.wait_ge(qk_normed, after(n))
                        act.wait_ge(act_read, after(n))
                        act.dma_start(strided(v["kv_p"][g][0, 0], at[0], P, at[1])[:, :, bass.ds(h, 1), :].rearrange("t k o e -> t k (o e)"),
                                      kv[:, j % RKV, :, :]).then_inc(kv_stored[j % RKV], 16)
                    else:
                        act.wait_ge(qk_normed, after(n))
                        act.wait_ge(act_read, after(n))
                        act.dma_start(samp_dram[:, :, bass.ds(h + g * HEADS, 1), :].rearrange("b i o e -> b i (o e)"),
                                      sq[:, j % 2, :, :]).then_inc(samp_stored[j % 2], 16)
                        act.dma_start(v["kv_s"][g][0, :, PATTERNS[g][0] - 1, :, bass.ds(h, 1), :].rearrange("b k o e -> b k (o e)"),
                                      sq[:, j % 2, 1:3, :]).then_inc(samp_stored[j % 2], 16)

                def evac_T(r, s):
                    u, b, j = plan[s]
                    g = u % GROUPS
                    if b == SAMP:
                        return
                    jj = r * NB + j
                    act.wait_ge(t_done, after(jj))
                    act.wait_ge(s_done, after(jj - RT + 1))
                    nc.scalar.activation(qkT[:, j % RT, :, :].rearrange("p i t -> p (i t)"), pqk[:, 0:2 * P], ACT.Copy).then_inc(t_evac, 1)

                def exponent(r, s):
                    u, b, j = plan[s]
                    g = u % GROUPS
                    if b == SAMP:
                        return
                    jj = r * NB + j
                    lo = 0 if block_tokens(g, b)[2] else P
                    act.wait_ge(max_neg, after(jj))
                    act.wait_ge(pt_done, after(jj - RS))
                    nc.scalar.activation(pr[:, j % RS, lo:], sm[:, j % RS, lo:], ACT.Exp, bias=nm[:, j % RS:j % RS + 1],
                                         accum_out=ot[:, j % RO, E:E + 1]).then_inc(exp_done, 1)

                def output(r, s):
                    u, b, j = plan[s]
                    g, h = u % GROUPS, head_of(r, u)
                    if b == SAMP:
                        return
                    jj = r * NB + j
                    t0, d, _ = block_tokens(g, b)
                    act.wait_ge(pv_done, after(jj))
                    nc.scalar.activation(ot[:, j % RO, 0:E], po[j % 2][:, 0:E], ACT.Copy).then_inc(o_evac, 1)
                    act.wait_ge(o_evac, after(jj))
                    act.dma_start(strided(o_dram, t0, P, d)[:, bass.ds(h + g * HEADS, 1), :].rearrange("t o e -> t (o e)"),
                                  ot[:, j % RO, :]).then_inc(o_stored[j % RO], 16)

                def body(r):
                    for s in range(STEPS + 4):
                        if s < STEPS:
                            project_read(r, s)
                        if 0 <= s - 1 < STEPS:
                            evac_T(r, s - 1)
                            store_kv(r, s - 1)
                        if 0 <= s - 2 < STEPS:
                            exponent(r, s - 2)
                        if 0 <= s - 4 < STEPS:
                            output(r, s - 4)
                rounds(act, body)
                for i in range(RKV):
                    act.wait_ge(kv_stored[i], LEAD_DMA + 16 * ROUNDS * kv_slot_total[i])
                for i in range(RO):
                    act.wait_ge(o_stored[i], LEAD_DMA + 16 * ROUNDS * NB // RO)
                for i in range(2):
                    act.wait_ge(samp_stored[i], LEAD_DMA + 16 * ROUNDS * UNITS)

            @block.vector
            def _(dve):
                for x in (w_lo, meaned, qk_normed, s_masked, max_neg, pt_evac):
                    dve.sem_inc(x, LEAD)
                dve.wait_ge(gain_in, 32)
                nc.vector.tensor_scalar(gains[:, 0, :, :], gains[:, 0, :, :], float(E) ** -0.5, None, ALU.mult).then_inc(gain_ready, 1)

                def split_lo(u, slot, k):
                    dve.wait_ge(w_hi, after(u * KT + k))
                    nc.vector.tensor_tensor(three(wL[slot][:, k, :]), wst[:, :, k, :],
                                            three(wH[slot][:, k, :]).bitcast(F32), ALU.subtract).then_inc(w_lo, 1)

                def mean(r, s):
                    u, b, j = plan[s]
                    g = u % GROUPS
                    n = r * STEPS + s
                    rows = P if b < BLOCKS else NS
                    dve.wait_ge(squared, after(2 * n + 1))
                    dve.wait_ge(powered, after(n - 1))
                    nc.vector.tensor_scalar(ms[0:rows, s % 2, :], ss[0:rows, s % 2, :], 1.0 / E, EPS, ALU.mult, ALU.add).then_inc(meaned, 1)

                def normalise(r, s):
                    u, b, j = plan[s]
                    g = u % GROUPS
                    n = r * STEPS + s
                    rows = P if b < BLOCKS else NS
                    src = pp[s % 2]
                    dve.wait_ge(powered, after(n))
                    if b < BLOCKS:
                        jj = r * NB + j
                        dve.wait_ge(t_done, after(jj - RQ))
                        qdst, kdst = qn[:, j % RQ, :], kv[:, j % RKV, 0, :]
                    else:
                        qdst, kdst = sq[:, j % 2, 0, :], sq[:, j % 2, 1, :]
                    dve.wait_ge(act_read, after(n))
                    nc.vector.scalar_tensor_tensor(qdst, src[0:rows, 0:P], rs[0:rows, s % 2, 0:1], gains[0:rows, 0, g, :], ALU.mult, ALU.mult)
                    nc.vector.scalar_tensor_tensor(kdst, src[0:rows, P:2 * P], rs[0:rows, s % 2, 1:2], gains[0:rows, 1, g, :],
                                                   ALU.mult, ALU.mult).then_inc(qk_normed, 1)

                def mask_max(r, s):
                    u, b, j = plan[s]
                    g = u % GROUPS
                    if b == SAMP:
                        return
                    jj = r * NB + j
                    lo = 0 if block_tokens(g, b)[2] else P
                    dve.wait_ge(s_done, after(jj))
                    dve.wait_ge(exp_done, after(jj - RS))
                    dve.wait_ge(o_stored[j % RO], r * (16 * NB // RO) + (LEAD_DMA + 16 * (j // RO)))
                    apart(dve, v["passed"])
                    nc.vector.tensor_tensor_reduce(sm[:, j % RS, lo:], psc[j % 2][:, lo:2 * P], mask[:, lo:], 1.0, -3e38,
                                                   ALU.subtract, ALU.max, ot[:, j % RO, E + 1:E + 2]).then_inc(s_masked, 1)
                    dve.wait_ge(s_masked, after(jj))
                    nc.vector.tensor_scalar(nm[:, j % RS:j % RS + 1], ot[:, j % RO, E + 1:E + 2], -1.0, None, ALU.mult).then_inc(max_neg, 1)

                def evac_PT(r, s):
                    u, b, j = plan[s]
                    g = u % GROUPS
                    if b == SAMP:
                        return
                    jj = r * NB + j
                    lo = 0 if block_tokens(g, b)[2] else P
                    dve.wait_ge(pt_done, after(jj))
                    dve.wait_ge(pv_done, after(jj - RS))
                    nc.vector.tensor_copy(prT[:, j % RS, lo:], ppt[:, lo:2 * P]).then_inc(pt_evac, 1)

                for k in range(KT):
                    split_lo(0, 0, k)
                dve.wait_ge(mask_step, 3)
                dve.wait_ge(gain_ready, 1)

                def body(r):
                    for s in range(STEPS + 4):
                        if s < STEPS:
                            mean(r, s)
                        if 0 <= s - 2 < STEPS:
                            mask_max(r, s - 2)
                        if s < STEPS:
                            normalise(r, s)
                        if 0 <= s - 3 < STEPS:
                            evac_PT(r, s - 3)
                        if s < STEPS:
                            u, b, _ = plan[s]
                            if 4 <= b < 4 + KT:
                                split_lo(r * UNITS + (u + 1), (u + 1) % 2, b - 4)
                rounds(dve, body)

            @block.tensor
            def _(pe):
                for x in (proj_done, t_done, s_done, pt_done, pv_done):
                    pe.sem_inc(x, LEAD)

                def project(r, s, slot):
                    u, b, j = plan[s]
                    g = u % GROUPS
                    n = r * STEPS + s
                    rows = P if b < BLOCKS else NS
                    cols = tokens(g, b)
                    pe.wait_ge(act_read, after(n - 2))
                    pe.wait_ge(qk_normed, after(n - 2))
                    split = (lambda k: pe.wait_ge(w_lo, after((r * UNITS + u) * KT + k))) if b == 0 else None
                    three_pass(nc, pp[s % 2][0:rows, 0:3 * P], [(hH[:, k, cols], hL[:, k, cols], wH[slot][:, k, :], wL[slot][:, k, :])
                                                                for k in range(KT)], split).then_inc(proj_done, 1)

                def transposes(r, s):
                    u, b, j = plan[s]
                    g = u % GROUPS
                    if b == SAMP:
                        return
                    jj = r * NB + j
                    pe.wait_ge(qk_normed, after(r * STEPS + s))
                    pe.wait_ge(t_evac, after(jj - 1))
                    nc.tensor.transpose(pqk[:, 0:P], qn[:, j % RQ, :], ident[:, :])
                    nc.tensor.transpose(pqk[:, P:2 * P], kv[:, j % RKV, 0, :], ident[:, :]).then_inc(t_done, 1)

                def scores(r, s):
                    u, b, j = plan[s]
                    g = u % GROUPS
                    if b == SAMP:
                        return
                    jj = r * NB + j
                    prev = block_tokens(g, b)[2]
                    pe.wait_ge(t_evac, after(jj))
                    pe.wait_ge(s_masked, after(jj - 2))
                    if prev:
                        nc.tensor.matmul(psc[j % 2][:, 0:P], qkT[:, j % RT, 0, :], qkT[:, (j - 1) % RT, 1, :], start=True, stop=True)
                    nc.tensor.matmul(psc[j % 2][:, P:2 * P], qkT[:, j % RT, 0, :], qkT[:, j % RT, 1, :], start=True, stop=True).then_inc(s_done, 1)

                def probs_T(r, s):
                    u, b, j = plan[s]
                    g = u % GROUPS
                    if b == SAMP:
                        return
                    jj = r * NB + j
                    pe.wait_ge(exp_done, after(jj))
                    pe.wait_ge(pt_evac, after(jj - 1))
                    if block_tokens(g, b)[2]:
                        nc.tensor.transpose(ppt[:, 0:P], pr[:, j % RS, 0:P], ident[:, :])
                    nc.tensor.transpose(ppt[:, P:2 * P], pr[:, j % RS, P:2 * P], ident[:, :]).then_inc(pt_done, 1)

                def values(r, s):
                    u, b, j = plan[s]
                    g = u % GROUPS
                    if b == SAMP:
                        return
                    jj = r * NB + j
                    prev = block_tokens(g, b)[2]
                    pe.wait_ge(pt_evac, after(jj))
                    pe.wait_ge(o_evac, after(jj - 2))
                    if prev:
                        nc.tensor.matmul(po[j % 2][:, 0:E], prT[:, j % RS, 0:P], kv[:, (j - 1) % RKV, 1, :], start=True, stop=False)
                    nc.tensor.matmul(po[j % 2][:, 0:E], prT[:, j % RS, P:2 * P], kv[:, j % RKV, 1, :], start=not prev, stop=True).then_inc(pv_done, 1)

                def body(r):
                    for s in range(STEPS + 4):
                        if s < STEPS:
                            project(r, s, plan[s][0] % 2)
                        if 0 <= s - 1 < STEPS:
                            transposes(r, s - 1)
                        if 0 <= s - 2 < STEPS:
                            scores(r, s - 2)
                        if 0 <= s - 3 < STEPS:
                            probs_T(r, s - 3)
                        if 0 <= s - 4 < STEPS:
                            values(r, s - 4)
                rounds(pe, body)


def combine(nc, scope, v):
    ident, aTs = v["ident"], v["aTs"]
    w_a, w_b, w_o = v["w_a_out"][0], v["w_b_out"][0], v["w_out"][0]
    o_dram, bT_dram, gT_dram, gate_dram = v["o_dram"], v["bT_dram"], v["gT_dram"], v["gate_dram"]
    xp, yp, xs, ys = v["xp"], v["yp"], v["xs"], v["ys"]
    NT, CW = 2, 2 * P
    CS = CW + NS
    NC = SEQ // CW
    RG, RA = 4, 4
    stack = ExitStack()
    with stack:
        sb, ps, sem = scope(stack)
        NW = 16
        wH = sb("m_wH", [P, NW, D], F32R)
        with ExitStack() as whole_weights:
            w_whole = scope(whole_weights)[0]("w_whole", [P, NW, D])
        wL = sb("m_wL", [P, NW, D], F32R)
        combine_tiles(lambda name, *args, **at: sb(name + "_place", *args, **at))
        ol, cw = v["ol"], v["cw"]
        bl = sb("bl", [P, 4, CS])
        zl = sb("zl", [P, 4, CW])
        gl = [sb(f"gl{i}", [P, 2, CS]) for i in range(RG)]
        xl = [sb(f"xl{i}", [P, D]) for i in range(NT)]
        yst = [sb(f"yst{i}", [P, D]) for i in range(NT)]
        a32 = sb("a32", [P, 4, CS])
        abH = sb("abH", [P, KT, CS], F32R)
        abL = sb("abL", [P, KT, CS], F32R)
        mH = sb("mH", [P, KT, CS], F32R)
        mL = sb("mL", [P, KT, CS], F32R)
        gm = [sb(f"gm{i}", [P, 2, CS]) for i in range(2)]
        m32 = [sb(f"m32{i}", [P, CS]) for i in range(2)]
        gate_b = sb("gate_b", [P, D])
        pT = ps("c_pT", [P, 512])
        pa = ps("c_pa", [P, RA, 512])
        py = [ps(f"c_py{i}", [P, 512]) for i in range(2)]

        names = ("cstep", "bl_in", "zl_in", "gate_in", "cexp", "cdiff", "weighted", "a_ready", "aT_done", "aT_gated", "ab_hi", "ab_lo",
                 "pa_done", "gmul", "m_sum", "m_hi", "m_lo", "y_done", "y_mul", "y_ready", "samp_in", "s_done", "s_step", "s_out", "a_hi", "w_whole_hi", "w_split", "w_pool_split")
        (cstep, bl_in, zl_in, gate_in, cexp, cdiff, weighted, a_ready, aT_done, aT_gated, ab_hi, ab_lo,
         pa_done, gmul, m_sum, m_hi, m_lo, y_done, y_mul, y_ready, samp_in, s_done, s_step, s_out, a_hi, w_whole_hi, w_split, w_pool_split) = (sem("c_" + n) for n in names)
        ol_in = [sem(f"ol_in{i}") for i in range(NT)]
        gl_in = [sem(f"gl_in{i}") for i in range(RG)]
        xl_in = [sem(f"xl_in{i}") for i in range(NT)]
        y_out = [sem(f"y_out{i}") for i in range(NT)]
        QC = D // 4
        pieces = [(slice(k, k + 4), slice(j * QC, (j + 1) * QC)) for j in range(4) for k in (0, 4)]
        pieces += [(slice(k, k + 2), slice(0, D)) for k in range(KT, NW, 2)]
        HI_AT = {1: (4,), 2: (5,), 3: (6, 7, 8), 4: (9,), 6: (10,), 7: (11,)}
        LO_AT = {1: (4,), 2: (5,), 3: (6, 7), 7: (10,), 8: (11,)}
        GROUPS_AT = ({KT - 1: 0}, {3: 0, KT - 1: 1}, {})
        POOLED = (8, 9)
        wo_landed = [sem(f"wo_landed{i}") for i in range(len(pieces))]

        def chunks(eng, body, first=None):
            if first:
                first()
            with eng.Fori(1 if first else 0, NC - 1) as c:
                body(c, False)
            body(NC - 1, True)

        def branch_banks(f, last):
            if last:
                return pa[:, 2 * (f % 2):2 * (f % 2) + 2, 0:CS]
            return pa[:, f % RA, :].rearrange("p (a t) -> p a t", a=2)

        with nc.Block() as block:
            @block.sync
            def _(sp):
                def attention(c):
                    for i in range(NT):
                        sp.wait_ge(aT_gated, after(c * NT + (i - NT)))
                        apart(sp, v["passed"])
                        sp.dma_start(ol[i][:, :, :].rearrange("p n e -> p (n e)"),
                                     o_dram[bass.ds(c * CW + i * P, P), :, :].rearrange("t n e -> t (n e)")).then_inc(ol_in[i], 16)
                    branch_inputs(c)

                def branch_inputs(c):
                    sp.wait_ge(aT_gated, after(c * NT - 1))
                    apart(sp, v["passed"])
                    sp.dma_start(zl[:, :, :], gT_dram[0:4, :, bass.ds(c * CW, CW)].rearrange("f p t -> p f t")).then_inc(zl_in, 16)
                    sp.wait_ge(ab_lo, after(c * 2 - 1))
                    apart(sp, v["passed"])
                    sp.dma_start(bl[:, :, :], bT_dram[:, :, bass.ds(c * CW, CS)].rearrange("f p t -> p f t")).then_inc(bl_in, 16)

                def gates(c, fs):
                    for f in fs:
                        sp.wait_ge(gmul, after(c * KT + (f - RG)))
                        apart(sp, v["passed"])
                        pair = gT_dram[4:20, :, bass.ds(c * CW, CS)].rearrange("(a f) p t -> f p a t", f=KT)
                        sp.dma_start(gl[f % RG][:, :, :], pair[f]).then_inc(gl_in[f % RG], 16)

                def load_weights(ns):
                    for n in ns:
                        tiles, cols = pieces[n]
                        w, k0 = (w_a, 0) if tiles.start < 4 else (w_b, 4) if tiles.start < KT else (w_o, KT)
                        sp.dma_start(w_whole[:, tiles, cols], w[(tiles.start - k0) * P:(tiles.stop - k0) * P, cols]
                                     .rearrange("(k p) c -> p k c", p=P)).then_inc(wo_landed[n], 16)

                for i in range(NT):
                    sp.sem_inc(ol_in[i], 16)
                branch_inputs(0)
                load_weights(range(4))
                gates(0, range(0, 2))
                gates(0, range(2, RG))
                load_weights(range(4, 10))
                gates(0, range(4, 6))
                load_weights(range(10, len(pieces)))
                gates(0, range(6, KT))
                sp.dma_start(gate_b[:, :], gate_dram[0:1, :].to_broadcast([P, D])).then_inc(gate_in, 16)

                def body(c, last, first=False):
                    for i in range(NT):
                        sp.wait_ge(y_ready, after((c * NT + (i - NT)) * 2 + 1))
                        apart(sp, v["passed"])
                        sp.dma_start(xl[i][:, :], xp[bass.ds(c * CW + i * P, P), :]).then_inc(xl_in[i], 16)
                    if not last:
                        attention(c + 1)
                    if not first:
                        gates(c, range(RG, KT))
                    if not last:
                        gates(c + 1, range(0, RG))
                chunks(sp, body, lambda: body(0, False, True))
                sp.wait_ge(aT_gated, after(NC * NT - 1))
                sp.dma_start(ol[0][0:NS, :, :].rearrange("p n e -> p (n e)")[:, 0:D], xs).then_inc(samp_in, 16)
                sp.dma_start(ol[1][0:NS, :, :].rearrange("p n e -> p (n e)")[:, 0:D], gate_dram[1:1 + NS, :]).then_inc(samp_in, 16)
                sp.wait_ge(s_step, 4)
                sp.dma_start(ys, ol[1][0:NS, :, :].rearrange("p n e -> p (n e)")[:, 0:D]).then_inc(s_out, 16)
                sp.wait_ge(s_out, 16)
                sp.wait_ge(v["bulk"], 16 * (2 * NS + 8 * NS))
                sp.wait_ge(v["late"], 48)

            @block.gpsimd
            def _(pool):
                def split(c):
                    pool.wait_ge(pa_done, after(c * KT - 1))
                    pool.wait_ge(bl_in, c * 16 + 16)
                    apart(pool, v["passed"])
                    nc.gpsimd.tensor_copy(abH[:, 4:8, :], bl[:, :, :]).then_inc(ab_hi, 1)
                for i, n in enumerate(POOLED):
                    tiles, cols = pieces[n]
                    pool.wait_ge(w_whole_hi, n + 1)
                    nc.gpsimd.tensor_tensor(wL[:, tiles, cols], w_whole[:, tiles, cols], wH[:, tiles, cols].bitcast(F32),
                                            ALU.subtract).then_inc(w_pool_split, 1)

                def body(c, last):
                    if not last:
                        split(c + 1)
                chunks(pool, body)

            @block.scalar
            def _(act):
                act.sem_inc(m_hi, LEAD)
                for x in y_out:
                    act.sem_inc(x, LEAD_DMA)

                def weights(t, i):
                    act.wait_ge(cdiff, t + 1)
                    nc.scalar.activation(cw[:, i, 2, :], cw[:, i, 1, :], ACT.Exp).then_inc(cexp, 1)

                def attention_hi(c):
                    act.wait_ge(pa_done, after(c * KT - 1))
                    act.wait_ge(aT_gated, after(c * NT + 1))
                    nc.scalar.activation(abH[:, 0:4, :], a32[:, :, :], ACT.Copy).then_inc(a_hi, 1)

                def body(c, last, split_weights=None):
                    cols = CS if last else CW
                    groups_at = GROUPS_AT[0 if split_weights else 2 if last else 1]
                    for f in range(KT):
                        if split_weights and f in HI_AT:
                            split_weights(HI_AT[f])
                        act.wait_ge(m_sum, after(c * KT + f))
                        act.wait_ge(y_done, after(c * (2 * NT) - 1))
                        nc.scalar.activation(mH[:, f, 0:cols], m32[f % 2][:, 0:cols], ACT.Copy).then_inc(m_hi, 1)
                        if f in groups_at:
                            weights(c * NT + NT + groups_at[f], groups_at[f])
                    for i in range(NT):
                        act.wait_ge(y_ready, after((c * NT + i) * 2 + 1))
                        act.dma_start(yp[bass.ds(c * CW + i * P, P), :], yst[i][:, :]).then_inc(y_out[i], 16)
                        if i == 0 and not last:
                            if split_weights:
                                weights(NT + 1, 1)
                            attention_hi(c + 1)

                def weights_hi(ns):
                    for n in ns:
                        tiles, cols = pieces[n]
                        act.wait_ge(wo_landed[n], 16)
                        nc.scalar.activation(wH[:, tiles, cols], w_whole[:, tiles, cols], ACT.Copy).then_inc(w_whole_hi, 1)

                act.sem_inc(cexp, NT)
                act.wait_ge(bl_in, 16)
                nc.scalar.activation(abH[:, 4:8, :], bl[:, :, :], ACT.Copy).then_inc(ab_hi, 1)
                attention_hi(0)
                weights_hi(range(4))
                chunks(act, body, lambda: body(0, False, weights_hi))
                for i in range(NT):
                    act.wait_ge(y_out[i], LEAD_DMA + 16 * NC)

            @block.vector
            def _(dve):
                for x in (a_ready, aT_gated, ab_lo, gmul, m_sum, m_lo, y_ready):
                    dve.sem_inc(x, LEAD)
                total = 7

                def groups(c, i):
                    t = c * NT + i
                    at = [0]

                    def chained(ins):
                        at[0] += 1
                        ins.then_inc(cstep, 1)
                        dve.wait_ge(cstep, t * total + at[0])

                    dve.wait_ge(ol_in[i], c * 16 + 16)
                    sum_groups(nc, ol[i][:, :, :], cw[:, i], chained, cdiff, lambda: dve.wait_ge(cexp, t + 1)).then_inc(a_ready, 1)
                    assert at[0] == total

                def gate_a(c, i):
                    t = c * NT + i
                    if i == 0:
                        dve.wait_ge(zl_in, c * 16 + 16)
                        dve.wait_ge(ab_lo, after(c * 2 - 1))
                    dve.wait_ge(aT_done, t + 1)
                    cols = slice(i * P, (i + 1) * P)
                    nc.vector.tensor_tensor(a32[:, :, cols], pT[:, :].rearrange("p (h t) -> p h t", t=P), zl[:, :, cols],
                                            ALU.mult).then_inc(aT_gated, 1)

                def split(c):
                    pooling_lo(c)
                    attention_lo(c)

                def pooling_lo(c):
                    dve.wait_ge(ab_hi, c + 1)
                    nc.vector.tensor_tensor(abL[:, 4:8, :], bl[:, :, :], abH[:, 4:8, :].bitcast(F32), ALU.subtract).then_inc(ab_lo, 1)

                def attention_lo(c):
                    dve.wait_ge(a_hi, c + 1)
                    nc.vector.tensor_tensor(abL[:, 0:4, :], a32[:, :, :], abH[:, 0:4, :].bitcast(F32), ALU.subtract).then_inc(ab_lo, 1)

                def branch(c, f, last):
                    n = c * KT + f
                    cols = CS if last else CW
                    dve.wait_ge(pa_done, after(n))
                    dve.wait_ge(gl_in[f % RG], c * (16 * KT // RG) + 16 * (f // RG + 1))
                    nc.vector.tensor_tensor(gm[f % 2][:, :, 0:cols], branch_banks(f, last), gl[f % RG][:, :, 0:cols], ALU.mult).then_inc(gmul, 1)
                    dve.wait_ge(gmul, after(n))
                    nc.vector.tensor_tensor(m32[f % 2][:, 0:cols], gm[f % 2][:, 0, 0:cols], gm[f % 2][:, 1, 0:cols], ALU.add).then_inc(m_sum, 1)
                    dve.wait_ge(m_hi, after(n))
                    nc.vector.tensor_tensor(mL[:, f, 0:cols], m32[f % 2][:, 0:cols], mH[:, f, 0:cols].bitcast(F32), ALU.subtract).then_inc(m_lo, 1)

                def result(c, i, j):
                    n = (c * NT + i) * 2 + j
                    cols = slice(j * 512, (j + 1) * 512)
                    dve.wait_ge(y_done, after(n))
                    if j == 0:
                        dve.wait_ge(y_out[i], c * 16 + LEAD_DMA)
                        dve.wait_ge(xl_in[i], c * 16 + 16)
                    nc.vector.tensor_tensor(yst[i][:, cols], py[j][:, :], gate_b[:, cols], ALU.mult).then_inc(y_mul, 1)
                    dve.wait_ge(y_mul, n + 1)
                    nc.vector.tensor_tensor(yst[i][:, cols], yst[i][:, cols], xl[i][:, cols], ALU.add).then_inc(y_ready, 1)

                def samples():
                    dve.wait_ge(samp_in, 32)
                    x_s, gate_s = (ol[i][0:NS, :, :].rearrange("p n e -> p (n e)") for i in range(NT))
                    for j in range(2):
                        cols = slice(j * 512, (j + 1) * 512)
                        dve.wait_ge(s_done, 1 + j)
                        nc.vector.tensor_tensor(gate_s[:, cols], py[j][0:NS, :], gate_s[:, cols], ALU.mult).then_inc(s_step, 1)
                        dve.wait_ge(s_step, 2 * j + 1)
                        nc.vector.tensor_tensor(gate_s[:, cols], gate_s[:, cols], x_s[:, cols], ALU.add).then_inc(s_step, 1)

                def weights_lo(n):
                    dve.wait_ge(w_whole_hi, n + 1)
                    tiles, cols = pieces[n]
                    nc.vector.tensor_tensor(wL[:, tiles, cols], w_whole[:, tiles, cols], wH[:, tiles, cols].bitcast(F32),
                                            ALU.subtract).then_inc(w_split, 1)

                nc.vector.tensor_copy(a32[:, :, CW:], aTs[:, :, :])
                dve.sem_inc(cstep, NT * total)
                dve.sem_inc(cdiff, NT)
                dve.sem_inc(a_ready, NT)
                for i in range(NT):
                    gate_a(0, i)
                pooling_lo(0)
                attention_lo(0)
                for n in range(2):
                    weights_lo(n)
                for n in range(2, 4):
                    weights_lo(n)

                def body(c, last, split_weights=None):
                    groups_at = GROUPS_AT[0 if split_weights else 2 if last else 1]
                    for f in range(KT):
                        if split_weights:
                            for n in LO_AT.get(f, ()):
                                split_weights(n)
                        branch(c, f, last)
                        if split_weights and f == KT - 1:
                            for n in LO_AT[KT]:
                                split_weights(n)
                        if f in groups_at:
                            groups(c + 1, groups_at[f])
                    if last:
                        samples()
                    if split_weights:
                        dve.wait_ge(gate_in, 16)
                    for j in range(2):
                        result(c, 0, j)
                    if split_weights:
                        groups(1, 1)
                    if not last:
                        gate_a(c + 1, 0)
                        gate_a(c + 1, 1)
                        split(c + 1)
                    for j in range(2):
                        result(c, 1, j)
                chunks(dve, body, lambda: body(0, False, weights_lo))

            @block.tensor
            def _(pe):
                pe.sem_inc(pa_done, LEAD)
                pe.sem_inc(y_done, LEAD)

                def transposes(c, i):
                    t = c * NT + i
                    pe.wait_ge(a_ready, after(t))
                    pe.wait_ge(aT_gated, after(t - 1))
                    for h in range(HEADS):
                        last = nc.tensor.transpose(pT[:, h * P:(h + 1) * P], ol[i][:, h, 0:E], ident[:, :])
                    last.then_inc(aT_done, 1)

                def branch(c, f, last):
                    n = c * KT + f
                    cols = CS if last else CW
                    pe.wait_ge(gmul, after(n - (2 if last else RA)))
                    for a in range(2):
                        done = three_pass(nc, branch_banks(f, last)[:, a, :],
                                          [(wH[:, k, f * P:(f + 1) * P], wL[:, k, f * P:(f + 1) * P], abH[:, k, 0:cols], abL[:, k, 0:cols])
                                           for k in range(4 * a, 4 * a + 4)])
                    done.then_inc(pa_done, 1)

                def out_terms(cols, j):
                    return [(mH[:, k, cols], mL[:, k, cols], wH[:, KT + k, j * 512:(j + 1) * 512], wL[:, KT + k, j * 512:(j + 1) * 512])
                            for k in range(KT)]

                def m_and_weights(c):
                    def before(k):
                        pe.wait_ge(m_lo, after(c * KT + k))
                        if k % 2 == 0 and k < 2 * len(POOLED):
                            pe.wait_ge(w_pool_split, k // 2 + 1)
                        elif k % 2 == 0:
                            pe.wait_ge(w_split, KT + k // 2 - len(POOLED) + 1)
                    return before

                def result(c, i, j, last):
                    n = (c * NT + i) * 2 + j
                    pe.wait_ge(y_ready, after(n - 2))
                    if last and i == 0:
                        pe.wait_ge(s_step, 2 * j + 1)
                    before = m_and_weights(c) if i == 0 and j == 0 and not last else None
                    three_pass(nc, py[j][:, :], out_terms(slice(i * P, (i + 1) * P), j), before).then_inc(y_done, 1)

                def samples(c, j):
                    pe.wait_ge(y_ready, after((c * NT - 1) * 2 + j))
                    before = m_and_weights(c) if j == 0 else None
                    three_pass(nc, py[j][0:NS, :], out_terms(slice(CW, CS), j), before).then_inc(s_done, 1)

                for i in range(NT):
                    transposes(0, i)

                def body(c, last):
                    pe.wait_ge(ab_lo, after(c * 2 + 1))
                    for f in range(KT):
                        if f % 2 == 0:
                            pe.wait_ge(w_split, f + 2)
                        branch(c, f, last)
                    if last:
                        for j in range(2):
                            samples(c, j)
                    for j in range(2):
                        result(c, 0, j, last)
                    if not last:
                        transposes(c + 1, 0)
                    result(c, 1, 0, last)
                    if not last:
                        transposes(c + 1, 1)
                    result(c, 1, 1, last)
                chunks(pe, body)


_INS = ["x_prompt", "x_sample", "state_kv_w128", "state_kv_w512", "state_kv_w2048", "state_pool", "c_prompt", "c_sample", "norm_g",
        "w_ada", "b_ada", "w_in", "q_gain", "k_gain", "w_pool", "b_pool", "pool_scale", "w_a_out", "w_b_out", "w_out"]
_OUTS = [(1, SEQ, D), (NS, 1, D), (1, 1, 128, 2, HEADS, E), (1, 1, 512, 2, HEADS, E), (1, 1, 2048, 2, HEADS, E), (1, 1, NPS, 512),
         (1, NS, 128, 2, HEADS, E), (1, NS, 512, 2, HEADS, E), (1, NS, 2048, 2, HEADS, E), (1, NS, NPS, 512)]


def kernel(**inputs):
    import numpy as _np
    import concourse.bacc as _bacc
    from concourse import mybir as _mybir
    from concourse.bass_utils import run_bass_kernel_spmd as _run

    nc = _bacc.Bacc("TRN2", target_bir_lowering=False, num_devices=1, dynamic_dma_scratch_size=1024)
    arrays, args = {}, []
    for name in _INS:
        a = _np.ascontiguousarray(inputs[name])
        arrays[f"in_{name}_dram"] = a
        args.append(nc.dram_tensor(f"in_{name}_dram", a.shape, _mybir.dt.from_np(a.dtype), kind="ExternalInput").ap())
    for i, shape in enumerate(_OUTS):
        args.append(nc.dram_tensor(f"out_{i}_dram", shape, F32, kind="ExternalOutput").ap())
    build(nc, *args)
    r = _run(nc, [arrays], core_ids=[0])
    return tuple(r.results[0][f"out_{i}_dram"] for i in range(len(_OUTS)))
```
